# Optimizing a Trainium2 kernel written in Bass

```python
import jax, jax.numpy as jnp
from jax import lax
import numpy as np

D_MODEL = 1024
BATCH = 1
SEQ = 1024
DEPTH = 1
DEC_BATCH = 8
DEC_SEQ = 8
PAST_LEN = 8192
PAGE_SIZE = 128

MIX_WIDTH = D_MODEL
C_CONV = MIX_WIDTH // 2
C_RWKV = MIX_WIDTH - C_CONV
HEAD_DIM = 64
N_HEADS = C_RWKV // HEAD_DIM
CONV_WIDTH = 31
D_DECAY_LORA = 64
D_AAA_LORA = 64
D_GATE_LORA = 128
D_SHIFT = 3 * C_RWKV + D_DECAY_LORA + D_AAA_LORA + D_GATE_LORA
D_IN = 2 * C_CONV + D_SHIFT
N_EXPERT_GROUPS = 4
EXPERTS_PER_GROUP = 8
TOP_K = 2
D_EXPERT = 256
RMS_EPS = 1e-6
LN_EPS = 1e-5
GN_EPS = 64e-5
RWKV_SPLITS = (C_RWKV, 2 * C_RWKV, 3 * C_RWKV, 3 * C_RWKV + D_DECAY_LORA,
               3 * C_RWKV + D_DECAY_LORA + D_AAA_LORA)

kernel_name = "hymba_conformer_rwkv7_hiermoe_step"

def rmsnorm(x, g):
    xf = x.astype(jnp.float32)
    y = xf * lax.rsqrt(jnp.mean(xf * xf, axis=-1, keepdims=True) + RMS_EPS)
    return (y * g.astype(jnp.float32)).astype(x.dtype)

def conv_mixer(u, conv_buf, conv_w, conv_b, ln_g, ln_b):
    val, gate = jnp.split(u, 2, axis=-1)
    h = val * jax.nn.sigmoid(gate)
    hx = jnp.concatenate([conv_buf.astype(h.dtype), h], axis=1)
    out = lax.conv_general_dilated(
        hx, conv_w.astype(hx.dtype)[:, None, :], window_strides=(1,), padding='VALID',
        dimension_numbers=('NWC', 'WIO', 'NWC'), feature_group_count=C_CONV) + conv_b
    new_buf = hx[:, -(CONV_WIDTH - 1):]
    of = out.astype(jnp.float32)
    mu = jnp.mean(of, axis=-1, keepdims=True)
    var = jnp.mean(jnp.square(of - mu), axis=-1, keepdims=True)
    of = (of - mu) * lax.rsqrt(var + LN_EPS) * ln_g.astype(jnp.float32) + ln_b.astype(jnp.float32)
    return jax.nn.silu(of).astype(u.dtype), new_buf

def wkv_step(S, inp):
    r_t, w_t, k_t, v_t, kk_t, a_t = inp
    sa = jnp.einsum('bhvk,bhk->bhv', S, -kk_t)
    S = (S * w_t[:, :, None, :] + sa[..., None] * (kk_t * a_t)[:, :, None, :]
         + v_t[..., None] * k_t[:, :, None, :])
    y = jnp.einsum('bhvk,bhk->bhv', S, r_t)
    return S, y

def rwkv_mixer(z, shift_buf, wkv_state, mu_shift, w0, w_decay_up, a0, w_aaa_up, w_gate_up,
               k_k, k_a, r_k, gn_g, gn_b):
    B, T, _ = z.shape
    f32 = jnp.float32
    z_prev = jnp.concatenate([shift_buf[:, None, :].astype(z.dtype), z[:, :-1]], axis=1)
    zs = z + (z_prev - z) * mu_shift
    new_shift = z[:, -1]
    r, k, v, wl, al, gl = jnp.split(zs, RWKV_SPLITS, axis=-1)
    w_log = -jax.nn.softplus(-(w0 + jnp.tanh(wl) @ w_decay_up).astype(f32)) - 0.5
    decay = jnp.exp(-jnp.exp(w_log))
    a = jax.nn.sigmoid((a0 + al @ w_aaa_up).astype(f32))
    g = jax.nn.sigmoid(gl) @ w_gate_up

    def heads(t):
        return t.astype(f32).reshape(B, T, N_HEADS, HEAD_DIM)

    kk = heads(k * k_k)
    kk = kk / jnp.maximum(jnp.sqrt(jnp.sum(kk * kk, axis=-1, keepdims=True)), 1e-12)
    k_mod = k.astype(f32) * (1.0 + (a - 1.0) * k_a.astype(f32))
    r_h, k_h, v_h, w_h, a_h = heads(r), heads(k_mod), heads(v), heads(decay), heads(a)
    xs = tuple(jnp.moveaxis(t, 1, 0) for t in (r_h, w_h, k_h, v_h, kk, a_h))
    S_final, y = lax.scan(wkv_step, wkv_state.astype(f32), xs)
    y = jnp.moveaxis(y, 0, 1)
    mu = jnp.mean(y, axis=-1, keepdims=True)
    var = jnp.mean(jnp.square(y - mu), axis=-1, keepdims=True)
    y_n = ((y - mu) * lax.rsqrt(var + GN_EPS)).reshape(B, T, C_RWKV)
    y_n = y_n * gn_g.astype(f32) + gn_b.astype(f32)
    bonus = jnp.sum(r_h * k_h * r_k.astype(f32).reshape(N_HEADS, HEAD_DIM), axis=-1,
                    keepdims=True) * v_h
    out = (y_n + bonus.reshape(B, T, C_RWKV)) * g.astype(f32)
    return out.astype(z.dtype), new_shift, S_final.astype(wkv_state.dtype)

def hier_moe(x, w_rg, b_rg, w_re, b_re, w_eg, w_eu, w_ed):
    B, T, D = x.shape
    xt = x.reshape(-1, D)
    g_logits = (xt @ w_rg + b_rg).astype(jnp.float32)
    g_prob = jax.nn.softmax(g_logits, axis=-1)
    g_idx = jnp.argmax(g_logits, axis=-1)
    e_logits = (xt @ w_re + b_re).astype(jnp.float32).reshape(-1, N_EXPERT_GROUPS, EXPERTS_PER_GROUP)
    e_in = jnp.take_along_axis(e_logits, g_idx[:, None, None], axis=1)[:, 0]
    top_vals, top_idx = lax.top_k(e_in, TOP_K)
    p_group = jnp.take_along_axis(g_prob, g_idx[:, None], axis=1)
    top_w = jax.nn.softmax(top_vals, axis=-1) * p_group
    comb_e = jnp.sum(jax.nn.one_hot(top_idx, EXPERTS_PER_GROUP, dtype=jnp.float32)
                     * top_w[..., None], axis=1)
    combine = comb_e[:, None, :] * jax.nn.one_hot(g_idx, N_EXPERT_GROUPS, dtype=jnp.float32)[:, :, None]
    y = jnp.zeros_like(xt)
    for gi in range(N_EXPERT_GROUPS):
        hg = jnp.einsum('nd,edf->nef', xt, w_eg[gi])
        hu = jnp.einsum('nd,edf->nef', xt, w_eu[gi])
        h = jax.nn.silu(hg) * hu * combine[:, gi, :, None].astype(xt.dtype)
        y = y + jnp.einsum('nef,efd->nd', h, w_ed[gi])
    return y.reshape(B, T, D)

def layer(x, conv_buf, shift_buf, wkv_state, lp):
    (norm1_g, w_in, conv_w, conv_b, conv_ln_g, conv_ln_b, mu_shift, w0, w_decay_up, a0,
     w_aaa_up, w_gate_up, k_k, k_a, r_k, gn_g, gn_b, w_out, norm2_g, w_router_group,
     b_router_group, w_router_expert, b_router_expert, w_exp_gate, w_exp_up, w_exp_down) = lp
    xn = rmsnorm(x, norm1_g)
    proj = xn @ w_in
    conv_out, new_conv = conv_mixer(proj[..., :2 * C_CONV], conv_buf, conv_w, conv_b,
                                    conv_ln_g, conv_ln_b)
    rwkv_out, new_shift, new_wkv = rwkv_mixer(proj[..., 2 * C_CONV:], shift_buf, wkv_state,
                                              mu_shift, w0, w_decay_up, a0, w_aaa_up,
                                              w_gate_up, k_k, k_a, r_k, gn_g, gn_b)
    h = x + jnp.concatenate([conv_out, rwkv_out], axis=-1) @ w_out
    h = h + hier_moe(rmsnorm(h, norm2_g), w_router_group, b_router_group, w_router_expert,
                     b_router_expert, w_exp_gate, w_exp_up, w_exp_down)
    return h, new_conv, new_shift, new_wkv

def setup_inputs(seed: int = 0) -> dict:
    key = jax.random.key(seed)
    ks = iter(jax.random.split(key, 40))
    f32 = jnp.float32

    def nrm(shape, scale):
        return jax.random.normal(next(ks), shape, f32) * scale

    L, G, E = DEPTH, N_EXPERT_GROUPS, EXPERTS_PER_GROUP
    return {
        "x_prompt": nrm((BATCH, SEQ, D_MODEL), 1.0),
        "x_sample": nrm((DEC_BATCH, DEC_SEQ, D_MODEL), 1.0),
        "state_conv": nrm((L, DEC_BATCH, CONV_WIDTH - 1, C_CONV), 0.5),
        "state_shift": nrm((L, DEC_BATCH, D_SHIFT), 1.0),
        "state_wkv": nrm((L, DEC_BATCH, N_HEADS, HEAD_DIM, HEAD_DIM), 0.1),
        "norm1_g": 1.0 + nrm((L, D_MODEL), 0.02),
        "w_in": nrm((L, D_MODEL, D_IN), D_MODEL ** -0.5),
        "conv_w": nrm((L, CONV_WIDTH, C_CONV), CONV_WIDTH ** -0.5),
        "conv_b": nrm((L, C_CONV), 0.02),
        "conv_ln_g": 1.0 + nrm((L, C_CONV), 0.02),
        "conv_ln_b": nrm((L, C_CONV), 0.02),
        "mu_shift": jax.random.uniform(next(ks), (L, D_SHIFT), f32),
        "w0": jax.random.uniform(next(ks), (L, C_RWKV), f32, -5.0, 1.0),
        "w_decay_up": nrm((L, D_DECAY_LORA, C_RWKV), 0.5 * D_DECAY_LORA ** -0.5),
        "a0": nrm((L, C_RWKV), 0.1),
        "w_aaa_up": nrm((L, D_AAA_LORA, C_RWKV), 0.5 * D_AAA_LORA ** -0.5),
        "w_gate_up": nrm((L, D_GATE_LORA, C_RWKV), D_GATE_LORA ** -0.5),
        "k_k": 0.85 + nrm((L, C_RWKV), 0.02),
        "k_a": 1.0 + nrm((L, C_RWKV), 0.02),
        "r_k": nrm((L, C_RWKV), 0.1),
        "gn_g": 1.0 + nrm((L, C_RWKV), 0.02),
        "gn_b": nrm((L, C_RWKV), 0.02),
        "w_out": nrm((L, MIX_WIDTH, D_MODEL), MIX_WIDTH ** -0.5),
        "norm2_g": 1.0 + nrm((L, D_MODEL), 0.02),
        "w_router_group": nrm((L, D_MODEL, G), D_MODEL ** -0.5),
        "b_router_group": nrm((L, G), 0.01),
        "w_router_expert": nrm((L, D_MODEL, G * E), D_MODEL ** -0.5),
        "b_router_expert": nrm((L, G * E), 0.01),
        "w_exp_gate": nrm((L, G, E, D_MODEL, D_EXPERT), D_MODEL ** -0.5),
        "w_exp_up": nrm((L, G, E, D_MODEL, D_EXPERT), D_MODEL ** -0.5),
        "w_exp_down": nrm((L, G, E, D_EXPERT, D_MODEL), D_EXPERT ** -0.5),
        "norm_f_g": 1.0 + nrm((D_MODEL,), 0.02),
    }

def reference(x_prompt, x_sample, state_conv, state_shift, state_wkv, norm1_g, w_in, conv_w,
              conv_b, conv_ln_g, conv_ln_b, mu_shift, w0, w_decay_up, a0, w_aaa_up, w_gate_up,
              k_k, k_a, r_k, gn_g, gn_b, w_out, norm2_g, w_router_group, b_router_group,
              w_router_expert, b_router_expert, w_exp_gate, w_exp_up, w_exp_down, norm_f_g):
    B = x_prompt.shape[0]
    dt = x_prompt.dtype
    h_p, h_s = x_prompt, x_sample
    conv_p, shift_p, wkv_p, conv_s, shift_s, wkv_s = [], [], [], [], [], []
    for l in range(DEPTH):
        lp = (norm1_g[l], w_in[l], conv_w[l], conv_b[l], conv_ln_g[l], conv_ln_b[l], mu_shift[l],
              w0[l], w_decay_up[l], a0[l], w_aaa_up[l], w_gate_up[l], k_k[l], k_a[l], r_k[l],
              gn_g[l], gn_b[l], w_out[l], norm2_g[l], w_router_group[l], b_router_group[l],
              w_router_expert[l], b_router_expert[l], w_exp_gate[l], w_exp_up[l], w_exp_down[l])
        h_p, c, s, w = layer(h_p,
                             jnp.zeros((B, CONV_WIDTH - 1, C_CONV), dt),
                             jnp.zeros((B, D_SHIFT), dt),
                             jnp.zeros((B, N_HEADS, HEAD_DIM, HEAD_DIM), dt), lp)
        conv_p.append(c); shift_p.append(s); wkv_p.append(w)
        h_s, c, s, w = layer(h_s, state_conv[l], state_shift[l], state_wkv[l], lp)
        conv_s.append(c); shift_s.append(s); wkv_s.append(w)
    y_prompt = rmsnorm(h_p, norm_f_g)
    y_sample = rmsnorm(h_s, norm_f_g)
    return (y_prompt, y_sample, jnp.stack(conv_p), jnp.stack(shift_p), jnp.stack(wkv_p),
            jnp.stack(conv_s), jnp.stack(shift_s), jnp.stack(wkv_s))


_drawn_inputs = setup_inputs


def setup_inputs(seed=0):
    import zlib

    import numpy as np

    out = dict(_drawn_inputs(seed))
    spreads = {}
    factors = {'conv_ln_b': 9.32,
     'k_k': 14.599,
     'gn_g': 4.613,
     'gn_b': 12.202,
     'b_router_group': 9.47,
     'b_router_expert': 15.106,
     'norm_f_g': 8.397,
     'conv_b': 4.013,
     'conv_ln_g': 5.733,
     'norm2_g': 3.707}
    for name, (base, spread) in spreads.items():
        noise = np.random.default_rng([zlib.crc32(name.encode()), seed]).standard_normal(out[name].shape)
        drawn = base * np.exp(spread * noise) if base else spread * noise
        out[name] = __import__('jax').numpy.asarray(drawn.astype(out[name].dtype))
    for name, factor in factors.items():
        out[name] = (out[name] * factor).astype(out[name].dtype)
    return out
```

```python
from contextlib import ExitStack

import numpy as np

import concourse.bass as bass
from concourse import mybir

F32 = mybir.dt.float32
U32 = mybir.dt.uint32
ALU = mybir.AluOpType
ACT = mybir.ActivationFunctionType
AX = mybir.AxisListType

P = 128
D = 1024
DC = D // P
SEQ = 1024
SB, ST = 8, 8
NS = SB * ST
N = SEQ + NS
NT = SEQ // P + 1
C = 512
CT = C // P
HD = 64
W = 31
HB = W - 1
DS = 1792
ZT = DS // P
MT = (2 * C + DS) // P
NG, EG = 4, 8
NE = NG * EG
F = 256
TOPK = 2
NX = (N * TOPK) // P
UN = 4
EXTRA = -(-NX // UN) * UN
NTILE_X = NE + EXTRA
RMS_EPS, LN_EPS, GN_EPS = 1e-6, 1e-5, 64e-5
LOGW = -float(np.exp(-0.5))
BIG = 1.0e30

HXW = HB + SEQ + SB * (HB + ST)
ZW = 1 + SEQ + SB * (1 + ST)
LV = 6
LV8 = 3

PR = {}
for _n, _c in (("mu", ZT), ("k_k", CT), ("k_a", CT), ("r_k", CT), ("a0", CT), ("gn_g", CT), ("gn_b", CT),
               ("conv_b", CT), ("ln_g", CT), ("ln_b", CT)):
    PR[_n] = (sum(c for _, c in PR.values()), _c)
NPR = sum(c for _, c in PR.values())

VAL, GATE, RR, KK, VV, WA, GL = 0, 4, 8, 12, 16, 20, 21
ORDER = [t for c in range(CT) for t in (GATE + c, VAL + c)] + [WA, GL] + [KK + c for c in range(CT)] \
    + [RR + c for c in range(CT)] + [VV + c for c in range(CT)]
NCONV = 2 * CT


def rows_of(i):
    return P if i < NT - 1 else NS


def hybrid_decoder_step(nc, x_prompt, x_sample, state_conv, state_shift, state_wkv, norm1_g, w_in, conv_w, conv_b,
                        conv_ln_g, conv_ln_b, mu_shift, w0, w_decay_up, a0, w_aaa_up, w_gate_up, k_k, k_a, r_k,
                        gn_g, gn_b, w_out, norm2_g, w_router_group, b_router_group, w_router_expert,
                        b_router_expert, w_exp_gate, w_exp_up, w_exp_down, norm_f_g,
                        y_prompt, y_sample, new_conv_p, new_shift_p, new_wkv_p, new_conv_s, new_shift_s, new_wkv_s):
    ctx = ExitStack()
    with ctx:
        def sb(name, shape, dt=F32):
            return ctx.enter_context(nc.sbuf_tensor(name, shape, dt))

        def sem(name):
            return ctx.enter_context(nc.semaphore(name))

        xn2_rows = nc.dram_tensor("xn2_rows", (N, D), F32, kind="Internal").ap()
        y_rows = nc.dram_tensor("y_rows", (N * TOPK, D), F32, kind="Internal").ap()

        ident = sb("ident", [P, P])
        tri_cum = sb("tri_cum", [P, 2, 2, 64])
        tri_cum8 = sb("tri_cum8", [NS, 2, 64])
        mask_ar = sb("mask_ar", [P, 2, 64])
        mask_ar8 = sb("mask_ar8", [P, 2, 64])
        mask_lv = sb("mask_lv", [P, LV, 64])
        mask_lv0t = sb("mask_lv0t", [P, 64])
        seqmask = sb("seqmask", [P, SB, 64])
        rowmask = sb("rowmask", [P, SB])
        headsum = sb("headsum", [P, P])
        headmean = sb("headmean", [P, P])
        head_sel = sb("head_sel", [P, CT, 8])
        head_back = sb("head_back", [8, CT, P])
        chmean = sb("chmean", [P, P])
        before = sb("before", [P, P])
        ones = sb("ones", [P, P])
        prm = sb("prm", [P, NPR])
        om_ka = sb("om_ka", [P, CT])
        cw = sb("cw", [P, W, CT])
        shift0 = sb("shift0", [P, ZT, SB])
        lastz = sb("lastz", [P, ZT, 1 + SB])
        gain = sb("gain", [P, D])
        w0_all = sb("w0_all", [P, C])
        w_da = sb("w_da", [P, C])
        w_g = sb("w_g", [P, C])
        stat = sb("stat", [P, 8, NT])

        ARENA = 46900
        arena = sb("arena", [P, ARENA])

        def at(off, *shape):
            n = int(np.prod(shape))
            assert off + n <= ARENA, (off, n)
            v = arena[:, off:off + n]
            if len(shape) > 1:
                names = "abcdef"[:len(shape)]
                v = v.rearrange(f"p ({' '.join(names)}) -> p {' '.join(names)}",
                                **{k: s for k, s in zip(names[1:], shape[1:])})
            return v

        O_ZS = 0
        O_XN = O_ZS + ZT * N
        O_R1 = O_XN + DC * N
        O_HX = O_R1
        O_WIN = O_HX + CT * HXW
        O_XR = O_WIN + 6 * DC * P
        O_CO = O_XR + 5 * D
        O_EX = O_CO + CT * N
        zs = at(O_ZS, ZT, N)
        squares = at(O_ZS, D)
        xnT = at(O_XN, DC, N)
        hx = at(O_HX, CT, HXW)
        win = [at(O_WIN + s * DC * P, DC, P) for s in range(6)]
        x_in = [at(O_XR + s * D, D) for s in range(3)]
        xn = [at(O_XR + (3 + s) * D, D) for s in range(2)]
        co = at(O_CO, CT, N)
        O_LD = O_CO
        ld_prm = at(O_LD, P)
        ld_cw = at(O_LD + P, P)
        ld_shift = at(O_LD + 2 * P, DS)
        ld_conv = at(O_LD + 2 * P + DS, 2, C)
        zbuf = [at(O_XR + s * ZW, ZW) for s in range(2)]
        zd = at(O_XR + 2 * ZW, N)
        sig = at(O_XR + 2 * ZW + N, N)

        ps = ctx.enter_context(nc.psum_tensor("ps", [P, 8, 512], F32))

        sgw = at(O_WIN, NT, C)
        yT = at(O_WIN, NT, CT, P)
        conv_tail = at(O_XN + 4 * N, 4, C)
        shift_tail = at(O_XN + 4 * N + 4 * C, DS)
        TG = [(0, 3), (3, 6), (6, SB)]
        SK = HB + ST
        nkk, kka = at(O_XN, CT, N), at(O_XN + CT * N, CT, N)
        iclr = [at(O_XR + s * N, N) for s in range(2)]
        kmul = at(O_XR + 2 * N, N)
        ksq = at(O_XR + 3 * N, N)
        knorm = at(O_EX, N)
        R0, K0, V0, WA0, GL0 = 0, 4, 8, 12, 13

        conv_sq = ksq
        conv_rstd = iclr[0]
        conv_sig = iclr[1]

        off = [O_HX]

        def take(*shape):
            v = at(off[0], *shape)
            off[0] += int(np.prod(shape))
            return v

        lwst = take(C)
        vst = take(CT, P)
        e_in, e_ex, e_neg = take(CT, P), take(CT, P), take(CT, P)
        AR = take(CT, 2, P)
        bt, kt = take(CT, P), take(CT, P)
        btok = take(2, CT, 64)
        assert off[0] <= O_WIN
        off[0] = O_XR
        PT = take(2, CT, 64)
        ktok = take(2, CT, 64)
        vtok = take(2, CT, 64)
        GB = take(2, CT, 2, 64)
        GK = take(2, CT, 2, 64)
        RHS, UU = take(CT, 64), take(CT, 64)
        assert off[0] <= O_XR + 5 * D
        off[0] = O_WIN + NT * C
        XX = take(2, 2, CT, 64)
        MM = take(2, CT, 64)
        assert off[0] <= O_XR
        ST0 = at(O_EX, CT, 64)

        S8 = at(O_EX + CT * 64, SB, 64)
        s_stage = at(O_EX + CT * 64 + SB * 64, SB * P)
        s_raw = gain[0:64, :].rearrange("v (b n) -> v b n", b=SB)
        A8 = GB[:, 1, :, :, :].rearrange("p h e n -> p (h e n)").rearrange("p (b n) -> p b n", b=SB)
        U8 = GK[:, 1, :, :, :].rearrange("p h e n -> p (h e n)").rearrange("p (b n) -> p b n", b=SB)
        V8 = XX[:, 1, :, :, :].rearrange("p x h n -> p (x h n)").rearrange("p (b n) -> p b n", b=SB)

        gn_sq = at(O_HX, N)
        gn_bonus = at(O_HX + N, N)
        gn_rstd = at(O_HX + 2 * N, N)
        wout = at(O_XN, DC, D)
        xres = [at(O_HX + s * D, D) for s in range(3)]
        hres = at(O_ZS, NT, D)
        off[0] = O_ZS + NT * D
        xn2 = [take(D) for _ in range(2)]
        x2T = [take(DC, P) for _ in range(2)]
        squares2 = take(D)
        assert off[0] <= O_XN

        def pieces(ap3, ap2, hp):
            return ((ap3[:, 0:NT - 1, hp, :], ap2[:, 0:SEQ].rearrange("p (i n) -> p i n", n=P)),
                    (ap3[:, NT - 1, hp, 0:NS], ap2[:, SEQ:N]))

        w_rt = w_da[:, 0:DC * (NG + NE)].rearrange("p (c n) -> p c n", c=DC)
        b_rt = w0_all[:, 0:NG + NE]
        lg = at(O_EX, NT, NG + NE)

        O_RT = O_ZS + NT * D + 2 * D
        NCOL = NTILE_X
        off[0] = O_EX + 330
        r_desc = take(EG)
        r_thr = take(EG)
        r_iote = take(NE)
        r_iots = take(P)
        r_iotc = take(NCOL)
        r_val = take(2, NT, TOPK)
        assert off[0] <= O_EX + 768
        off[0] = O_CO
        r_gmax, r_pg, r_gd, r_key4, r_g1 = take(NT), take(NT), take(NT, NG), take(NT, NG), take(NT, NG)
        r_km = take(NT)
        r_e4, r_es, r_key8 = take(NT, NG, EG), take(NT, EG), take(NT, EG)
        r_m1, r_m2, r_ex, r_den = take(NT), take(NT), take(NT), take(NT)
        r_o = take(TOPK, NT, EG)
        r_oh = take(TOPK, NT, NE)
        r_m = take(NT, NE)
        r_cum = take(NT + 1, NE)
        r_c = take(NT + 1, NE)
        r_tmp = take(TOPK, NT, NE)
        assert off[0] <= O_EX
        r_rank, r_exp, r_base, r_q, r_q1, r_tile, r_slot = (
            at(O_RT + 32 * k, TOPK * NT) for k in range(7))
        off[0] = O_RT + 224
        r_qc = take(TOPK * NT, EG)
        r_xc = take(NE, EG)
        r_s = [take(2, NE) for _ in range(2)]
        r_x = take(NE)
        r_tc = take(EXTRA, NE)
        r_te = take(EXTRA)
        r_n = take(2)
        r_os = [take(P) for _ in range(2)]
        r_ot = [take(2, NCOL) for _ in range(2)]
        r_f = take(2, NCOL)
        r_z = take(2, NCOL)
        assert off[0] <= O_XN

        WSZ = 3 * DC * F
        wx = [at(O_XN + s * WSZ, WSZ) for s in range(UN)]
        assert O_XN + UN * WSZ <= O_CO
        off[0] = O_ZS + NT * D
        xgT = [take(DC, P) for _ in range(2)]
        ye = [take(D) for _ in range(2)]
        gs, gu = take(F), take(F)
        hT = take(2, P)
        assert off[0] <= O_XN
        off[0] = O_XN + UN * WSZ
        xg = [take(D) for _ in range(UN)]
        g_idx = [sb(f"g_idx{s}", [P, 1], U32) for s in range(UN)]
        s_idx = [sb(f"s_idx{s}", [P, 1], U32) for s in range(2)]
        yk = [at(O_XN + s * 2 * D, TOPK, D) for s in range(2)]
        fin = [at(O_XN + 4 * D + s * D, D) for s in range(2)]
        fin_sq = at(O_XN + 6 * D, D)

        def banks(b, n=1):
            return ps[:, b:b + n, :].rearrange("p b n -> p (b n)")

        const_ready = sem("const_ready")
        pool_chain = sem("pool_chain")
        dve_chain = sem("dve_chain")
        tables_in = sem("tables_in")
        tables_psum = sem("tables_psum")
        tables_done = sem("tables_done")
        gain1_in = sem("gain1_in")
        x_loaded = [sem(f"x_loaded{s}") for s in range(3)]
        sq_done, ms_done, std_done, xn_done = sem("sq_done"), sem("ms_done"), sem("std_done"), sem("xn_done")
        xT_psum, xT_act, xT_dve = sem("xT_psum"), sem("xT_act"), sem("xT_dve")
        w_loaded = [sem(f"w_loaded{s}") for s in range(6)]
        proj_done, proj_read = sem("proj_done"), sem("proj_read")
        sig_done = sem("sig_done")
        z_ready = sem("z_ready")
        zs_done, last_done, hx_ready, conv_tap = sem("zs_done"), sem("last_done"), sem("hx_ready"), sem("conv_tap")
        tail_psum, tail_copied = sem("tail_psum"), sem("tail_copied")

        tanh_done = sem("tanh_done")
        decay_psum, decay_sum, decay_done = sem("decay_psum"), sem("decay_sum"), sem("decay_done")
        kkr_done, iclr_psum, iclr_done, ksq_done = sem("kkr_done"), sem("iclr_psum"), sem("iclr_done"), sem("ksq_done")
        knorm_part, knorm_root, knorm_done = sem("knorm_part"), sem("knorm_root"), sem("knorm_done")
        kprep_done, kback_psum, kk_done = sem("kprep_done"), sem("kback_psum"), sem("kk_done")
        tails_out = sem("tails_out")

        cmean_psum, cdev_done, csq_done, cvar_part = (sem(n) for n in ("cmean_psum", "cdev_done", "csq_done",
                                                                       "cvar_part"))
        cvar_done, cstd_done, csig_done, cnorm_done = (sem(n) for n in (
            "cvar_done", "cstd_done", "csig_done", "cnorm_done"))
        co_done = sem("co_done")

        c_in, c_psum, e_done, prod_done = sem("c_in"), sem("c_psum"), sem("e_done"), sem("prod_done")
        prod2_done = sem("prod2_done")
        tok_psum, tok_act, tok_dve = sem("tok_psum"), sem("tok_act"), sem("tok_dve")
        gb_psum, gk_psum, gb_done, gk_done, pt_done = (sem(n) for n in ("gb_psum", "gk_psum", "gb_done", "gk_done",
                                                                        "pt_done"))
        x1t_done, m_psum, m_done, x_psum, x_done = (sem(n) for n in ("x1t_done", "m_psum", "m_done", "x_psum",
                                                                     "x_done"))
        rhs_psum, rhs_done, u_psum, u_done = (sem(n) for n in ("rhs_psum", "rhs_done", "u_psum", "u_done"))
        s_psum, s_sum, s_done, y_psum, y_done = (sem(n) for n in ("s_psum", "s_sum", "s_done", "y_psum", "y_done"))
        s0_done = sem("s0_done")
        pe_past_waits = sem("pe_past_waits")

        fin_psum, fin_copied, fin_stored = sem("fin_psum"), sem("fin_copied"), sem("fin_stored")
        s_loaded, s8_psum, s8_in = sem("s_loaded"), sem("s8_psum"), sem("s8_in")
        a8_done, uv8_done, s8_done = sem("a8_done"), sem("uv8_done"), sem("s8_done")

        gmean_psum, gdev_done, gsq_done, gvar_part = (sem(n) for n in ("gmean_psum", "gdev_done", "gsq_done",
                                                                       "gvar_part"))
        gvar_done, gstd_done, grstd_done = sem("gvar_done"), sem("gstd_done"), sem("grstd_done")
        gback_psum, gback_used, rk_done, rk_psum, rk_used = (sem(n) for n in ("gback_psum", "gback_used", "rk_done",
                                                                              "rk_psum", "rk_used"))
        gate_psum, mix_done = sem("gate_psum"), sem("mix_done")
        tables2_in = sem("tables2_in")
        o_psum, h_done, xn2_done = sem("o_psum"), sem("h_done"), sem("xn2_done")
        xn2_stored = [sem(f"xn2_stored{s}") for s in range(2)]
        lg_psum, lg_done = sem("lg_psum"), sem("lg_done")

        idx = sb("idx", [P, 2, NCOL], U32)
        te_u = sb("te_u", [1, NTILE_X], U32)
        last_turn = sb("last_turn", [1, 1], U32)
        w_k = shift0[:, :, :].rearrange("p t b -> p (t b)")[:, 0:TOPK * NT].rearrange("p (k i) -> p k i", k=TOPK)
        iota_done, softmax_in, softmax_done = sem("iota_done"), sem("softmax_in"), sem("softmax_done")
        cum_done, rank_psum, onehot_done, onehot_used, idx_done = (sem(n) for n in (
            "cum_done", "rank_psum", "onehot_done", "onehot_used", "idx_done"))

        wx_in = w_loaded[0:UN]
        wx_0 = [16 * len(range(s, MT, 6)) for s in range(UN)]
        xg_zero = sem("xg_zero")
        pool_past_waits = sem("pool_past_waits")
        gi_ready, si_ready = sem("gi_ready"), sem("si_ready")
        xg_in = [sem(f"xg_in{s}") for s in range(UN)]
        ye_out = [sem(f"ye_out{s}") for s in range(2)]
        gu_psum, gs_done, gmul_done, hx_done, ht_psum, ht_done = (sem(n) for n in (
            "gu_psum", "gs_done", "gmul_done", "hx_done", "ht_psum", "ht_done"))
        yd_psum, ye_act, ye_dve = sem("yd_psum"), sem("ye_act"), sem("ye_dve")
        yk_in = [sem(f"yk_in{s}") for s in range(2)]
        ff_done, fin_done = sem("ff_done"), sem("fin_done")
        fin_out = [sem(f"fin_out{s}") for s in range(2)]

        def expert_turns(engine, step):
            last = engine.value_load(last_turn[0:1, 0:1], min_val=NE // UN - 1, max_val=NTILE_X // UN - 1)
            with engine.Fori(0, last) as t:
                for s in range(UN):
                    step(t, s, UN)
            for s in range(UN):
                step(last, s, UN - 1 - s)
            return last

        block = ctx.enter_context(nc.Block())

        @block.sync
        def _(sp):
            def load_x(i):
                if i >= 3:
                    sp.wait_ge(xn_done, i - 2)
                src = x_prompt[0, i * P:(i + 1) * P, :] if i < NT - 1 else x_sample.rearrange("b t d -> (b t) d")
                sp.dma_start(x_in[i % 3][0:rows_of(i), :], src).then_inc(x_loaded[i % 3], 16)

            load_x(0)
            sp.dma_start(gain[:, :], norm1_g[0, :].partition_broadcast(P)).then_inc(gain1_in, 16)
            load_x(1)
            load_x(2)
            for vec, name in ((mu_shift, "mu"), (k_k, "k_k"), (k_a, "k_a"), (r_k, "r_k"), (a0, "a0"), (gn_g, "gn_g"),
                              (gn_b, "gn_b"), (conv_b, "conv_b"), (conv_ln_g, "ln_g"), (conv_ln_b, "ln_b")):
                r0, n = PR[name]
                sp.dma_start(ld_prm[r0:r0 + n, :], vec[0, :].rearrange("(t p) -> t p", p=P)).then_inc(tables_in, 16)
            sp.dma_start(ld_cw[0:W * CT, :], conv_w[0].rearrange("k (c p) -> (k c) p", p=P)).then_inc(tables_in, 16)
            sp.dma_start(ld_shift[0:SB, :], state_shift[0]).then_inc(tables_in, 16)
            sc = state_conv[0].rearrange("(h b) k c -> h (b k) c", h=2)
            for h in range(2):
                sp.dma_start(ld_conv[0:4 * HB, h, :], sc[h]).then_inc(tables_in, 16)
            sp.dma_start(w0_all[:, :], w0[0, :].partition_broadcast(P)).then_inc(tables_in, 16)
            sp.dma_start(w_da[0:64, :], w_decay_up[0]).then_inc(tables_in, 16)
            sp.dma_start(w_da[64:128, :], w_aaa_up[0]).then_inc(tables_in, 16)
            sp.dma_start(w_g[:, :], w_gate_up[0]).then_inc(tables_in, 16)
            for i in range(3, NT):
                load_x(i)
            for q, t in enumerate(ORDER):
                if q >= 6:
                    sp.wait_ge(proj_done, q - 5)
                sp.dma_start(win[q % 6][:, :, :], w_in[0, :, t * P:(t + 1) * P].rearrange("(c p) n -> p c n", p=P))\
                    .then_inc(w_loaded[q % 6], 16)

            sp.wait_ge(tail_copied, 2)
            sp.dma_start(new_shift_p[0], shift_tail[0:1, :]).then_inc(tails_out, 16)
            sp.dma_start(new_shift_s[0], shift_tail[1:1 + SB, :]).then_inc(tails_out, 16)
            sp.wait_ge(tail_copied, 6)
            sp.dma_start(new_conv_p[0, 0], conv_tail[0:HB, 0, :]).then_inc(tails_out, 16)
            for g, (b0, b1) in enumerate(TG):
                for b in range(b0, b1):
                    r0 = (b - b0) * SK + ST
                    sp.dma_start(new_conv_s[0, b], conv_tail[r0:r0 + HB, 1 + g, :]).then_inc(tails_out, 16)

            def load_states(hp):
                for p in range(2):
                    sp.dma_start(s_raw[:, :, p * 64:p * 64 + 64], state_wkv[0, :, 2 * hp + p].rearrange(
                        "b v k -> v b k")).then_inc(s_loaded, 16)

            load_states(0)
            for hp in range(-1, CT):
                sp.wait_ge(fin_copied, hp + 2)
                for p in range(2):
                    if hp < 0:
                        sp.dma_start(new_wkv_p[0, 0].rearrange("(h p) v k -> p v h k", p=2)[p],
                                     s_stage[0:64, 0:CT * P].rearrange("v (h p k) -> v h p k", h=CT, p=2)[:, :, p, :])\
                            .then_inc(fin_stored, 16)
                    else:
                        sp.dma_start(new_wkv_s[0, :, 2 * hp + p].rearrange("b v k -> v b k"),
                                     s_stage[0:64, :].rearrange("v (b p k) -> v b p k", b=SB, p=2)[:, :, p, :])\
                            .then_inc(fin_stored, 16)
                if 0 <= hp < CT - 1:
                    load_states(hp + 1)



            sp.wait_ge(prod_done, NT)
            sp.dma_start(wout, w_out[0].rearrange("(c p) n -> p c n", p=P)).then_inc(tables2_in, 16)
            sp.wait_ge(s8_psum, CT)
            sp.dma_start(gain[:, :], norm2_g[0, :].partition_broadcast(P)).then_inc(tables2_in, 16)
            sp.dma_start(w_rt[:, :, 0:NG], w_router_group[0].rearrange("(p c) n -> p c n", c=DC)).then_inc(tables2_in, 16)
            sp.dma_start(w_rt[:, :, NG:], w_router_expert[0].rearrange("(p c) n -> p c n", c=DC)).then_inc(tables2_in, 16)
            sp.dma_start(b_rt[:, 0:NG], b_router_group[0, :].partition_broadcast(P)).then_inc(tables2_in, 16)
            sp.dma_start(b_rt[:, NG:], b_router_expert[0, :].partition_broadcast(P)).then_inc(tables2_in, 16)
            sp.wait_ge(mix_done, CT)
            for i in range(NT):
                r = rows_of(i)
                if i >= 3:
                    sp.wait_ge(h_done, i - 2)
                src = x_prompt[0, i * P:(i + 1) * P, :] if i < NT - 1 else x_sample.rearrange("b t d -> (b t) d")
                sp.dma_start(xres[i % 3][0:r, :], src).then_inc(x_loaded[i % 3], 16)
                if i >= 2:
                    j = i - 2
                    sp.wait_ge(xn2_done, j + 1)
                    sp.dma_start(xn2_rows[j * P:j * P + rows_of(j), :], xn2[j % 2][0:rows_of(j), :])\
                        .then_inc(xn2_stored[j % 2], 16)
            for j in range(NT - 2, NT):
                sp.wait_ge(xn2_done, j + 1)
                sp.dma_start(xn2_rows[j * P:j * P + rows_of(j), :], xn2[j % 2][0:rows_of(j), :])\
                    .then_inc(xn2_stored[j % 2], 16)

            def load_expert(e, s):
                for part, (w, m) in enumerate(((w_exp_gate, DC), (w_exp_up, DC), (w_exp_down, 2))):
                    src = w[0].rearrange("g e (p c) n -> (g e) p (c n)", c=m)
                    sp.dma_start(wx[s][:, part * DC * F:(part + 1) * DC * F],
                                 src[bass.ds(e, 1), :, :].rearrange("a p n -> (a p) n"))\
                        .then_inc(wx_in[s], 16)

            sp.wait_ge(o_psum, NT)
            sp.wait_ge(h_done, NT)
            for s in range(UN):
                load_expert(s, s)
            sp.wait_ge(idx_done, 1)
            last_sp = sp.value_load(last_turn[0:1, 0:1], min_val=NE // UN - 1, max_val=NTILE_X // UN - 1)
            with sp.Fori(0, last_sp) as t:
                for s in range(UN):
                    sp.wait_ge(yd_psum, UN * t + s + 1)
                    e = sp.value_load(te_u[0:1, bass.ds(UN * t + s + UN, 1)], min_val=0, max_val=NE - 1)
                    load_expert(e, s)
            sp.dma_start(gain[:, :], norm_f_g.partition_broadcast(P)).then_inc(tables2_in, 16)
            for s in range(2):
                sp.wait_ge(ye_out[s], last_sp * (16 * UN // 2) + 16 * UN // 2)
            sp.wait_ge(yd_psum, last_sp * UN + UN)
            y_pairs = y_rows.rearrange("(n k) d -> n k d", k=TOPK)

            def result_out(i):
                r = rows_of(i)
                sp.wait_ge(fin_done, i + 1)
                dst = y_prompt[0, i * P:(i + 1) * P, :] if i < NT - 1 else y_sample.rearrange("b t d -> (b t) d")
                sp.dma_start(dst, fin[i % 2][0:r, :]).then_inc(fin_out[i % 2], 16)

            for i in range(NT):
                r = rows_of(i)
                if i >= 2:
                    sp.wait_ge(ff_done, i - 1)
                sp.dma_start(yk[i % 2][0:r, :, :], y_pairs[i * P:i * P + r, :, :]).then_inc(yk_in[i % 2], 16)
                if i >= 2:
                    result_out(i - 2)
            for i in range(NT - 2, NT):
                result_out(i)
            sp.wait_ge(fin_out[0], 16 * ((NT + 1) // 2))
            sp.wait_ge(fin_out[1], 16 * (NT // 2))
            sp.wait_ge(fin_stored, 32 * (CT + 1))
            sp.wait_ge(tails_out, 16 * (3 + SB))

        N_TABLES = 18

        @block.gpsimd
        def _(pool):
            step = [0]

            def link(ins):
                step[0] += 1
                ins.then_inc(pool_chain, 1)
                pool.wait_ge(pool_chain, step[0])

            def select(v, cmp, base, cm, pattern, fill=0.0):
                link(pool.affine_select(out=v, in_=v, compare_op=cmp, fill=fill, base=base, pattern=pattern,
                                        channel_multiplier=cm))

            link(pool.memset(ident[:, :], 0.0))
            select(ident[:, :], ALU.not_equal, 0, 1, [[-1, P]], 1.0)
            link(pool.memset(tri_cum[:, :, :, :], LOGW))
            select(tri_cum[:, 0, :, :], ALU.is_ge, 0, -1, [[64, 2], [1, 64]])
            select(tri_cum[:, 1, :, :], ALU.is_ge, -1, -1, [[64, 2], [1, 64]])
            for e in range(2):
                select(tri_cum[:, e, :, :], ALU.is_ge, 0, 1, [[-64, 2], [0, 64]])
            link(pool.memset(tri_cum8[:, :, :], LOGW))
            select(tri_cum8[:, 0, :], ALU.is_ge, 0, -1, [[1, 64]])
            select(tri_cum8[:, 1, :], ALU.is_ge, -1, -1, [[1, 64]])
            for e in range(2):
                select(tri_cum8[:, e, :], ALU.is_ge, 0, 1, [[-ST, SB], [0, ST]])
            link(pool.memset(mask_ar[0:64, :, :], 1.0))
            select(mask_ar[0:64, 0, :], ALU.is_ge, -1, -1, [[1, 64]])
            select(mask_ar[0:64, 1, :], ALU.is_ge, 0, -1, [[1, 64]])
            link(pool.memset(mask_ar8[0:64, :, :], 1.0))
            select(mask_ar8[0:64, 0, :], ALU.is_ge, -1, -1, [[1, 64]])
            select(mask_ar8[0:64, 1, :], ALU.is_ge, 0, -1, [[1, 64]])
            for e in range(2):
                select(mask_ar8[0:64, e, :], ALU.is_ge, 0, 1, [[-ST, SB], [0, ST]])
            link(pool.memset(mask_lv[0:64, :, :], 1.0))
            for k in range(LV):
                m = 1 << k
                blocks = [[0, 32 // m], [0, 2 * m]]
                v = mask_lv[0:64, k, :]
                select(v, ALU.is_ge, -m, 1, [[-2 * m, 32 // m], [0, 2 * m]])
                select(v, ALU.is_ge, 2 * m - 1, -1, [[2 * m, 32 // m], [0, 2 * m]])
                select(v, ALU.is_ge, m - 1, 0, [[0, 32 // m], [-1, 2 * m]])
                select(v, ALU.not_equal, 0, 1, [[-1, 64]], 1.0)
            link(pool.memset(mask_lv0t[0:64, :], 1.0))
            select(mask_lv0t[0:64, :], ALU.is_ge, 0, 1, [[-2, 32], [0, 2]])
            select(mask_lv0t[0:64, :], ALU.is_ge, 0, -1, [[2, 32], [0, 2]])
            select(mask_lv0t[0:64, :], ALU.is_ge, -1, 0, [[0, 32], [1, 2]])
            select(mask_lv0t[0:64, :], ALU.not_equal, 0, 1, [[-1, 64]], 1.0)
            link(pool.memset(rowmask[0:64, :], 1.0))
            select(rowmask[0:64, :], ALU.is_ge, 0, 1, [[-ST, SB]])
            select(rowmask[0:64, :], ALU.is_ge, ST - 1, -1, [[ST, SB]])
            link(pool.memset(seqmask[:, :, :], 1.0))
            select(seqmask[:, :, :], ALU.is_ge, 0, 0, [[-ST, SB], [1, 64]])
            select(seqmask[:, :, :], ALU.is_ge, ST - 1, 0, [[ST, SB], [-1, 64]])
            for m, v in ((headsum, 1.0), (headmean, 1.0 / HD)):
                link(pool.memset(m[:, :], 0.0))
                link(pool.memset(m[0:64, 0:64], v))
                link(pool.memset(m[64:128, 64:128], v))
            link(pool.memset(head_sel[:, :, :], 0.0))
            for hp in range(CT):
                link(pool.memset(head_sel[0:64, hp, 2 * hp:2 * hp + 1], 1.0))
                link(pool.memset(head_sel[64:128, hp, 2 * hp + 1:2 * hp + 2], 1.0))
            link(pool.memset(head_back[:, :, :], 0.0))
            for hp in range(CT):
                select(head_back[:, hp, :], ALU.not_equal, 2 * hp, -1, [[1, 2], [0, 64]], 1.0)
            link(pool.memset(chmean[:, :], 1.0 / C))
            link(pool.memset(ones[:, :], 1.0))
            link(pool.memset(before[:, :], 1.0))
            pool.affine_select(out=before[:, :], in_=before[:, :], compare_op=ALU.is_ge, fill=0.0, base=-1,
                               pattern=[[1, P]], channel_multiplier=-1).then_inc(const_ready, 1)

            for j in range(ZT):
                q = NCONV + j
                zt = ORDER[q] - 8
                pool.wait_ge(z_ready, j + 1)
                pool.tensor_copy(lastz[:, zt, 0:1], zbuf[j % 2][:, SEQ:SEQ + 1])
                pool.tensor_copy(lastz[:, zt, 1:1 + SB], zbuf[j % 2][:, 1 + SEQ:].rearrange(
                    "p (b t) -> p b t", b=SB)[:, :, ST]).then_inc(last_done, 1)
            pool.wait_ge(kk_done, CT)
            pool.wait_ge(co_done, CT)
            pool.wait_ge(decay_done, NT)
            pool.memset(ST0, 0.0).then_inc(s0_done, 1)

            def stage_in(i, r):
                pool.wait_ge(c_psum, i)
                pool.tensor_copy(lwst[0:r, :].rearrange("p (a n) -> p a n", a=1), sgw[0:r, bass.ds(i, 1), :])
                pool.wait_ge(tok_psum, 3 * i)
                pool.tensor_copy(vst[:, :, 0:r], zs[:, V0:V0 + CT, bass.ds(i * P, r)]).then_inc(c_in, 1)

            def scaled_r_k(i, r):
                pool.wait_ge(e_done, i + 1)
                pool.wait_ge(y_done, 2 * i)
                pool.wait_ge(s_done, 2 * i)
                pool.tensor_tensor(AR[:, :, 1, 0:r], zs[:, R0:R0 + CT, bass.ds(i * P, r)], e_in[:, :, 0:r], ALU.mult)
                pool.tensor_tensor(kt[:, :, 0:r], zs[:, K0:K0 + CT, bass.ds(i * P, r)], e_neg[:, :, 0:r], ALU.mult)\
                    .then_inc(prod2_done, 1)

            def x1t(n, c):
                pool.wait_ge(pt_done, n + 1)
                pool.tensor_tensor(XX[:, c, 1, :, :], PT[:, c, :, :],
                                   mask_lv0t[:, :].unsqueeze(1).broadcast_to([P, CT, 64]), ALU.mult)\
                    .then_inc(x1t_done, 1)

            with pool.Fori(0, NT - 1) as i:
                stage_in(i, P)
                scaled_r_k(i, P)
                for c in range(2):
                    x1t(2 * i + c, c)
            stage_in(NT - 1, NS)
            scaled_r_k(NT - 1, NS)
            x1t(2 * (NT - 1), 0)

            pool.wait_ge(fin_psum, CT + 1)
            for v, pattern, base, cm in ((r_desc, [[-1, EG]], EG, 0), (r_thr, [[P, EG]], P, 0), (r_iote, [[1, NE]], 0, 0),
                                         (r_iots, [[1, P]], 0, 0), (r_iotc, [[1, NCOL]], 0, 0),
                                         (r_val[:, 0, :, :], [[TOPK * P, NT], [1, TOPK]], 1, TOPK),
                                         (r_val[:, 1, :, :], [[P, NT], [0, TOPK]], 1, 1)):
                ins = pool.iota(v, pattern=pattern, base=base, channel_multiplier=cm,
                                allow_small_or_imprecise_dtypes=True)
            ins.then_inc(iota_done, 1)

            pool.wait_ge(idx_done, 1)
            pool.wait_ge(xn2_stored[0], 16 * ((NT + 1) // 2))
            pool.wait_ge(xn2_stored[1], 16 * (NT // 2))
            pool.wait_ge(lg_done, NT)
            for s in range(UN):
                ins = pool.memset(xg[s], 0.0)
            ins.then_inc(xg_zero, 1)
            pool.wait_ge(xg_zero, 1)

            def gather(u, s):
                pool.tensor_copy(g_idx[s][:, :], idx[:, 1, bass.ds(u, 1)]).then_inc(gi_ready, 1)
                pool.wait_ge(gi_ready, u + 1)
                pool.sem_inc(pool_past_waits, 1)
                pool.indirect_dma_start(out=xg[s], out_offset=None, in_=xn2_rows,
                                        in_offset=bass.IndirectOffsetOnAxis(ap=g_idx[s][:, :], axis=0),
                                        bounds_check=N - 1, oob_is_err=False).then_inc(xg_in[s], 16)

            def scatter(u, s):
                pool.wait_ge(ye_act, u + 1)
                pool.wait_ge(ye_dve, u + 1)
                pool.tensor_copy(s_idx[s][:, :], idx[:, 0, bass.ds(u, 1)]).then_inc(si_ready, 1)
                pool.wait_ge(si_ready, u + 1)
                pool.sem_inc(pool_past_waits, 1)
                pool.indirect_dma_start(out=y_rows, out_offset=bass.IndirectOffsetOnAxis(ap=s_idx[s][:, :], axis=0),
                                        in_=ye[s], in_offset=None, bounds_check=N * TOPK - 1, oob_is_err=False)\
                    .then_inc(ye_out[s], 16)

            def pool_step(turn, s, ahead):
                u = UN * turn + s
                if ahead >= 3:
                    pool.wait_ge(xT_psum, 2 * NT + u)
                    gather(u + 3, (s + 3) % UN)
                scatter(u, s % 2)

            for u in range(3):
                gather(u, u)
            expert_turns(pool, pool_step)


        @block.scalar
        def _(act):
            def square(i):
                r = rows_of(i)
                act.wait_ge(x_loaded[i % 3], 16 * (i // 3 + 1))
                act.activation(squares[0:r, :], x_in[i % 3][0:r, :], ACT.Square,
                               accum_out=stat[0:r, 0, i:i + 1]).then_inc(sq_done, 1)

            def root(i):
                r = rows_of(i)
                act.wait_ge(ms_done, i + 1)
                act.activation(stat[0:r, 2, i:i + 1], stat[0:r, 1, i:i + 1], ACT.Sqrt).then_inc(std_done, 1)

            def copy_T(i):
                act.wait_ge(xT_psum, i + 1)
                r = rows_of(i)
                act.activation(xnT[:, 0:4, i * P:i * P + r],
                               banks(2 * (i % 2)).rearrange("p (c n) -> p c n", c=4)[:, :, 0:r], ACT.Copy)\
                    .then_inc(xT_act, 1)

            square(0)
            root(0)
            square(1)
            root(1)
            for i in range(NT):
                if i + 2 < NT:
                    square(i + 2)
                    root(i + 2)
                copy_T(i)

            for q, t in enumerate(ORDER):
                pr = banks(3 * (q % 2), 3)
                act.wait_ge(proj_done, q + 1)
                if q < NCONV:
                    if q % 2 == 0:
                        if q >= 2:
                            act.wait_ge(hx_ready, q // 2)
                        else:
                            act.wait_ge(xn_done, NT)
                            act.wait_ge(xT_psum, NT)
                        act.activation(sig[:, :], pr[:, 0:N], ACT.Sigmoid).then_inc(sig_done, 1)
                    continue
                j = q - NCONV
                zb = zbuf[j % 2]
                if j >= 2:
                    act.wait_ge(zs_done, j - 1)
                    act.wait_ge(last_done, j - 1)
                act.activation(zb[:, 1:1 + SEQ], pr[:, 0:SEQ], ACT.Copy)
                act.activation(zb[:, 1 + SEQ:].rearrange("p (b t) -> p b t", b=SB)[:, :, 1:],
                               pr[:, SEQ:N].rearrange("p (b t) -> p b t", b=SB), ACT.Copy)
                act.activation(zb[:, 1 + SEQ:].rearrange("p (b t) -> p b t", b=SB)[:, :, 0],
                               shift0[:, t - 8, :], ACT.Copy)
                act.activation(zb[:, 0:1], stat[:, 7, 0:1], ACT.Copy).then_inc(z_ready, 1)

            act.wait_ge(zs_done, ZT)
            act.activation(zs[0:64, WA0, :], zs[0:64, WA0, :], ACT.Tanh)
            act.activation(zs[:, GL0, :], zs[:, GL0, :], ACT.Sigmoid).then_inc(tanh_done, 1)
            for h in range(2):
                act.wait_ge(tail_psum, h + 1)
                act.activation(shift_tail[0:1 + SB, h * 7 * P:(h + 1) * 7 * P], banks(6, 2)[0:1 + SB, 0:7 * P],
                               ACT.Copy).then_inc(tail_copied, 1)
            for j, rows in enumerate([HB] + [(b1 - b0) * SK for b0, b1 in TG]):
                act.wait_ge(tail_psum, 3 + j)
                act.activation(conv_tail[0:rows, j, :], banks((6, 7, 6, 7)[j])[0:rows, :], ACT.Copy)\
                    .then_inc(tail_copied, 1)
            for i in range(NT):
                act.wait_ge(decay_sum, i + 1)
                r = rows_of(i)
                act.activation(sgw[0:r, i, :], sgw[0:r, i, :], ACT.Sigmoid).then_inc(decay_done, 1)
            for hp in range(CT):
                act.wait_ge(iclr_psum, hp + 1)
                if hp >= 2:
                    act.wait_ge(kprep_done, hp - 1)
                a0_col = PR["a0"][0] + hp
                act.activation(iclr[hp % 2], banks(3, 3)[:, 0:N], ACT.Sigmoid, bias=prm[:, a0_col:a0_col + 1])\
                    .then_inc(iclr_done, 1)
                act.wait_ge(kkr_done, hp + 1)
                if hp >= 1:
                    act.wait_ge(knorm_part, hp)
                act.activation(ksq, nkk[:, hp, :], ACT.Square).then_inc(ksq_done, 1)
            act.wait_ge(knorm_part, CT)
            act.activation(knorm[0:8, :], banks(0, 3)[0:8, 0:N], ACT.Sqrt).then_inc(knorm_root, 1)

            for c in range(CT):
                act.wait_ge(cdev_done, c + 1)
                act.wait_ge(knorm_part, CT)
                if c:
                    act.wait_ge(cvar_part, c)
                act.activation(conv_sq, co[:, c, :], ACT.Square).then_inc(csq_done, 1)
            act.wait_ge(cvar_done, 1)
            act.activation(conv_rstd, conv_rstd, ACT.Sqrt).then_inc(cstd_done, 1)
            for c in range(CT):
                act.wait_ge(cnorm_done, c + 1)
                if c:
                    act.wait_ge(co_done, c)
                g0, b0 = PR["ln_g"][0] + c, PR["ln_b"][0] + c
                act.activation(conv_sig, co[:, c, :], ACT.Sigmoid, scale=prm[:, g0:g0 + 1], bias=prm[:, b0:b0 + 1])\
                    .then_inc(csig_done, 1)

            def exps(i, r, cum_in, cum_ex):
                act.wait_ge(c_psum, i + 1)
                act.wait_ge(s_done, 2 * i)
                act.activation(e_in[:, :, 0:r], cum_in, ACT.Exp)
                act.activation(e_neg[:, :, 0:r], cum_in, ACT.Exp, scale=-1.0)
                act.activation(e_ex[:, :, 0:r], cum_ex, ACT.Exp).then_inc(e_done, 1)

            def tok_copies(i, r):
                for j, (dst, b) in enumerate(((vtok, 0), (btok, 1), (ktok, 0))):
                    act.wait_ge(tok_psum, 3 * i + j + 1)
                    src = banks(b).rearrange("p (h n) -> p h n", h=CT)
                    act.activation(dst[0:64, 0, :, :], src[0:64, :, 0:64], ACT.Copy)
                    act.activation(dst[64:128, 0, :, :], src[0:64, :, 64:128], ACT.Copy).then_inc(tok_act, 1)

            def x_copy(n, c, both=True):
                act.wait_ge(x_psum, n + 1)
                src = banks(6 + c).rearrange("p (x h n) -> p x h n", x=2, h=CT)
                if both:
                    act.activation(XX[:, c, :, :, :], src, ACT.Copy).then_inc(x_done, 1)
                else:
                    act.activation(XX[:, c, 1, :, :], src[:, 1, :, :], ACT.Copy).then_inc(x_done, 1)

            def rhs_copy(n):
                act.wait_ge(rhs_psum, n + 1)
                act.activation(RHS, banks(2)[:, 0:CT * 64].rearrange("p (h n) -> p h n", h=CT), ACT.Copy)\
                    .then_inc(rhs_done, 1)

            def y_copy(i, n, c):
                act.wait_ge(y_psum, n + 1)
                act.activation(yT[:, bass.ds(i, 1), :, c * 64:c * 64 + 64].rearrange("p a h n -> p (a h) n"),
                               banks(4)[:, 0:CT * 64].rearrange("p (h n) -> p h n", h=CT), ACT.Copy)\
                    .then_inc(y_done, 1)

            act.wait_ge(co_done, CT)
            cum = ps[:, 0:2, :].rearrange("p b (h e n) -> p (b h) e n", h=2, e=2)
            with act.Fori(0, NT - 1) as i:
                exps(i, P, cum[:, :, 0, :], cum[:, :, 1, :])
                tok_copies(i, P)
                for k in range(1, LV):
                    for c in range(2):
                        x_copy(2 * (LV - 1) * i + 2 * (k - 1) + c, c, k < LV - 1)
                for c in range(2):
                    rhs_copy(2 * i + c)
                    y_copy(i, 2 * i + c, c)

            def final_copy(n, width):
                act.wait_ge(fin_psum, n + 1)
                if n:
                    act.wait_ge(fin_stored, 32 * n)
                act.activation(s_stage[0:64, 0:width], banks(0, 2)[0:64, 0:width], ACT.Copy).then_inc(fin_copied, 1)

            final_copy(0, CT * P)
            i8, n8 = NT - 1, 2 * (NT - 1)
            exps(i8, NS, banks(0).rearrange("p (h e n) -> p h e n", h=CT, e=2)[:, :, 0, :],
                 banks(0).rearrange("p (h e n) -> p h e n", h=CT, e=2)[:, :, 1, :])
            tok_copies(i8, NS)
            for k in range(1, LV8):
                x_copy(2 * (LV - 1) * i8 + k - 1, 0, k < LV8 - 1)
            for hp in range(CT):
                act.wait_ge(s8_psum, hp + 1)
                if hp:
                    act.wait_ge(fin_psum, hp + 1)
                act.activation(S8, banks(7).rearrange("p (b n) -> p b n", b=SB), ACT.Copy).then_inc(s8_in, 1)
                act.wait_ge(rhs_psum, n8 + hp + 1)
                act.activation(RHS[:, hp, :], banks(2)[:, 0:64], ACT.Copy).then_inc(rhs_done, 1)
                act.wait_ge(y_psum, n8 + hp + 1)
                act.activation(yT[:, i8, hp, 0:64], banks(4)[:, 0:64], ACT.Copy).then_inc(y_done, 1)
                final_copy(hp + 1, SB * P)

            for hp in range(CT):
                act.wait_ge(gdev_done, hp + 1)
                if hp:
                    act.wait_ge(gvar_part, hp)
                for m, (y3, flat) in enumerate(pieces(yT, gn_sq, hp)):
                    ins = act.activation(flat, y3, ACT.Square)
                ins.then_inc(gsq_done, 1)
            act.wait_ge(gvar_done, 1)
            act.activation(gn_rstd[0:8, :], gn_rstd[0:8, :], ACT.Sqrt).then_inc(gstd_done, 1)

            def square2(i):
                r = rows_of(i)
                act.wait_ge(h_done, i + 1)
                act.activation(squares2[0:r, :], hres[0:r, i, :], ACT.Square, accum_out=stat[0:r, 4, i:i + 1])\
                    .then_inc(sq_done, 1)
                act.wait_ge(ms_done, NT + i + 1)
                act.activation(stat[0:r, 6, i:i + 1], stat[0:r, 5, i:i + 1], ACT.Sqrt).then_inc(std_done, 1)

            def copy_T2(i):
                r = rows_of(i)
                act.wait_ge(xT_psum, NT + i + 1)
                if i >= 2:
                    act.wait_ge(lg_psum, i - 1)
                act.activation(x2T[i % 2][:, 0:4, 0:r], banks(4).rearrange("p (c n) -> p c n", c=4)[:, :, 0:r],
                               ACT.Copy).then_inc(xT_act, 1)

            for i in range(NT):
                square2(i)
                if i:
                    copy_T2(i - 1)
            copy_T2(NT - 1)

            act.wait_ge(softmax_in, 1)
            act.activation(r_gd, r_gd, ACT.Exp).then_inc(softmax_done, 1)
            act.wait_ge(softmax_in, 2)
            act.activation(r_ex, r_ex, ACT.Exp).then_inc(softmax_done, 1)

            def sigmoid(u, s):
                act.wait_ge(gu_psum, u + 1)
                act.wait_ge(hx_done, u)
                act.activation(gs, banks(s % 2)[:, 0:F], ACT.Sigmoid).then_inc(gs_done, 1)

            def copy_xg(u, s):
                act.wait_ge(xT_psum, 2 * NT + u + 1)
                act.activation(xgT[s % 2][:, 0:4, :], banks(2).rearrange("p (c n) -> p c n", c=4), ACT.Copy)\
                    .then_inc(xT_act, 1)

            def act_step(turn, s, ahead):
                u = UN * turn + s
                if ahead >= 1:
                    sigmoid(u + 1, s + 1)
                if ahead >= 2:
                    copy_xg(u + 2, s)
                act.wait_ge(yd_psum, u + 1)
                act.wait_ge(ye_out[s % 2], 16 * ((UN // 2) * turn + s // 2))
                act.activation(ye[s % 2][:, 0:512], banks(5), ACT.Copy).then_inc(ye_act, 1)

            copy_xg(0, 0)
            sigmoid(0, 0)
            copy_xg(1, 1)
            last_act = expert_turns(act, act_step)

            act.wait_ge(yd_psum, last_act * UN + UN)
            for i in range(NT):
                r = rows_of(i)
                act.wait_ge(ff_done, i + 1)
                act.activation(fin_sq[0:r, :], hres[0:r, i, :], ACT.Square, accum_out=stat[0:r, 0, i:i + 1])\
                    .then_inc(sq_done, 1)
                act.wait_ge(ms_done, 2 * NT + i + 1)
                act.activation(stat[0:r, 2, i:i + 1], stat[0:r, 1, i:i + 1], ACT.Sqrt).then_inc(std_done, 1)

        @block.tensor
        def _(pe):
            pe.wait_ge(const_ready, 1)
            pe.wait_ge(tables_in, 16 * N_TABLES)
            tb = banks(6)
            pe.transpose(tb[:, 0:NPR], ld_prm[0:NPR, :], ident[0:NPR, 0:NPR])
            pe.transpose(tb[:, 64:64 + W * CT], ld_cw[0:W * CT, :], ident[0:W * CT, 0:W * CT])
            for t in range(ZT):
                pe.transpose(tb[:, 192 + SB * t:192 + SB * (t + 1)], ld_shift[0:SB, t * P:(t + 1) * P],
                             ident[0:SB, 0:SB])
            for h in range(2):
                for c in range(CT):
                    ins = pe.transpose(banks(4 + h)[:, c * 4 * HB:(c + 1) * 4 * HB],
                                       ld_conv[0:4 * HB, h, c * P:(c + 1) * P], ident[0:4 * HB, 0:4 * HB])
            ins.then_inc(tables_psum, 1)

            for i in range(NT):
                r = rows_of(i)
                pe.wait_ge(xn_done, i + 1)
                if i >= 2:
                    pe.wait_ge(xT_act, i - 1)
                    pe.wait_ge(xT_dve, i - 1)
                for c in range(DC):
                    ins = pe.transpose(banks(2 * (i % 2) + c // 4)[:, (c % 4) * P:(c % 4) * P + r],
                                       xn[i % 2][0:r, c * P:(c + 1) * P], ident[0:r, 0:r])
                ins.then_inc(xT_psum, 1)

            pe.wait_ge(xT_act, NT)
            pe.wait_ge(xT_dve, NT)
            pe.wait_ge(tables_done, 1)
            for q in range(MT):
                pe.wait_ge(w_loaded[q % 6], 16 * (q // 6 + 1))
                if q >= 2:
                    if q - 2 < NCONV:
                        if (q - 2) % 2 == 0:
                            pe.wait_ge(sig_done, (q - 2) // 2 + 1)
                        else:
                            pe.wait_ge(hx_ready, (q - 2) // 2 + 1)
                    else:
                        pe.wait_ge(z_ready, q - 2 - NCONV + 1)
                pr = banks(3 * (q % 2), 3)
                for n0 in range(0, N, 512):
                    n1 = min(n0 + 512, N)
                    for c in range(DC):
                        ins = pe.matmul(pr[:, n0:n1], win[q % 6][:, c, :], xnT[:, c, n0:n1],
                                        start=(c == 0), stop=(c == DC - 1))
                ins.then_inc(proj_done, 1)

            def tail(step, dst, srcs):
                if step:
                    pe.wait_ge(tail_copied, step)
                else:
                    pe.wait_ge(last_done, ZT)
                    pe.wait_ge(hx_ready, CT)
                for j, src in enumerate(srcs):
                    ins = pe.transpose(dst[0:src.shape[1], j * P:(j + 1) * P], src, ident[:, :])
                ins.then_inc(tail_psum, 1)

            for h in range(2):
                tail(h, banks(6, 2), [lastz[:, 7 * h + t, :] for t in range(7)])
            tail(2, banks(6), [hx[:, c, SEQ:SEQ + HB] for c in range(CT)])
            for g, (b0, b1) in enumerate(TG):
                tail(3 + g, banks(7 - g % 2), [hx[:, c, HB + SEQ + b0 * SK:HB + SEQ + b1 * SK] for c in range(CT)])

            pe.wait_ge(tail_copied, 6)
            pe.wait_ge(tanh_done, 1)
            for i in range(NT):
                r = rows_of(i)
                if i >= 2:
                    pe.wait_ge(decay_sum, i - 1)
                pe.matmul(banks(6 + i % 2)[0:r, :], zs[0:64, WA0, i * P:i * P + r], w_da[0:64, :],
                          start=True, stop=True).then_inc(decay_psum, 1)
            kn = banks(0, 3)
            for hp in range(CT):
                if hp >= 1:
                    pe.wait_ge(iclr_done, hp)
                for n0 in range(0, N, 512):
                    n1 = min(n0 + 512, N)
                    ins = pe.matmul(banks(3, 3)[:, n0:n1], w_da[64:128, hp * P:(hp + 1) * P], zs[64:128, WA0, n0:n1],
                                    start=True, stop=True)
                ins.then_inc(iclr_psum, 1)
                pe.wait_ge(ksq_done, hp + 1)
                for n0 in range(0, N, 512):
                    n1 = min(n0 + 512, N)
                    ins = pe.matmul(kn[0:8, n0:n1], head_sel[:, hp, :], ksq[:, n0:n1], start=(hp == 0),
                                    stop=(hp == CT - 1))
                ins.then_inc(knorm_part, 1)
            pe.wait_ge(knorm_done, 1)
            pe.wait_ge(iclr_done, CT)
            for hp in range(CT):
                if hp >= 2:
                    pe.wait_ge(kk_done, hp - 1)
                for n0 in range(0, N, 512):
                    n1 = min(n0 + 512, N)
                    ins = pe.matmul(banks(3 * (hp % 2), 3)[:, n0:n1], head_back[:, hp, :], knorm[0:8, n0:n1],
                                    start=True, stop=True)
                ins.then_inc(kback_psum, 1)

            pe.wait_ge(kk_done, CT)
            pe.wait_ge(conv_tap, 2 * CT * W)
            for n0 in range(0, N, 512):
                n1 = min(n0 + 512, N)
                for c in range(CT):
                    ins = pe.matmul(banks(0, 3)[:, n0:n1], chmean[:, :], co[:, c, n0:n1], start=(c == 0),
                                    stop=(c == CT - 1))
            ins.then_inc(cmean_psum, 1)
            for c in range(CT):
                pe.wait_ge(csq_done, c + 1)
                for n0 in range(0, N, 512):
                    n1 = min(n0 + 512, N)
                    ins = pe.matmul(banks(3, 3)[:, n0:n1], chmean[:, :], conv_sq[:, n0:n1], start=(c == 0),
                                    stop=(c == CT - 1))
                ins.then_inc(cvar_part, 1)
            pe.wait_ge(cdev_done, CT)
            pe.wait_ge(cvar_done, 1)

            def carry_waits():
                pe.sem_inc(pe_past_waits, 1)

            def cumulate(i, r):
                pe.wait_ge(c_in, i + 1)
                pe.wait_ge(tok_act, 3 * i)
                pe.wait_ge(tok_dve, 3 * i)
                for hp in range(CT):
                    if r == P:
                        ins = pe.matmul(banks(hp // 2)[:, hp % 2 * 256:hp % 2 * 256 + 256],
                                        lwst[:, hp * P:(hp + 1) * P], tri_cum[:, :, :, :].rearrange(
                                            "p e c t -> p (e c t)"), start=True, stop=True)
                    else:
                        ins = pe.matmul(banks(0)[:, hp * P:hp * P + P], lwst[0:r, hp * P:(hp + 1) * P],
                                        tri_cum8[:, :, :].rearrange("p e t -> p (e t)"), start=True, stop=True)
                ins.then_inc(c_psum, 1)

            def to_tokens(b, src, r):
                for hp in range(CT):
                    ins = pe.transpose(banks(b)[0:r, hp * P:(hp + 1) * P], src[:, hp, 0:r], ident[:, :])
                ins.then_inc(tok_psum, 1)

            def gram(b, lhs, done, chunks):
                carry_waits()
                for c in range(chunks):
                    t0 = c * 64
                    for hp in range(CT):
                        for p in (0, 64):
                            ins = pe.matmul(banks(b + c)[p:p + 64, hp * P:(hp + 1) * P],
                                            lhs[p:p + 64, hp, t0:t0 + 64], AR[p:p + 64, hp, :, t0:t0 + 64],
                                            start=True, stop=True)
                    ins.then_inc(done, 1)

            def each(dst, lhs, rhs):
                carry_waits()
                for hp in range(CT):
                    for p in (0, 64):
                        ins = pe.matmul(dst[p:p + 64, hp * 64:hp * 64 + 64], lhs(p, hp), rhs(p, hp),
                                        start=True, stop=True)
                return ins

            def prepare(i, r, chunks):
                cumulate(i, r)
                pe.wait_ge(e_done, i + 1)
                to_tokens(0, vst, r)
                pe.wait_ge(prod_done, i + 1)
                to_tokens(1, bt, r)
                pe.wait_ge(prod2_done, i + 1)
                pe.wait_ge(rhs_done, 2 * i)
                pe.wait_ge(u_done, 2 * i)
                pe.wait_ge(y_done, 2 * i)
                pe.wait_ge(s_done, 2 * i)
                gram(2, bt, gb_psum, chunks)
                pe.wait_ge(tok_act, 3 * i + 1)
                if chunks == 2:
                    pe.wait_ge(tok_dve, 3 * i + 1)
                to_tokens(0, kt, r)
                gram(4, kt, gk_psum, chunks)

            def invert(i, chunks, levels):
                for k in range(levels):
                    for c in range(chunks):
                        if k == 0:
                            pe.wait_ge(pt_done, 2 * i + c + 1)
                            pe.wait_ge(x_done, 2 * (LV - 1) * i)
                            ins = each(banks(6 + c), lambda p, hp: PT[p:p + 64, c, hp, :],
                                       lambda p, hp: ident[p:p + 64, p:p + 64])
                        else:
                            if k == 1:
                                pe.wait_ge(m_done, 2 * LV * i + c + 1)
                                pe.wait_ge(x1t_done, 2 * i + c + 1)
                                X = MM[:, c, :, :]
                            else:
                                pe.wait_ge(x_done, 2 * (LV - 1) * i + chunks * (k - 2) + c + 1)
                                X = XX[:, c, 0, :, :]
                            ins = each(banks(6 + c), lambda p, hp: PT[p:p + 64, c, hp, :],
                                       lambda p, hp: X[p:p + 64, hp, :])
                        ins.then_inc(m_psum, 1)
                    if k == 0:
                        continue
                    for c in range(chunks):
                        pe.wait_ge(m_done, 2 * LV * i + chunks * k + c + 1)
                        if k < levels - 1:
                            each(banks(6 + c), lambda p, hp: XX[p:p + 64, c, 1, hp, :],
                                 lambda p, hp: MM[p:p + 64, c, hp, :])
                        each(banks(6 + c)[:, 256:512], lambda p, hp: MM[p:p + 64, c, hp, :],
                             lambda p, hp: XX[p:p + 64, c, 1, hp, :]).then_inc(x_psum, 1)

            def group(dst, terms, fresh=True, last=True):
                carry_waits()
                for m, (lhs, rhs) in enumerate(terms):
                    for hp in range(CT):
                        for p in (0, 64):
                            ins = pe.matmul(dst[p:p + 64, hp * 64:hp * 64 + 64], lhs(p, hp), rhs(p, hp),
                                            start=(fresh and m == 0 and hp == 0),
                                            stop=(last and m == len(terms) - 1), skip_group_check=True)
                return ins

            def chain(i, c):
                n = 2 * i + c
                t0 = c * 64
                if c == 0:
                    pe.wait_ge(x_done, 2 * (LV - 1) * (i + 1))
                    pe.wait_ge(tok_act, 3 * i + 3)
                    pe.wait_ge(gb_done, 2 * i + 2)
                    pe.wait_ge(gk_done, 2 * i + 2)
                    pe.wait_ge(s0_done, 1)
                else:
                    pe.wait_ge(tok_dve, 3 * i + 3)
                pe.wait_ge(s_done, n)
                S = ST0
                group(banks(2), [
                    (lambda p, hp: GK[p:p + 64, c, hp, 0, :], lambda p, hp: vtok[p:p + 64, c, hp, :]),
                    (lambda p, hp: AR[p:p + 64, hp, 0, t0:t0 + 64], lambda p, hp: S[p:p + 64, hp, :]),
                ]).then_inc(rhs_psum, 1)
                if c:
                    pe.wait_ge(y_done, n)
                group(banks(4), [
                    (lambda p, hp: S[p:p + 64, hp, :], lambda p, hp: AR[p:p + 64, hp, 1, t0:t0 + 64]),
                    (lambda p, hp: vtok[p:p + 64, c, hp, :], lambda p, hp: GK[p:p + 64, c, hp, 1, :]),
                ], last=False)
                pe.wait_ge(rhs_done, n + 1)
                each(banks(3), lambda p, hp: XX[p:p + 64, c, 1, hp, :], lambda p, hp: RHS[p:p + 64, hp, :])\
                    .then_inc(u_psum, 1)
                group(banks(5), [(lambda p, hp: ktok[p:p + 64, c, hp, :], lambda p, hp: vtok[p:p + 64, c, hp, :])],
                      last=False)
                pe.wait_ge(u_done, n + 1)
                group(banks(5), [(lambda p, hp: btok[p:p + 64, c, hp, :], lambda p, hp: UU[p:p + 64, hp, :])],
                      fresh=False).then_inc(s_psum, 1)
                group(banks(4), [(lambda p, hp: UU[p:p + 64, hp, :], lambda p, hp: GB[p:p + 64, c, hp, 1, :])],
                      fresh=False).then_inc(y_psum, 1)

            with pe.Fori(0, NT - 1) as i:
                prepare(i, P, 2)
                invert(i, 2, LV)
                for c in range(2):
                    chain(i, c)

            pe.wait_ge(s_done, 2 * (NT - 1))
            pe.wait_ge(tok_act, 3 * (NT - 1))
            pe.wait_ge(tok_dve, 3 * (NT - 1))
            for hp in range(CT):
                ins = pe.transpose(banks(0)[0:64, hp * P:(hp + 1) * P], ST0[:, hp, :], ident[:, :])
            ins.then_inc(fin_psum, 1)
            pe.wait_ge(fin_copied, 1)
            i8, n8 = NT - 1, 2 * (NT - 1)
            prepare(i8, NS, 1)
            invert(i8, 1, LV8)
            pe.wait_ge(x_done, 2 * (LV - 1) * i8 + LV8 - 1)
            pe.wait_ge(tok_act, 3 * i8 + 3)
            pe.wait_ge(gb_done, n8 + 1)
            pe.wait_ge(gk_done, n8 + 1)
            for hp in range(CT):
                pe.wait_ge(s_loaded, 32 * (hp + 1))
                if hp:
                    pe.wait_ge(s8_in, hp)
                for b in range(SB):
                    ins = pe.transpose(banks(7)[:, b * 64:b * 64 + 64], s_raw[:, b, :], ident[0:64, 0:64])
                ins.then_inc(s8_psum, 1)
                pe.wait_ge(s8_in, hp + 1)
                pe.wait_ge(a8_done, hp + 1)
                if hp:
                    pe.wait_ge(rhs_done, n8 + hp)
                for b in range(-1, SB):
                    for p in (0, 64):
                        lhs = GK[p:p + 64, 0, hp, 0, :] if b < 0 else A8[p:p + 64, b, :]
                        rhs = vtok[p:p + 64, 0, hp, :] if b < 0 else S8[p:p + 64, b, :]
                        ins = pe.matmul(banks(2)[p:p + 64, 0:64], lhs, rhs, start=(b < 0), stop=(b == SB - 1))
                ins.then_inc(rhs_psum, 1)
                pe.wait_ge(rhs_done, n8 + hp + 1)
                for p in (0, 64):
                    ins = pe.matmul(banks(3)[p:p + 64, 0:64], XX[p:p + 64, 0, 1, hp, :], RHS[p:p + 64, hp, :],
                                    start=True, stop=True)
                ins.then_inc(u_psum, 1)
                pe.wait_ge(u_done, n8 + hp + 1)
                for p in (0, 64):
                    pe.matmul(banks(4)[p:p + 64, 0:64], UU[p:p + 64, hp, :], GB[p:p + 64, 0, hp, 1, :],
                              start=True, stop=False, skip_group_check=True)
                    pe.matmul(banks(4)[p:p + 64, 0:64], vtok[p:p + 64, 0, hp, :], GK[p:p + 64, 0, hp, 1, :],
                              start=False, stop=False, skip_group_check=True)
                    for b in range(SB):
                        ins = pe.matmul(banks(4)[p:p + 64, b * ST:(b + 1) * ST], S8[p:p + 64, b, :],
                                        AR[p:p + 64, hp, 1, b * ST:(b + 1) * ST], start=False, stop=(b == SB - 1),
                                        skip_group_check=True)
                ins.then_inc(y_psum, 1)
                pe.wait_ge(uv8_done, hp + 1)
                for p in (0, 64):
                    pe.matmul(banks(5)[p:p + 64, :], btok[p:p + 64, 0, hp, :],
                              U8[p:p + 64, :, :].rearrange("p b n -> p (b n)"), start=True, stop=False)
                    ins = pe.matmul(banks(5)[p:p + 64, :], ktok[p:p + 64, 0, hp, :],
                                    V8[p:p + 64, :, :].rearrange("p b n -> p (b n)"), start=False, stop=True)
                ins.then_inc(s_psum, 1)
                pe.wait_ge(s8_done, hp + 1)
                pe.wait_ge(fin_copied, hp + 1)
                for b in range(SB):
                    ins = pe.transpose(banks(b // 4)[0:64, b % 4 * P:(b % 4 + 1) * P], S8[:, b, :], ident[:, :])
                ins.then_inc(fin_psum, 1)

            pe.wait_ge(fin_copied, CT + 1)
            pe.wait_ge(y_done, 2 * (NT - 1) + CT)
            pe.wait_ge(s8_done, CT)

            def over_tokens(dst, lhs, hp, src=None, **flags):
                for n0 in range(0, N, 512):
                    n1 = min(n0 + 512, N)
                    if src is not None:
                        rhs = src[:, n0:n1]
                    elif n1 < N:
                        rhs = yT[:, n0 // P:n1 // P, hp, :]
                    else:
                        rhs = yT[:, NT - 1, hp, 0:NS]
                    ins = pe.matmul(dst[:, n0:n1], lhs, rhs, **flags)
                return ins

            for hp in range(CT):
                if hp:
                    pe.wait_ge(gdev_done, hp)
                over_tokens(banks(0, 3), headmean[:, :], hp, start=True, stop=True).then_inc(gmean_psum, 1)
                pe.wait_ge(gsq_done, hp + 1)
                over_tokens(banks(3, 3)[0:8, :], head_sel[:, hp, :], hp, gn_sq, start=(hp == 0),
                            stop=(hp == CT - 1)).then_inc(gvar_part, 1)
            pe.wait_ge(grstd_done, 1)
            for hp in range(CT):
                if hp:
                    pe.wait_ge(gback_used, hp)
                over_tokens(banks(0, 3), head_back[:, hp, :], hp, gn_rstd[0:8, :], start=True, stop=True)\
                    .then_inc(gback_psum, 1)
                pe.wait_ge(rk_done, hp + 1)
                if hp:
                    pe.wait_ge(mix_done, hp)
                over_tokens(banks(3, 3), headsum[:, :], hp, gn_bonus, start=True, stop=True).then_inc(rk_psum, 1)
                pe.wait_ge(rk_used, hp + 1)
                over_tokens(banks(3, 3), w_g[:, hp * P:(hp + 1) * P], hp, zs[:, GL0, :], start=True, stop=True)\
                    .then_inc(gate_psum, 1)
            pe.wait_ge(mix_done, CT)
            pe.wait_ge(tables2_in, 16 * 6)

            def project(i):
                r = rows_of(i)
                if i >= 2:
                    pe.wait_ge(h_done, i - 1)
                for half in range(2):
                    for c in range(2 * CT):
                        lhs = co[:, c, i * P:i * P + r] if c < CT else yT[:, i, c - CT, 0:r]
                        ins = pe.matmul(banks(2 * (i % 2) + half)[0:r, :], lhs, wout[:, c, half * 512:half * 512 + 512],
                                        start=(c == 0), stop=(c == 2 * CT - 1))
                ins.then_inc(o_psum, 1)

            def route(i):
                r = rows_of(i)
                pe.wait_ge(xn2_done, i + 1)
                if i:
                    pe.wait_ge(xT_act, NT + i)
                    pe.wait_ge(xT_dve, NT + i)
                for c in range(DC):
                    ins = pe.transpose(banks(4 + c // 4)[:, (c % 4) * P:(c % 4) * P + r],
                                       xn2[i % 2][0:r, c * P:(c + 1) * P], ident[0:r, 0:r])
                ins.then_inc(xT_psum, 1)

            def logits(i):
                r = rows_of(i)
                pe.wait_ge(xT_act, NT + i + 1)
                pe.wait_ge(xT_dve, NT + i + 1)
                if i:
                    pe.wait_ge(lg_done, i)
                for c in range(DC):
                    ins = pe.matmul(banks(6)[0:r, 0:NG + NE], x2T[i % 2][:, c, 0:r], w_rt[:, c, :], start=(c == 0),
                                    stop=(c == DC - 1))
                ins.then_inc(lg_psum, 1)

            for i in range(NT):
                project(i)
                if i:
                    route(i - 1)
                if i >= 2:
                    logits(i - 2)
            route(NT - 1)
            logits(NT - 2)
            logits(NT - 1)

            pe.wait_ge(cum_done, 1)
            rk = banks(7)
            for i in range(NT):
                pe.matmul(rk[:, i * NE:(i + 1) * NE], before[:, :], r_m[:, i, :], start=True, stop=False)
                pe.matmul(rk[:, i * NE:(i + 1) * NE], ones[:, :], r_cum[:, i, :], start=False, stop=True)
            pe.matmul(rk[:, NT * NE:(NT + 1) * NE], ones[:, :], r_cum[:, NT, :], start=True, stop=True)\
                .then_inc(rank_psum, 1)
            for k in range(TOPK):
                for i in range(NT):
                    n = k * NT + i
                    r = rows_of(i)
                    pe.wait_ge(onehot_done, n + 1)
                    pe.matmul(banks(6)[:, 0:2 * NCOL], r_os[n % 2][0:r, :], r_ot[n % 2][0:r, :, :].rearrange(
                        "p a n -> p (a n)"), start=(n == 0), stop=(n == TOPK * NT - 1)).then_inc(onehot_used, 1)

            def transpose_rows(u, turn, v):
                pe.wait_ge(xg_in[v % UN], 16 * (turn + v // UN) + 16)
                for c in range(DC):
                    ins = pe.transpose(banks(2 + c // 4)[:, (c % 4) * P:(c % 4 + 1) * P],
                                       xg[v % UN][:, c * P:(c + 1) * P], ident[:, :])
                ins.then_inc(xT_psum, 1)

            def gate_up(u, turn, v):
                pe.wait_ge(xT_act, 2 * NT + u + 1)
                pe.wait_ge(xT_dve, 2 * NT + u + 1)
                pe.wait_ge(wx_in[v % UN], 48 * (turn + v // UN) + 48 + wx_0[v % UN])
                wgu = wx[v % UN][:, 0:2 * DC * F].rearrange("p (w c f) -> p w c f", w=2, c=DC)
                for c in range(DC):
                    ins = pe.matmul(banks(v % 2), xgT[v % 2][:, c, :], wgu[:, :, c, :], start=(c == 0),
                                    stop=(c == DC - 1))
                ins.then_inc(gu_psum, 1)

            def pe_step(turn, s, ahead):
                u = UN * turn + s
                if ahead >= 1:
                    gate_up(u + 1, turn, s + 1)
                pe.wait_ge(hx_done, u + 1)
                for c in range(2):
                    ins = pe.transpose(banks(4)[:, c * P:(c + 1) * P], gu[:, c * P:(c + 1) * P], ident[:, :])
                ins.then_inc(ht_psum, 1)
                if ahead >= 2:
                    transpose_rows(u + 2, turn, s + 2)
                pe.wait_ge(ht_done, u + 1)
                pe.wait_ge(ye_act, u)
                pe.wait_ge(ye_dve, u)
                wd = wx[s][:, 2 * DC * F:].rearrange("p (c n) -> p c n", c=2)
                for half in range(2):
                    for c in range(2):
                        ins = pe.matmul(banks(5 + half), hT[:, c, :], wd[:, c, half * 512:half * 512 + 512],
                                        start=(c == 0), stop=(c == 1))
                ins.then_inc(yd_psum, 1)

            transpose_rows(0, 0, 0)
            gate_up(0, 0, 0)
            transpose_rows(1, 0, 1)
            expert_turns(pe, pe_step)

        @block.vector
        def _(dve):
            step = [0]

            def link(ins):
                step[0] += 1
                ins.then_inc(dve_chain, 1)
                dve.wait_ge(dve_chain, step[0])

            dve.memset(stat[:, 7, :], 0.0)
            dve.memset(hx[:, :, 0:HB], 0.0)
            dve.wait_ge(const_ready, 1)
            for m in (mask_ar, mask_ar8, mask_lv, mask_lv0t, rowmask):
                flat = m[:, :] if len(m.shape) == 2 else m[:, :, :].rearrange("p a b -> p (a b)")
                dve.tensor_copy(flat[64:128, :], flat[0:64, :])

            def mean_square(i):
                r = rows_of(i)
                dve.wait_ge(sq_done, i + 1)
                dve.tensor_scalar(stat[0:r, 1, i:i + 1], stat[0:r, 0, i:i + 1], 1.0 / D, RMS_EPS, ALU.mult, ALU.add)\
                    .then_inc(ms_done, 1)

            def scale(i):
                r = rows_of(i)
                dve.wait_ge(std_done, i + 1)
                link(dve.reciprocal(stat[0:r, 3, i:i + 1], stat[0:r, 2, i:i + 1]))
                if i == 0:
                    dve.wait_ge(gain1_in, 16)
                if i >= 2:
                    dve.wait_ge(xT_psum, i - 1)
                dve.scalar_tensor_tensor(out=xn[i % 2][0:r, :], in0=x_in[i % 3][0:r, :],
                                         scalar=stat[0:r, 3, i:i + 1], in1=gain[0:r, :], op0=ALU.mult,
                                         op1=ALU.mult).then_inc(xn_done, 1)

            def copy_T(i):
                dve.wait_ge(xT_psum, i + 1)
                r = rows_of(i)
                dve.tensor_copy(xnT[:, 4:8, i * P:i * P + r],
                                banks(2 * (i % 2) + 1).rearrange("p (c n) -> p c n", c=4)[:, :, 0:r])\
                    .then_inc(xT_dve, 1)

            mean_square(0)
            for i in range(NT):
                if i + 1 < NT:
                    mean_square(i + 1)
                scale(i)
                if i >= 1:
                    copy_T(i - 1)
                if i == 1:
                    dve.wait_ge(tables_psum, 1)
                    tb = banks(6)
                    dve.tensor_copy(prm[:, :], tb[:, 0:NPR])
                    dve.tensor_copy(cw[:, :, :].rearrange("p k c -> p (k c)"), tb[:, 64:64 + W * CT])
                    dve.tensor_copy(shift0[:, :, :].rearrange("p t b -> p (t b)"), tb[:, 192:192 + ZT * SB])
                    for h in range(2):
                        for c in range(CT):
                            ins = dve.tensor_copy(
                                hx[:, c, HB + SEQ:].rearrange("p (b k) -> p b k", b=SB)[:, 4 * h:4 * h + 4, 0:HB],
                                banks(4 + h)[:, c * 4 * HB:(c + 1) * 4 * HB].rearrange("p (b k) -> p b k", b=4))
                    link(ins)
                    dve.tensor_scalar(om_ka[:, :], prm[:, PR["k_a"][0]:PR["k_a"][0] + CT], -1.0, 1.0,
                                      ALU.mult, ALU.add).then_inc(tables_done, 1)
            copy_T(NT - 1)

            taps = [(c, k) for c in range(CT) for k in range(W)]
            done = [0]

            def conv(n):
                for _ in range(n):
                    if done[0] == len(taps):
                        return
                    j = done[0]
                    c, k = taps[j]
                    w = cw[:, k, c:c + 1]
                    src_p = hx[:, c, k:k + SEQ]
                    src_s = hx[:, c, HB + SEQ:].rearrange("p (b k) -> p b k", b=SB)[:, :, k:k + ST]
                    dst_p, dst_s = co[:, c, 0:SEQ], co[:, c, SEQ:N].rearrange("p (b t) -> p b t", b=SB)
                    for m, (dst, src) in enumerate(((dst_p, src_p), (dst_s, src_s))):
                        if k == 0:
                            bias = prm[:, PR["conv_b"][0] + c:PR["conv_b"][0] + c + 1]
                            dve.tensor_scalar(dst, src, w, bias, ALU.mult, ALU.add).then_inc(conv_tap, 1)
                        else:
                            dve.wait_ge(conv_tap, 2 * j + m - 1)
                            dve.scalar_tensor_tensor(out=dst, in0=src, scalar=w, in1=dst, op0=ALU.mult,
                                                     op1=ALU.add).then_inc(conv_tap, 1)
                    done[0] += 1

            for q, t in enumerate(ORDER):
                pr = banks(3 * (q % 2), 3)
                if q < NCONV:
                    if q % 2 == 1:
                        c = q // 2
                        dve.wait_ge(proj_done, q + 1)
                        dve.wait_ge(sig_done, c + 1)
                        dve.tensor_tensor(hx[:, c, HB:HB + SEQ], pr[:, 0:SEQ], sig[:, 0:SEQ], ALU.mult)
                        dve.tensor_tensor(hx[:, c, HB + SEQ:].rearrange("p (b k) -> p b k", b=SB)[:, :, HB:],
                                          pr[:, SEQ:N].rearrange("p (b t) -> p b t", b=SB),
                                          sig[:, SEQ:N].rearrange("p (b t) -> p b t", b=SB), ALU.mult)\
                            .then_inc(hx_ready, 1)
                        dve.wait_ge(hx_ready, c + 1)
                        conv(6)
                    continue
                j = q - NCONV
                zb = zbuf[j % 2]
                dve.wait_ge(z_ready, j + 1)
                if j >= 1:
                    dve.wait_ge(zs_done, j)
                dve.tensor_tensor(zd[:, 0:SEQ], zb[:, 0:SEQ], zb[:, 1:1 + SEQ], ALU.subtract)
                zsm = zb[:, 1 + SEQ:].rearrange("p (b t) -> p b t", b=SB)
                link(dve.tensor_tensor(zd[:, SEQ:N].rearrange("p (b t) -> p b t", b=SB), zsm[:, :, 0:ST],
                                       zsm[:, :, 1:], ALU.subtract))
                mu = prm[:, PR["mu"][0] + t - 8:PR["mu"][0] + t - 7]
                dve.scalar_tensor_tensor(out=zs[:, t - 8, 0:SEQ], in0=zd[:, 0:SEQ], scalar=mu, in1=zb[:, 1:1 + SEQ],
                                         op0=ALU.mult, op1=ALU.add)
                dve.scalar_tensor_tensor(out=zs[:, t - 8, SEQ:N].rearrange("p (b t) -> p b t", b=SB),
                                         in0=zd[:, SEQ:N].rearrange("p (b t) -> p b t", b=SB), scalar=mu,
                                         in1=zsm[:, :, 1:], op0=ALU.mult, op1=ALU.add).then_inc(zs_done, 1)
                dve.wait_ge(zs_done, j + 1)
                conv(8)
            conv(len(taps))
            for i in range(NT):
                r = rows_of(i)
                dve.wait_ge(decay_psum, i + 1)
                dve.tensor_tensor(sgw[0:r, i, :], banks(6 + i % 2)[0:r, :], w0_all[0:r, :], ALU.add)\
                    .then_inc(decay_sum, 1)
            dve.wait_ge(tails_out, 16 * (3 + SB))
            for hp in range(CT):
                def col(name):
                    c0 = PR[name][0] + hp
                    return prm[:, c0:c0 + 1]

                dve.tensor_scalar(nkk[:, hp, :], zs[:, K0 + hp, :], col("k_k"), None, ALU.mult).then_inc(kkr_done, 1)
                dve.wait_ge(iclr_done, hp + 1)
                dve.tensor_scalar(kmul, iclr[hp % 2], col("k_a"), om_ka[:, hp:hp + 1], ALU.mult, ALU.add)\
                    .then_inc(dve_chain, 1)
                step[0] += 1
                dve.wait_ge(kkr_done, hp + 1)
                dve.tensor_tensor(kka[:, hp, :], nkk[:, hp, :], iclr[hp % 2], ALU.mult)
                dve.wait_ge(dve_chain, step[0])
                dve.tensor_tensor(zs[:, K0 + hp, :], zs[:, K0 + hp, :], kmul, ALU.mult).then_inc(kprep_done, 1)
                dve.wait_ge(kprep_done, hp + 1)
            dve.wait_ge(knorm_root, 1)
            link(dve.tensor_scalar(knorm[0:8, :], knorm[0:8, :], 1e-12, None, ALU.max))
            dve.reciprocal(knorm[0:8, :], knorm[0:8, :]).then_inc(knorm_done, 1)
            for hp in range(CT):
                dve.wait_ge(kback_psum, hp + 1)
                kb = banks(3 * (hp % 2), 3)[:, 0:N]
                dve.tensor_tensor(kka[:, hp, :], kka[:, hp, :], kb, ALU.mult)
                dve.scalar_tensor_tensor(out=nkk[:, hp, :], in0=nkk[:, hp, :], scalar=-1.0, in1=kb, op0=ALU.mult,
                                         op1=ALU.mult).then_inc(kk_done, 1)
            dve.wait_ge(cmean_psum, 1)
            dve.wait_ge(kprep_done, CT)
            for c in range(CT):
                dve.tensor_tensor(co[:, c, :], co[:, c, :], banks(0, 3)[:, 0:N], ALU.subtract).then_inc(cdev_done, 1)
            dve.wait_ge(cvar_part, CT)
            dve.tensor_scalar(conv_rstd, banks(3, 3)[:, 0:N], LN_EPS, None, ALU.add).then_inc(cvar_done, 1)
            dve.wait_ge(cstd_done, 1)
            link(dve.reciprocal(conv_rstd, conv_rstd))
            for c in range(CT):
                dve.tensor_tensor(co[:, c, :], co[:, c, :], conv_rstd, ALU.mult).then_inc(cnorm_done, 1)
            for c in range(CT):
                g0, b0 = PR["ln_g"][0] + c, PR["ln_b"][0] + c
                dve.wait_ge(csig_done, c + 1)
                link(dve.tensor_scalar(co[:, c, :], co[:, c, :], prm[:, g0:g0 + 1], prm[:, b0:b0 + 1], ALU.mult,
                                       ALU.add))
                dve.tensor_tensor(co[:, c, :], co[:, c, :], conv_sig, ALU.mult).then_inc(co_done, 1)

            def scaled_a_b(i, r):
                dve.wait_ge(e_done, i + 1)
                dve.wait_ge(y_psum, 2 * i)
                dve.tensor_tensor(AR[:, :, 0, 0:r], nkk[:, :, bass.ds(i * P, r)], e_ex[:, :, 0:r], ALU.mult)
                dve.tensor_tensor(bt[:, :, 0:r], kka[:, :, bass.ds(i * P, r)], e_neg[:, :, 0:r], ALU.mult)\
                    .then_inc(prod_done, 1)

            def tok_copy(i, j, dst, b):
                dve.wait_ge(tok_psum, 3 * i + j + 1)
                src = banks(b).rearrange("p (h n) -> p h n", h=CT)
                dve.tensor_copy(dst[0:64, 1, :, :], src[64:128, :, 0:64])
                dve.tensor_copy(dst[64:128, 1, :, :], src[64:128, :, 64:128]).then_inc(tok_dve, 1)

            def masked(n, c, b, dst, psum_sem, done, mask):
                dve.wait_ge(psum_sem, n + 1)
                dve.tensor_tensor(dst[:, c, :, :, :].rearrange("p h e n -> p h (e n)"),
                                  banks(b + c).rearrange("p (h n) -> p h n", h=CT),
                                  mask[:, :, :].rearrange("p e n -> p (e n)").unsqueeze(1).broadcast_to([P, CT, P]),
                                  ALU.mult).then_inc(done, 1)

            def plus_identity(n, c):
                dve.wait_ge(gb_done, n + 1)
                for p in (0, 64):
                    ins = dve.tensor_tensor(PT[p:p + 64, c, :, :], GB[p:p + 64, c, :, 0, :],
                                            ident[p:p + 64, p:p + 64].unsqueeze(1).broadcast_to([64, CT, 64]),
                                            ALU.add)
                ins.then_inc(pt_done, 1)

            def level_mask(n, k, c):
                dve.wait_ge(m_psum, n + 1)
                dve.tensor_tensor(MM[:, c, :, :], banks(6 + c)[:, 0:CT * 64].rearrange("p (h n) -> p h n", h=CT),
                                  mask_lv[:, k, :].unsqueeze(1).broadcast_to([P, CT, 64]), ALU.mult)\
                    .then_inc(m_done, 1)

            def u_copy(n):
                dve.wait_ge(u_psum, n + 1)
                dve.tensor_copy(UU, banks(3)[:, 0:CT * 64].rearrange("p (h n) -> p h n", h=CT)).then_inc(u_done, 1)

            def new_state(n, c):
                dve.wait_ge(s_psum, n + 1)
                dve.tensor_tensor(ST0, banks(5)[:, 0:CT * 64].rearrange("p (h n) -> p h n", h=CT), ST0, ALU.add)\
                    .then_inc(s_sum, 1)
                dve.wait_ge(s_sum, n + 1)
                dve.tensor_tensor(ST0, ST0, e_in[:, :, c * 64 + 63:c * 64 + 64].broadcast_to([P, CT, 64]), ALU.mult)\
                    .then_inc(s_done, 1)

            dve.wait_ge(co_done, CT)
            with dve.Fori(0, NT - 1) as i:
                scaled_a_b(i, P)
                tok_copy(i, 0, vtok, 0)
                tok_copy(i, 1, btok, 1)
                for c in range(2):
                    masked(2 * i + c, c, 2, GB, gb_psum, gb_done, mask_ar)
                    plus_identity(2 * i + c, c)
                tok_copy(i, 2, ktok, 0)
                for c in range(2):
                    masked(2 * i + c, c, 4, GK, gk_psum, gk_done, mask_ar)
                for k in range(LV):
                    for c in range(2):
                        level_mask(2 * LV * i + 2 * k + c, k, c)
                for c in range(2):
                    u_copy(2 * i + c)
                    new_state(2 * i + c, c)

            i8, n8 = NT - 1, 2 * (NT - 1)
            scaled_a_b(i8, NS)
            masked(n8, 0, 2, GB, gb_psum, gb_done, mask_ar8)
            plus_identity(n8, 0)
            masked(n8, 0, 4, GK, gk_psum, gk_done, mask_ar8)
            for k in range(LV8):
                level_mask(2 * LV * i8 + k, k, 0)
            for hp in range(CT):
                if hp:
                    dve.wait_ge(y_psum, n8 + hp)
                dve.tensor_tensor(A8, AR[:, hp, 0, 0:64].unsqueeze(1).broadcast_to([P, SB, 64]), seqmask[:, :, :],
                                  ALU.mult).then_inc(a8_done, 1)
                dve.wait_ge(u_psum, n8 + hp + 1)
                dve.tensor_copy(UU[:, hp, :], banks(3)[:, 0:64]).then_inc(u_done, 1)
                dve.wait_ge(u_done, n8 + hp + 1)
                if hp:
                    dve.wait_ge(s_psum, n8 + hp)
                else:
                    dve.wait_ge(tok_act, 3 * NT)
                rows = rowmask[:, :].unsqueeze(2).broadcast_to([P, SB, 64])
                dve.tensor_tensor(U8, UU[:, hp, :].unsqueeze(1).broadcast_to([P, SB, 64]), rows, ALU.mult)
                dve.tensor_tensor(V8, vtok[:, 0, hp, :].unsqueeze(1).broadcast_to([P, SB, 64]), rows, ALU.mult)\
                    .then_inc(uv8_done, 1)
                dve.wait_ge(s_psum, n8 + hp + 1)
                link(dve.tensor_tensor(S8, banks(5).rearrange("p (b n) -> p b n", b=SB), S8, ALU.add))
                dve.tensor_tensor(S8, S8, e_in[:, hp, 0:64].rearrange("p (b t) -> p b t", b=SB)[:, :, ST - 1]
                                  .unsqueeze(2).broadcast_to([P, SB, 64]), ALU.mult).then_inc(s8_done, 1)

            for hp in range(CT):
                dve.wait_ge(gmean_psum, hp + 1)
                for y3, mean in pieces(yT, banks(0, 3)[:, 0:N], hp):
                    ins = dve.tensor_tensor(y3, y3, mean, ALU.subtract)
                ins.then_inc(gdev_done, 1)
            dve.wait_ge(gvar_part, CT)
            dve.tensor_scalar(gn_rstd[0:8, :], banks(3, 3)[0:8, 0:N], 1.0 / HD, GN_EPS, ALU.mult, ALU.add)\
                .then_inc(gvar_done, 1)
            dve.wait_ge(gstd_done, 1)
            dve.reciprocal(gn_rstd[0:8, :], gn_rstd[0:8, :]).then_inc(grstd_done, 1)
            for hp in range(CT):
                def col(name):
                    c0 = PR[name][0] + hp
                    return prm[:, c0:c0 + 1]

                if hp:
                    dve.wait_ge(mix_done, hp)
                dve.scalar_tensor_tensor(out=gn_bonus, in0=zs[:, R0 + hp, :], scalar=col("r_k"),
                                         in1=zs[:, K0 + hp, :], op0=ALU.mult, op1=ALU.mult).then_inc(rk_done, 1)
                dve.wait_ge(gback_psum, hp + 1)
                for y3, rstd in pieces(yT, banks(0, 3)[:, 0:N], hp):
                    ins = dve.tensor_tensor(y3, y3, rstd, ALU.mult)
                ins.then_inc(gback_used, 1)
                dve.wait_ge(gback_used, hp + 1)
                for y3, _ in pieces(yT, gn_bonus, hp):
                    ins = dve.tensor_scalar(y3, y3, col("gn_g"), col("gn_b"), ALU.mult, ALU.add)
                dve.wait_ge(rk_psum, hp + 1)
                link(ins)
                dve.tensor_tensor(gn_bonus, banks(3, 3)[:, 0:N], zs[:, V0 + hp, :], ALU.mult).then_inc(rk_used, 1)
                dve.wait_ge(rk_used, hp + 1)
                for y3, bonus in pieces(yT, gn_bonus, hp):
                    ins = dve.tensor_tensor(y3, y3, bonus, ALU.add)
                link(ins)
                dve.wait_ge(gate_psum, hp + 1)
                for y3, gate in pieces(yT, banks(3, 3)[:, 0:N], hp):
                    ins = dve.tensor_tensor(y3, y3, gate, ALU.mult)
                ins.then_inc(mix_done, 1)
            link(dve.memset(lg, 0.0))

            def residual(i):
                r = rows_of(i)
                dve.wait_ge(o_psum, i + 1)
                dve.wait_ge(x_loaded[i % 3], 16 * (NT // 3 + i // 3 + 1))
                dve.tensor_tensor(hres[0:r, i, :], banks(2 * (i % 2), 2)[0:r, :], xres[i % 3][0:r, :], ALU.add)\
                    .then_inc(h_done, 1)

            def norm2(i):
                r = rows_of(i)
                dve.wait_ge(sq_done, NT + i + 1)
                dve.tensor_scalar(stat[0:r, 5, i:i + 1], stat[0:r, 4, i:i + 1], 1.0 / D, RMS_EPS, ALU.mult, ALU.add)\
                    .then_inc(ms_done, 1)
                dve.wait_ge(std_done, NT + i + 1)
                link(dve.reciprocal(stat[0:r, 6, i:i + 1], stat[0:r, 6, i:i + 1]))
                if i == 0:
                    dve.wait_ge(tables2_in, 16 * 6)
                if i >= 2:
                    dve.wait_ge(xT_psum, NT + i - 1)
                    dve.wait_ge(xn2_stored[i % 2], 16 * (i // 2))
                dve.scalar_tensor_tensor(out=xn2[i % 2][0:r, :].rearrange("q (c p) -> q p c", c=DC),
                                         in0=hres[0:r, i, :].rearrange("q (p c) -> q p c", c=DC),
                                         scalar=stat[0:r, 6, i:i + 1],
                                         in1=gain[0:r, :].rearrange("q (p c) -> q p c", c=DC), op0=ALU.mult,
                                         op1=ALU.mult).then_inc(xn2_done, 1)

            def copy_T2(i):
                r = rows_of(i)
                dve.wait_ge(xT_psum, NT + i + 1)
                if i >= 2:
                    dve.wait_ge(lg_psum, i - 1)
                dve.tensor_copy(x2T[i % 2][:, 4:8, 0:r], banks(5).rearrange("p (c n) -> p c n", c=4)[:, :, 0:r])\
                    .then_inc(xT_dve, 1)

            def add_bias(i):
                r = rows_of(i)
                dve.wait_ge(lg_psum, i + 1)
                dve.tensor_tensor(lg[0:r, i, :], banks(6)[0:r, 0:NG + NE], b_rt[0:r, :], ALU.add).then_inc(lg_done, 1)

            for i in range(NT):
                residual(i)
                norm2(i)
                if i:
                    copy_T2(i - 1)
                if i >= 2:
                    add_bias(i - 2)
            copy_T2(NT - 1)
            add_bias(NT - 2)
            add_bias(NT - 1)

            def TT(out, a, b, op):
                link(dve.tensor_tensor(out, a, b, op))

            def TS(out, a, s1, s2, op0, op1=ALU.bypass):
                link(dve.tensor_scalar(out, a, s1, s2, op0, op1))

            def RED(out, a, op):
                link(dve.tensor_reduce(out, a, AX.X, op))

            def last_dim(v, n):
                return v.unsqueeze(len(v.shape)).broadcast_to([*v.shape, n])

            def first(out, values, top, n, key):
                TT(key, values, last_dim(top, n), ALU.is_equal)
                TT(key, key, r_desc[:, EG - n:].unsqueeze(1).broadcast_to([P, NT, n]), ALU.mult)
                RED(r_km, key, ALU.max)
                TT(out, key, last_dim(r_km, n), ALU.is_equal)

            dve.wait_ge(lg_done, NT)
            dve.wait_ge(iota_done, 1)
            gl, el = lg[:, :, 0:NG], lg[:, :, NG:]
            RED(r_gmax, gl, ALU.max)
            first(r_g1, gl, r_gmax, NG, r_key4)
            dve.tensor_tensor(r_gd, gl, last_dim(r_gmax, NG), ALU.subtract).then_inc(softmax_in, 1)
            TT(r_e4, el.rearrange("p i (g e) -> p i g e", g=NG), last_dim(r_g1, EG), ALU.mult)
            RED(r_es, r_e4.rearrange("p i g e -> p i e g"), ALU.add)
            RED(r_m1, r_es, ALU.max)
            first(r_o[:, 0], r_es, r_m1, EG, r_key8)
            link(dve.scalar_tensor_tensor(out=r_es, in0=r_o[:, 0], scalar=-BIG, in1=r_es, op0=ALU.mult, op1=ALU.add))
            RED(r_m2, r_es, ALU.max)
            first(r_o[:, 1], r_es, r_m2, EG, r_key8)
            dve.tensor_tensor(r_ex, r_m2, r_m1, ALU.subtract).then_inc(softmax_in, 1)
            dve.wait_ge(softmax_done, 1)
            RED(r_pg, r_gd, ALU.add)
            dve.wait_ge(softmax_done, 2)
            TS(r_den, r_ex, 1.0, None, ALU.add)
            TT(r_den, r_den, r_pg, ALU.mult)
            link(dve.reciprocal(w_k[:, 0, :], r_den))
            TT(w_k[:, 1, :], w_k[:, 0, :], r_ex, ALU.mult)
            for k in range(TOPK):
                TT(r_oh[:, k].rearrange("p i (g e) -> p i g e", g=NG), r_o[:, k].unsqueeze(2).broadcast_to([P, NT, NG, EG]),
                   last_dim(r_g1, EG), ALU.mult)
            link(dve.memset(r_oh[NS:P, :, NT - 1, :], 0.0))
            TT(r_m, r_oh[:, 0], r_oh[:, 1], ALU.add)
            link(dve.memset(r_cum[:, 0, :], 0.0))
            for i in range(NT - 1):
                TT(r_cum[:, i + 1, :], r_cum[:, i, :], r_m[:, i, :], ALU.add)
            dve.tensor_tensor(r_cum[:, NT, :], r_cum[:, NT - 1, :], r_m[:, NT - 1, :], ALU.add).then_inc(cum_done, 1)
            dve.wait_ge(rank_psum, 1)
            link(dve.tensor_copy(r_c, banks(7)[:, 0:(NT + 1) * NE].rearrange("p (i e) -> p i e", e=NE)))
            flat = "p k i e -> p (k i) e"

            def pick(out, table):
                TT(r_tmp, r_oh, table, ALU.mult)
                RED(out, r_tmp.rearrange(flat), ALU.add)

            def per_expert(v):
                return v.unsqueeze(1).unsqueeze(1).broadcast_to([P, TOPK, NT, NE])

            pick(r_rank, r_c[:, 0:NT, :].unsqueeze(1).broadcast_to([P, TOPK, NT, NE]))
            pick(r_exp, per_expert(r_iote))
            TT(r_xc, last_dim(r_c[:, NT, :], EG), r_thr.unsqueeze(1).broadcast_to([P, NE, EG]), ALU.is_gt)
            for s in r_s:
                link(dve.memset(s, 0.0))
            RED(r_x, r_xc, ALU.add)
            TS(r_s[0][:, 1, :], r_x, 0.0, None, ALU.add)
            a, b = r_s
            for d in (1, 2, 4, 8, 16):
                fa = a.rearrange("p a n -> p (a n)")
                TT(b[:, 1, :], fa[:, NE:], fa[:, NE - d:2 * NE - d], ALU.add)
                a, b = b, a
            upto = a[:, 1, :]
            TT(r_x, upto, r_x, ALU.subtract)
            pick(r_base, per_expert(r_x))
            TT(r_qc, last_dim(r_rank, EG), r_thr.unsqueeze(1).broadcast_to([P, TOPK * NT, EG]), ALU.is_ge)
            RED(r_q, r_qc, ALU.add)
            link(dve.scalar_tensor_tensor(out=r_slot, in0=r_q, scalar=-float(P), in1=r_rank, op0=ALU.mult, op1=ALU.add))
            TS(r_q1, r_q, 1.0, None, ALU.min)
            TT(r_tile, r_base, r_q, ALU.add)
            TT(r_tile, r_tile, r_exp, ALU.subtract)
            TS(r_tile, r_tile, float(NE - 1), None, ALU.add)
            TT(r_tile, r_tile, r_q1, ALU.mult)
            TT(r_tile, r_tile, r_exp, ALU.add)
            for k in range(TOPK):
                for i in range(NT):
                    n = k * NT + i
                    if n >= 2:
                        dve.wait_ge(onehot_used, n - 1)
                    dve.tensor_scalar(r_os[n % 2], r_iots, r_slot[:, n:n + 1], None, ALU.is_equal)
                    for a in range(2):
                        ins = dve.tensor_scalar(r_ot[n % 2][:, a, :], r_iotc, r_tile[:, n:n + 1],
                                                r_val[:, a, i, k:k + 1], ALU.is_equal, ALU.mult)
                    ins.then_inc(onehot_done, 1)
            TT(r_tc, upto.unsqueeze(1).broadcast_to([P, EXTRA, NE]), last_dim(r_iotc[:, 0:EXTRA], NE), ALU.is_le)
            RED(r_te, r_tc, ALU.add)
            TS(r_te, r_te, float(NE - 1), None, ALU.min)
            link(dve.tensor_copy(te_u[:, 0:NE], r_iotc[0:1, 0:NE]))
            link(dve.tensor_copy(te_u[:, NE:], r_te[0:1, :]))
            TS(r_tc[:, 0, 0:EXTRA // UN], r_iotc[:, 0:EXTRA // UN], float(UN), None, ALU.mult)
            TS(r_tc[:, 0, 0:EXTRA // UN], r_tc[:, 0, 0:EXTRA // UN], upto[:, NE - 1:NE], None, ALU.is_lt)
            RED(r_n[:, 0:1], r_tc[:, 0, 0:EXTRA // UN], ALU.add)
            TS(r_n[:, 0:1], r_n[:, 0:1], float(NE // UN - 1), None, ALU.add)
            link(dve.tensor_copy(last_turn[:, :], r_n[0:1, 0:1]))
            dve.wait_ge(onehot_used, TOPK * NT)
            link(dve.tensor_copy(r_f, banks(6)[:, 0:2 * NCOL].rearrange("p (a n) -> p a n", a=2)))
            TS(r_z, r_f, 0.0, 65536.0, ALU.is_equal, ALU.mult)
            TS(r_f, r_f, -1.0, None, ALU.add)
            TT(r_f, r_f, r_z, ALU.add)
            dve.tensor_copy(idx[:, :, :], r_f).then_inc(idx_done, 1)

            def copy_xg(u, s):
                dve.wait_ge(xT_psum, 2 * NT + u + 1)
                dve.tensor_copy(xgT[s % 2][:, 4:8, :], banks(3).rearrange("p (c n) -> p c n", c=4)).then_inc(xT_dve, 1)

            def hidden(u, s):
                bank = banks(s % 2)
                dve.wait_ge(gs_done, u + 1)
                dve.tensor_tensor(gs, bank[:, 0:F], gs, ALU.mult).then_inc(gmul_done, 1)
                dve.wait_ge(gmul_done, u + 1)
                dve.tensor_tensor(gu.rearrange("q (c p) -> q p c", c=2), bank[:, F:2 * F].rearrange(
                    "q (p c) -> q p c", c=2), gs.rearrange("q (p c) -> q p c", c=2), ALU.mult).then_inc(hx_done, 1)

            def dve_step(turn, s, ahead):
                u = UN * turn + s
                dve.wait_ge(ht_psum, u + 1)
                dve.tensor_copy(hT, banks(4)[:, 0:F].rearrange("p (c n) -> p c n", c=2)).then_inc(ht_done, 1)
                if ahead >= 2:
                    copy_xg(u + 2, s)
                if ahead >= 1:
                    hidden(u + 1, s + 1)
                dve.wait_ge(yd_psum, u + 1)
                dve.wait_ge(ye_out[s % 2], 16 * ((UN // 2) * turn + s // 2))
                dve.tensor_copy(ye[s % 2][:, 512:], banks(6)).then_inc(ye_dve, 1)

            copy_xg(0, 0)
            hidden(0, 0)
            copy_xg(1, 1)
            expert_turns(dve, dve_step)
            for i in range(NT):
                r = rows_of(i)
                dve.wait_ge(yk_in[i % 2], 16 * (i // 2 + 1))
                for k in range(TOPK):
                    ins = dve.scalar_tensor_tensor(out=hres[0:r, i, :], in0=yk[i % 2][0:r, k, :],
                                                   scalar=w_k[0:r, k, i:i + 1], in1=hres[0:r, i, :], op0=ALU.mult,
                                                   op1=ALU.add)
                    if k == 0:
                        link(ins)
                ins.then_inc(ff_done, 1)
                dve.wait_ge(ff_done, i + 1)
                dve.wait_ge(sq_done, 2 * NT + i + 1)
                dve.tensor_scalar(stat[0:r, 1, i:i + 1], stat[0:r, 0, i:i + 1], 1.0 / D, RMS_EPS, ALU.mult, ALU.add)\
                    .then_inc(ms_done, 1)
                dve.wait_ge(std_done, 2 * NT + i + 1)
                link(dve.reciprocal(stat[0:r, 3, i:i + 1], stat[0:r, 2, i:i + 1]))
                if i == 0:
                    dve.wait_ge(tables2_in, 16 * 7)
                if i >= 2:
                    dve.wait_ge(fin_out[i % 2], 16 * (i // 2))
                dve.scalar_tensor_tensor(out=fin[i % 2][0:r, :], in0=hres[0:r, i, :], scalar=stat[0:r, 3, i:i + 1],
                                         in1=gain[0:r, :], op0=ALU.mult, op1=ALU.mult).then_inc(fin_done, 1)



_INS = ['x_prompt', 'x_sample', 'state_conv', 'state_shift', 'state_wkv', 'norm1_g', 'w_in', 'conv_w', 'conv_b',
        'conv_ln_g', 'conv_ln_b', 'mu_shift', 'w0', 'w_decay_up', 'a0', 'w_aaa_up', 'w_gate_up', 'k_k', 'k_a', 'r_k',
        'gn_g', 'gn_b', 'w_out', 'norm2_g', 'w_router_group', 'b_router_group', 'w_router_expert',
        'b_router_expert', 'w_exp_gate', 'w_exp_up', 'w_exp_down', 'norm_f_g']
_OUTS = [((1, SEQ, D), 'float32'), ((SB, ST, D), 'float32'), ((1, 1, HB, C), 'float32'), ((1, 1, DS), 'float32'),
         ((1, 1, 2 * CT, HD, HD), 'float32'), ((1, SB, HB, C), 'float32'), ((1, SB, DS), 'float32'),
         ((1, SB, 2 * CT, HD, HD), 'float32')]


def kernel(**inputs):
    import numpy as _np
    import concourse.bacc as _bacc
    from concourse import mybir as _mybir
    from concourse.bass_utils import run_bass_kernel_spmd as _run

    nc = _bacc.Bacc("TRN2", target_bir_lowering=False, num_devices=1)
    arrays, args = {}, []
    for name in _INS:
        a = _np.ascontiguousarray(inputs[name])
        arrays[f"in_{name}_dram"] = a
        args.append(nc.dram_tensor(f"in_{name}_dram", a.shape, _mybir.dt.from_np(a.dtype), kind="ExternalInput").ap())
    for i, (shape, dtype) in enumerate(_OUTS):
        dt = _mybir.dt.from_np(_np.dtype(dtype))
        args.append(nc.dram_tensor(f"out_{i}_dram", shape, dt, kind="ExternalOutput").ap())
    hybrid_decoder_step(nc, *args)
    r = _run(nc, [arrays], core_ids=[0])
    return tuple(r.results[0][f"out_{i}_dram"] for i in range(len(_OUTS)))
```

```python
from contextlib import ExitStack

import numpy as np

import concourse.bass as bass
from concourse import mybir

F32 = mybir.dt.float32
U32 = mybir.dt.uint32
ALU = mybir.AluOpType
ACT = mybir.ActivationFunctionType
AX = mybir.AxisListType

P = 128
D = 1024
DC = D // P
SEQ = 1024
SB, ST = 8, 8
NS = SB * ST
N = SEQ + NS
NT = SEQ // P + 1
C = 512
CT = C // P
HD = 64
W = 31
HB = W - 1
DS = 1792
ZT = DS // P
MT = (2 * C + DS) // P
NG, EG = 4, 8
NE = NG * EG
F = 256
TOPK = 2
NX = (N * TOPK) // P
UN = 4
EXTRA = -(-NX // UN) * UN
NTILE_X = NE + EXTRA
RMS_EPS, LN_EPS, GN_EPS = 1e-6, 1e-5, 64e-5
LOGW = -float(np.exp(-0.5))
BIG = 1.0e30

HXW = HB + SEQ + SB * (HB + ST)
ZW = 1 + SEQ + SB * (1 + ST)
LV = 6
LV8 = 3

PR = {}
for _n, _c in (("mu", ZT), ("k_k", CT), ("k_a", CT), ("r_k", CT), ("a0", CT), ("gn_g", CT), ("gn_b", CT),
               ("conv_b", CT), ("ln_g", CT), ("ln_b", CT)):
    PR[_n] = (sum(c for _, c in PR.values()), _c)
NPR = sum(c for _, c in PR.values())

VAL, GATE, RR, KK, VV, WA, GL = 0, 4, 8, 12, 16, 20, 21
ORDER = [t for c in range(CT) for t in (GATE + c, VAL + c)] + [WA, GL] + [KK + c for c in range(CT)] \
    + [RR + c for c in range(CT)] + [VV + c for c in range(CT)]
NCONV = 2 * CT


def rows_of(i):
    return P if i < NT - 1 else NS


def hybrid_decoder_step(nc, x_prompt, x_sample, state_conv, state_shift, state_wkv, norm1_g, w_in, conv_w, conv_b,
                        conv_ln_g, conv_ln_b, mu_shift, w0, w_decay_up, a0, w_aaa_up, w_gate_up, k_k, k_a, r_k,
                        gn_g, gn_b, w_out, norm2_g, w_router_group, b_router_group, w_router_expert,
                        b_router_expert, w_exp_gate, w_exp_up, w_exp_down, norm_f_g,
                        y_prompt, y_sample, new_conv_p, new_shift_p, new_wkv_p, new_conv_s, new_shift_s, new_wkv_s):
    ctx = ExitStack()
    with ctx:
        def sb(name, shape, dt=F32):
            return ctx.enter_context(nc.sbuf_tensor(name, shape, dt))

        def sem(name):
            return ctx.enter_context(nc.semaphore(name))

        xn2_rows = nc.dram_tensor("xn2_rows", (N, D), F32, kind="Internal").ap()
        y_rows = nc.dram_tensor("y_rows", (N * TOPK, D), F32, kind="Internal").ap()

        ident = sb("ident", [P, P])
        tri_cum = sb("tri_cum", [P, 2, 2, 64])
        tri_cum8 = sb("tri_cum8", [NS, 2, 64])
        mask_ar = sb("mask_ar", [P, 2, 64])
        mask_ar8 = sb("mask_ar8", [P, 2, 64])
        mask_lv = sb("mask_lv", [P, LV, 64])
        mask_lv0t = sb("mask_lv0t", [P, 64])
        seqmask = sb("seqmask", [P, SB, 64])
        rowmask = sb("rowmask", [P, SB])
        headsum = sb("headsum", [P, P])
        headmean = sb("headmean", [P, P])
        head_sel = sb("head_sel", [P, CT, 8])
        head_back = sb("head_back", [P, CT, P])
        chmean = sb("chmean", [P, P])
        before = sb("before", [P, P])
        ones = sb("ones", [P, P])
        prm = sb("prm", [P, NPR])
        om_ka = sb("om_ka", [P, CT])
        cw = sb("cw", [P, W, CT])
        shift0 = sb("shift0", [P, ZT, SB])
        lastz = sb("lastz", [P, ZT, 1 + SB])
        gain = sb("gain", [P, D])
        w0_all = sb("w0_all", [P, C])
        w_da = sb("w_da", [P, C])
        w_g = sb("w_g", [P, C])
        stat = sb("stat", [P, 8, NT])

        ARENA = 46904
        arena = sb("arena", [P, ARENA])

        def at(off, *shape):
            n = int(np.prod(shape))
            assert off + n <= ARENA, (off, n)
            v = arena[:, off:off + n]
            if len(shape) > 1:
                names = "abcdef"[:len(shape)]
                v = v.rearrange(f"p ({' '.join(names)}) -> p {' '.join(names)}",
                                **{k: s for k, s in zip(names[1:], shape[1:])})
            return v

        O_ZS = 0
        O_XN = O_ZS + ZT * N
        O_R1 = O_XN + DC * N
        O_HX = O_R1
        O_WIN = O_HX + CT * HXW
        O_XR = O_WIN + 6 * DC * P
        O_CO = O_XR + 5 * D
        O_EX = O_CO + CT * N
        zs = at(O_ZS, ZT, N)
        squares = at(O_ZS, D)
        xnT = at(O_XN, DC, N)
        hx = at(O_HX, CT, HXW)
        win = [at(O_WIN + s * DC * P, DC, P) for s in range(6)]
        x_in = [at(O_XR + s * D, D) for s in range(3)]
        xn = [at(O_XR + (3 + s) * D, D) for s in range(2)]
        co = at(O_CO, CT, N)
        O_LD = O_CO
        ld_prm = at(O_LD, P)
        ld_cw = at(O_LD + P, P)
        ld_shift = at(O_LD + 2 * P, DS)
        ld_conv = at(O_LD + 2 * P + DS, 2, C)
        zbuf = [at(O_XR + s * ZW, ZW) for s in range(2)]
        zd = at(O_XR + 2 * ZW, N)
        sig = at(O_XR + 2 * ZW + N, N)

        ps = ctx.enter_context(nc.psum_tensor("ps", [P, 8, 512], F32))

        sgw = at(O_WIN, NT, C)
        yT = at(O_WIN, NT, CT, P)
        conv_tail = at(O_XN + 4 * N, 4, C)
        shift_tail = at(O_XN + 4 * N + 4 * C, DS)
        TG = [(0, 3), (3, 6), (6, SB)]
        SK = HB + ST
        nkk, kka = at(O_XN, CT, N), at(O_XN + CT * N, CT, N)
        iclr = [at(O_XR + s * N, N) for s in range(2)]
        kmul = at(O_XR + 2 * N, N)
        ksq = at(O_XR + 3 * N, N)
        knorm = at(O_EX, N)
        w_aa = at(O_EX + N, C)
        R0, K0, V0, WA0, GL0 = 0, 4, 8, 12, 13

        conv_sq = ksq
        conv_rstd = [at(O_XR + 5 * D - SEQ, SEQ), at(O_HX + 10 * C, NS)]

        off = [O_HX]

        def take(*shape):
            v = at(off[0], *shape)
            off[0] += int(np.prod(shape))
            return v

        lwst = take(C)
        vst = take(CT, P)
        e_in = [take(CT, P), at(O_EX + CT * 64, CT, P)]
        e_ex, e_neg = take(CT, P), take(CT, P)
        AR = [take(CT, 2, P), at(O_EX + CT * 64 + CT * P, CT, 2, P)]
        bt, kt = take(CT, P), take(CT, P)
        GK0 = [take(CT, P)]
        btok = [gain[:, c * C:(c + 1) * C].rearrange("p (h n) -> p h n", h=CT) for c in range(2)]
        ktok = [t[:, :].rearrange("p (h n) -> p h n", h=CT) for t in (w_da, w0_all)]
        assert off[0] <= O_WIN
        off[0] = O_XR
        MM = take(2, CT, 64)
        GK0.append(take(CT, P))
        vtok = take(2, CT, 64)
        GB = take(2, CT, 2, 64)
        GK1 = take(2, CT, 64)
        UB = take(CT, P)
        RHS, UU = take(CT, 64), take(CT, 64)
        assert off[0] <= O_XR + 5 * D
        off[0] = O_WIN + NT * C
        X = take(2, CT, 64)
        XT = take(2, CT, P)
        PT = at(O_ZS + WA0 * N, 2, CT, P)
        assert off[0] <= O_XR
        ST0 = at(O_EX, CT, 64)

        s_raw = [at(O_XN + hp * SB * P, SB, P)[0:64, :, :] for hp in range(CT)]
        off[0] = O_XN + CT * SB * P
        S8 = [take(SB, 64) for _ in range(CT)]
        A8 = [take(SB, 64) for _ in range(CT)]
        V8 = [take(SB, 64)]
        assert off[0] <= O_R1
        V8.append(PT[:, 1, :, :].rearrange("p h n -> p (h n)").rearrange("p (b n) -> p b n", b=SB))
        U8 = [t.rearrange("p (b n) -> p b n", b=SB) for t in (
            GB[:, 1, :, :, :].rearrange("p h e n -> p (h e n)"), e_ex.rearrange("p h n -> p (h n)"))]
        s_stage = at(O_EX + CT * 64 + CT * P, CT * P)
        S_IN, S_NEW, S_OUT = (7, 3, 5, 7), (5, 6, 7, 5), (0, 2, 0, 2)

        gn_sq = at(O_HX, N)
        gn_bonus = at(O_HX + N, N)
        gn_rstd = at(O_HX + 2 * N, N)
        wout = at(O_XN, DC, D)
        xres = [at(O_HX + s * D, D) for s in range(3)]
        hres = at(O_ZS, NT, D)
        off[0] = O_ZS + NT * D
        xn2 = [take(D) for _ in range(2)]
        x2T = [take(DC, P) for _ in range(2)]
        squares2 = take(D)
        assert off[0] <= O_XN

        def pieces(ap3, ap2, hp):
            return ((ap3[:, 0:NT - 1, hp, :], ap2[:, 0:SEQ].rearrange("p (i n) -> p i n", n=P)),
                    (ap3[:, NT - 1, hp, 0:NS], ap2[:, SEQ:N]))

        w_rt = w_da[:, 0:DC * (NG + NE)].rearrange("p (c n) -> p c n", c=DC)
        b_rt = w0_all[:, 0:NG + NE]
        lg = at(O_EX, NT, NG + NE)

        O_RT = O_ZS + NT * D + 2 * D
        NCOL = NTILE_X
        off[0] = O_EX + 330
        r_desc = take(EG)
        r_thr = take(EG)
        r_iote = take(NE)
        r_iots = take(P)
        r_iotc = take(NCOL)
        r_val = take(2, NT, TOPK)
        assert off[0] <= O_EX + 768
        off[0] = O_CO
        r_gmax, r_pg, r_gd, r_key4, r_g1 = take(NT), take(NT), take(NT, NG), take(NT, NG), take(NT, NG)
        r_km = take(NT)
        r_e4, r_es, r_key8 = take(NT, NG, EG), take(NT, EG), take(NT, EG)
        r_m1, r_m2, r_ex, r_den = take(NT), take(NT), take(NT), take(NT)
        r_o = take(TOPK, NT, EG)
        O_OH = off[0]
        r_oh = take(TOPK, NT, NE)
        r_m = take(NT, NE)
        r_cum = take(NT + 1, NE)
        r_c = take(NT + 1, NE)
        r_tmp = take(TOPK, NT, NE)
        r_eq = take(NT, NCOL)
        assert off[0] <= O_EX
        r_rank, r_exp, r_base, r_q, r_q1, r_tile, r_slot = (
            at(O_RT + 32 * k, TOPK * NT) for k in range(7))
        off[0] = O_RT + 224
        r_qc = take(TOPK * NT, EG)
        r_xc = take(NE, EG)
        r_s = [take(2, NE) for _ in range(2)]
        r_x = take(NE)
        r_tc = take(EXTRA, NE)
        r_te = take(EXTRA)
        r_n = take(2)
        r_f = take(2, NCOL)
        r_z = take(2, NCOL)
        r_os = [take(NT, P), at(O_EX + 768, NT, P)]
        assert off[0] <= O_XN
        r_ot = [at(O_OH, NT, 2, NCOL), at(O_OH + NT * 2 * NCOL, NT, 2, NCOL)]
        assert O_OH + 2 * NT * 2 * NCOL <= O_EX

        WSZ = 3 * DC * F
        wx = [at(O_XN + s * WSZ, WSZ) for s in range(UN)]
        assert O_XN + UN * WSZ <= O_CO
        off[0] = O_ZS + NT * D
        xg = [take(D) for _ in range(UN)]
        assert off[0] <= O_XN
        off[0] = O_XN + UN * WSZ
        xgT = [take(DC, P) for _ in range(2)]
        ye = [take(D) for _ in range(2)]
        gs, gu = take(F), take(F)
        hT = take(2, P)
        g_idx = [sb(f"g_idx{s}", [P, 1], U32) for s in range(UN)]
        s_idx = [sb(f"s_idx{s}", [P, 1], U32) for s in range(2)]
        YS = 3
        yk = [at(O_XN + s * 2 * D, TOPK, D) for s in range(YS)]
        fin = [at(O_XN + (2 * YS + s) * D, D) for s in range(2)]
        fin_sq = [at(O_XN + (2 * YS + 2 + s) * D, D) for s in range(2)]

        def banks(b, n=1):
            return ps[:, b:b + n, :].rearrange("p b n -> p (b n)")

        const_ready = sem("const_ready")
        pool_chain = sem("pool_chain")
        dve_chain = sem("dve_chain")
        tables_in = sem("tables_in")
        tables_psum = sem("tables_psum")
        tables_done = sem("tables_done")
        gain1_in = sem("gain1_in")
        x_loaded = [sem(f"x_loaded{s}") for s in range(3)]
        sq_done, ms_done, std_done, xn_done = sem("sq_done"), sem("ms_done"), sem("std_done"), sem("xn_done")
        xT_psum, xT_act, xT_dve = sem("xT_psum"), sem("xT_act"), sem("xT_dve")
        w_loaded = [sem(f"w_loaded{s}") for s in range(6)]
        proj_done = sem("proj_done")
        sig_done = sem("sig_done")
        z_ready = sem("z_ready")
        zs_done, last_done, hx_ready, conv_tap = sem("zs_done"), sem("last_done"), sem("hx_ready"), sem("conv_tap")
        tail_psum, tail_copied = sem("tail_psum"), sem("tail_copied")

        tanh_done = sem("tanh_done")
        decay_psum, decay_sum, decay_done = sem("decay_psum"), sem("decay_sum"), sem("decay_done")
        kkr_done, iclr_psum, iclr_done, ksq_done = sem("kkr_done"), sem("iclr_psum"), sem("iclr_done"), sem("ksq_done")
        knorm_part, knorm_root, knorm_done = sem("knorm_part"), sem("knorm_root"), sem("knorm_done")
        kprep_done, kback_psum, kk_done = sem("kprep_done"), sem("kback_psum"), sem("kk_done")
        tails_out = sem("tails_out")

        cmean_psum, cdev_done, csq_done, cvar_part = (sem(n) for n in ("cmean_psum", "cdev_done", "csq_done",
                                                                       "cvar_part"))
        cvar_done, cstd_done = sem("cvar_done"), sem("cstd_done")
        ln_step, ln_sig, ln_done = sem("ln_step"), sem("ln_sig"), sem("ln_done")

        c_in, c_psum, e_done, prod_done = sem("c_in"), sem("c_psum"), sem("e_done"), sem("prod_done")
        prod2_done, ub_done = sem("prod2_done"), sem("ub_done")
        tok_psum, tok_act, tok_dve = sem("tok_psum"), sem("tok_act"), sem("tok_dve")
        gb_psum, gk_psum, gb_done, gk_done, pt_done = (sem(n) for n in ("gb_psum", "gk_psum", "gb_done", "gk_done",
                                                                        "pt_done"))
        x1t_done, m_psum, m_done, x_psum, x_done, xt_act = (sem(n) for n in (
            "x1t_done", "m_psum", "m_done", "x_psum", "x_done", "xt_act"))
        MC, MD, XC, TC = 2 * (LV + 1), 2 * LV + 1, 2 * (LV - 1), LV - 1
        rhs_psum, rhs_done, u_psum, u_done = (sem(n) for n in ("rhs_psum", "rhs_done", "u_psum", "u_done"))
        s_psum, s_sum, s_done, y_psum, y_done = (sem(n) for n in ("s_psum", "s_sum", "s_done", "y_psum", "y_done"))
        pe_past_waits = sem("pe_past_waits")

        def conv_tile(i, r):
            return co[:, :, bass.ds(i * P, r)]

        conv_sig = lwst.rearrange("p (c n) -> p c n", c=CT)

        def token_rows(t, c, p):
            return vtok[p:p + 64, c, :, :] if t is vtok else t[c][p:p + 64, :, p:p + 64]

        def rwkv_turns(engine, turn):
            with engine.Fori(0, (NT - 1) // 2 - 1) as t:
                for q in range(2):
                    turn(2 * t + q, q, P)
            turn(NT - 3, 0, P)
            turn(NT - 2, 1, NS)

        fin_psum, fin_copied, fin_stored = sem("fin_psum"), sem("fin_copied"), sem("fin_stored")
        s_loaded, s8_psum, s8_in = sem("s_loaded"), sem("s8_psum"), sem("s8_in")
        a8_done, uv8_done, s8_done = sem("a8_done"), sem("uv8_done"), sem("s8_done")

        gmean_psum, gdev_done, gsq_done, gvar_part = (sem(n) for n in ("gmean_psum", "gdev_done", "gsq_done",
                                                                       "gvar_part"))
        gvar_done, gstd_done, grstd_done = sem("gvar_done"), sem("gstd_done"), sem("grstd_done")
        gback_psum, gback_used, rk_done, rk_psum, rk_used = (sem(n) for n in ("gback_psum", "gback_used", "rk_done",
                                                                              "rk_psum", "rk_used"))
        gate_psum, mix_done = sem("gate_psum"), sem("mix_done")
        tables2_in = sem("tables2_in")
        o_psum, h_done, xn2_done = sem("o_psum"), sem("h_done"), sem("xn2_done")
        xn2_stored = [sem(f"xn2_stored{s}") for s in range(2)]
        lg_psum, lg_done = sem("lg_psum"), sem("lg_done")

        idx = sb("idx", [P, 2, NCOL], U32)
        te_u = sb("te_u", [1, NTILE_X], U32)
        last_turn = sb("last_turn", [1, 1], U32)
        w_k = shift0[:, :, :].rearrange("p t b -> p (t b)")[:, 0:TOPK * NT].rearrange("p (k i) -> p k i", k=TOPK)
        turns_ready = sem("turns_ready")
        iota_done, softmax_in, softmax_done = sem("iota_done"), sem("softmax_in"), sem("softmax_done")
        cum_done, rank_psum, onehot_done, onehot_used, idx_done = (sem(n) for n in (
            "cum_done", "rank_psum", "onehot_done", "onehot_used", "idx_done"))

        wx_in = w_loaded[0:UN]
        wx_0 = [16 * len(range(s, MT, 6)) for s in range(UN)]
        xg_zero = sem("xg_zero")
        pool_past_waits = sem("pool_past_waits")
        gi_ready, si_ready = sem("gi_ready"), sem("si_ready")
        xg_in = [sem(f"xg_in{s}") for s in range(UN)]
        ye_out = [sem(f"ye_out{s}") for s in range(2)]
        gu_psum, gs_done, gmul_done, hx_done, ht_psum, ht_done = (sem(n) for n in (
            "gu_psum", "gs_done", "gmul_done", "hx_done", "ht_psum", "ht_done"))
        yd_psum, ye_act, ye_dve = sem("yd_psum"), sem("ye_act"), sem("ye_dve")
        yk_in = [sem(f"yk_in{s}") for s in range(YS)]
        ff_done, fin_done = sem("ff_done"), sem("fin_done")
        fin_out = [sem(f"fin_out{s}") for s in range(2)]

        def expert_turns(engine, step):
            engine.wait_ge(turns_ready, 1)
            last = engine.value_load(last_turn[0:1, 0:1], min_val=NE // UN - 1, max_val=NTILE_X // UN - 1)
            with engine.Fori(0, last) as t:
                for s in range(UN):
                    step(t, s, UN)
            for s in range(UN):
                step(last, s, UN - 1 - s)
            return last

        block = ctx.enter_context(nc.Block())

        @block.sync
        def _(sp):
            def load_x(i):
                if i >= 3:
                    sp.wait_ge(xn_done, i - 2)
                src = x_prompt[0, i * P:(i + 1) * P, :] if i < NT - 1 else x_sample.rearrange("b t d -> (b t) d")
                sp.dma_start(x_in[i % 3][0:rows_of(i), :], src).then_inc(x_loaded[i % 3], 16)

            load_x(0)
            sp.dma_start(gain[:, :], norm1_g[0, :].partition_broadcast(P)).then_inc(gain1_in, 16)
            load_x(1)
            load_x(2)
            for vec, name in ((mu_shift, "mu"), (k_k, "k_k"), (k_a, "k_a"), (r_k, "r_k"), (a0, "a0"), (gn_g, "gn_g"),
                              (gn_b, "gn_b"), (conv_b, "conv_b"), (conv_ln_g, "ln_g"), (conv_ln_b, "ln_b")):
                r0, n = PR[name]
                sp.dma_start(ld_prm[r0:r0 + n, :], vec[0, :].rearrange("(t p) -> t p", p=P)).then_inc(tables_in, 16)
            sp.dma_start(ld_cw[0:W * CT, :], conv_w[0].rearrange("k (c p) -> (k c) p", p=P)).then_inc(tables_in, 16)
            sp.dma_start(ld_shift[0:SB, :], state_shift[0]).then_inc(tables_in, 16)
            sc = state_conv[0].rearrange("(h b) k c -> h (b k) c", h=2)
            for h in range(2):
                sp.dma_start(ld_conv[0:4 * HB, h, :], sc[h]).then_inc(tables_in, 16)
            sp.dma_start(w0_all[:, :], w0[0, :].partition_broadcast(P)).then_inc(tables_in, 16)
            sp.dma_start(w_da[0:64, :], w_decay_up[0]).then_inc(tables_in, 16)
            sp.dma_start(w_aa[64:128, :], w_aaa_up[0]).then_inc(tables_in, 16)
            sp.dma_start(w_g[:, :], w_gate_up[0]).then_inc(tables_in, 16)
            for i in range(3, NT):
                load_x(i)
            for q, t in enumerate(ORDER):
                if q >= 6:
                    sp.wait_ge(proj_done, q - 5)
                sp.dma_start(win[q % 6][:, :, :], w_in[0, :, t * P:(t + 1) * P].rearrange("(c p) n -> p c n", p=P))\
                    .then_inc(w_loaded[q % 6], 16)

            sp.wait_ge(tail_copied, 2)
            sp.dma_start(new_shift_p[0], shift_tail[0:1, :]).then_inc(tails_out, 16)
            sp.dma_start(new_shift_s[0], shift_tail[1:1 + SB, :]).then_inc(tails_out, 16)
            sp.wait_ge(tail_copied, 6)
            sp.dma_start(new_conv_p[0, 0], conv_tail[0:HB, 0, :]).then_inc(tails_out, 16)
            for g, (b0, b1) in enumerate(TG):
                for b in range(b0, b1):
                    r0 = (b - b0) * SK + ST
                    sp.dma_start(new_conv_s[0, b], conv_tail[r0:r0 + HB, 1 + g, :]).then_inc(tails_out, 16)

            sp.wait_ge(prod_done, NT)
            for hp in range(CT):
                for p in range(2):
                    sp.dma_start(s_raw[hp][:, :, p * 64:p * 64 + 64], state_wkv[0, :, 2 * hp + p].rearrange(
                        "b v k -> v b k")).then_inc(s_loaded, 16)
            sp.wait_ge(fin_copied, 1)
            for p in range(2):
                sp.dma_start(new_wkv_p[0, 0].rearrange("(h p) v k -> p v h k", p=2)[p],
                             s_stage[0:64, :].rearrange("v (h p k) -> v h p k", h=CT, p=2)[:, :, p, :])\
                    .then_inc(fin_stored, 16)
            for hp in range(CT):
                sp.wait_ge(fin_copied, hp + 2)
                for p in range(2):
                    sp.dma_start(new_wkv_s[0, :, 2 * hp + p].rearrange("b v k -> v b k"),
                                 s_raw[hp][:, :, p * 64:p * 64 + 64]).then_inc(fin_stored, 16)

            sp.dma_start(gain[:, :], norm2_g[0, :].partition_broadcast(P)).then_inc(tables2_in, 16)
            sp.dma_start(w_rt[:, :, 0:NG], w_router_group[0].rearrange("(p c) n -> p c n", c=DC)).then_inc(tables2_in, 16)
            sp.dma_start(w_rt[:, :, NG:], w_router_expert[0].rearrange("(p c) n -> p c n", c=DC)).then_inc(tables2_in, 16)
            sp.dma_start(b_rt[:, 0:NG], b_router_group[0, :].partition_broadcast(P)).then_inc(tables2_in, 16)
            sp.dma_start(b_rt[:, NG:], b_router_expert[0, :].partition_broadcast(P)).then_inc(tables2_in, 16)
            sp.wait_ge(fin_stored, 32 * (CT + 1))
            sp.dma_start(wout, w_out[0].rearrange("(c p) n -> p c n", p=P)).then_inc(tables2_in, 16)
            sp.wait_ge(mix_done, CT)
            for i in range(NT):
                r = rows_of(i)
                if i >= 3:
                    sp.wait_ge(h_done, i - 2)
                src = x_prompt[0, i * P:(i + 1) * P, :] if i < NT - 1 else x_sample.rearrange("b t d -> (b t) d")
                sp.dma_start(xres[i % 3][0:r, :], src).then_inc(x_loaded[i % 3], 16)
                if i >= 2:
                    j = i - 2
                    sp.wait_ge(xn2_done, j + 1)
                    sp.dma_start(xn2_rows[j * P:j * P + rows_of(j), :], xn2[j % 2][0:rows_of(j), :])\
                        .then_inc(xn2_stored[j % 2], 16)
            for j in range(NT - 2, NT):
                sp.wait_ge(xn2_done, j + 1)
                sp.dma_start(xn2_rows[j * P:j * P + rows_of(j), :], xn2[j % 2][0:rows_of(j), :])\
                    .then_inc(xn2_stored[j % 2], 16)

            def load_expert(e, s):
                for part, (w, m) in enumerate(((w_exp_gate, DC), (w_exp_up, DC), (w_exp_down, 2))):
                    src = w[0].rearrange("g e (p c) n -> (g e) p (c n)", c=m)
                    sp.dma_start(wx[s][:, part * DC * F:(part + 1) * DC * F],
                                 src[bass.ds(e, 1), :, :].rearrange("a p n -> (a p) n"))\
                        .then_inc(wx_in[s], 16)

            sp.wait_ge(o_psum, NT)
            sp.wait_ge(h_done, NT)
            for s in range(UN):
                load_expert(s, s)
            sp.wait_ge(turns_ready, 1)
            last_sp = sp.value_load(last_turn[0:1, 0:1], min_val=NE // UN - 1, max_val=NTILE_X // UN - 1)
            with sp.Fori(0, last_sp) as t:
                for s in range(UN):
                    sp.wait_ge(yd_psum, UN * t + s + 1)
                    e = sp.value_load(te_u[0:1, bass.ds(UN * t + s + UN, 1)], min_val=0, max_val=NE - 1)
                    load_expert(e, s)
            sp.dma_start(gain[:, :], norm_f_g.partition_broadcast(P)).then_inc(tables2_in, 16)
            for s in range(2):
                sp.wait_ge(ye_out[s], last_sp * (16 * UN // 2) + 16 * UN // 2)
            sp.wait_ge(yd_psum, last_sp * UN + UN)
            y_pairs = y_rows.rearrange("(n k) d -> n k d", k=TOPK)

            def result_out(i):
                r = rows_of(i)
                sp.wait_ge(fin_done, i + 1)
                dst = y_prompt[0, i * P:(i + 1) * P, :] if i < NT - 1 else y_sample.rearrange("b t d -> (b t) d")
                sp.dma_start(dst, fin[i % 2][0:r, :]).then_inc(fin_out[i % 2], 16)

            for i in range(NT):
                r = rows_of(i)
                if i >= YS:
                    sp.wait_ge(ff_done, i - YS + 1)
                sp.dma_start(yk[i % YS][0:r, :, :], y_pairs[i * P:i * P + r, :, :]).then_inc(yk_in[i % YS], 16)
                if i >= YS:
                    result_out(i - YS)
            for i in range(NT - YS, NT):
                result_out(i)
            sp.wait_ge(fin_out[0], 16 * ((NT + 1) // 2))
            sp.wait_ge(fin_out[1], 16 * (NT // 2))
            sp.wait_ge(fin_stored, 32 * (CT + 1))
            sp.wait_ge(tails_out, 16 * (3 + SB))

        N_TABLES = 18

        @block.gpsimd
        def _(pool):
            step = [0]

            def link(ins):
                step[0] += 1
                ins.then_inc(pool_chain, 1)
                pool.wait_ge(pool_chain, step[0])

            def select(v, cmp, base, cm, pattern, fill=0.0):
                link(pool.affine_select(out=v, in_=v, compare_op=cmp, fill=fill, base=base, pattern=pattern,
                                        channel_multiplier=cm))

            link(pool.memset(ident[:, :], 0.0))
            select(ident[:, :], ALU.not_equal, 0, 1, [[-1, P]], 1.0)
            pool.sem_inc(const_ready, 1)
            link(pool.memset(tri_cum[:, :, :, :], LOGW))
            select(tri_cum[:, 0, :, :], ALU.is_ge, 0, -1, [[64, 2], [1, 64]])
            select(tri_cum[:, 1, :, :], ALU.is_ge, -1, -1, [[64, 2], [1, 64]])
            for e in range(2):
                select(tri_cum[:, e, :, :], ALU.is_ge, 0, 1, [[-64, 2], [0, 64]])
            link(pool.memset(tri_cum8[:, :, :], LOGW))
            select(tri_cum8[:, 0, :], ALU.is_ge, 0, -1, [[1, 64]])
            select(tri_cum8[:, 1, :], ALU.is_ge, -1, -1, [[1, 64]])
            for e in range(2):
                select(tri_cum8[:, e, :], ALU.is_ge, 0, 1, [[-ST, SB], [0, ST]])
            link(pool.memset(mask_ar[0:64, :, :], 1.0))
            select(mask_ar[0:64, 0, :], ALU.is_ge, -1, -1, [[1, 64]])
            select(mask_ar[0:64, 1, :], ALU.is_ge, 0, -1, [[1, 64]])
            link(pool.memset(mask_ar8[0:64, :, :], 1.0))
            select(mask_ar8[0:64, 0, :], ALU.is_ge, -1, -1, [[1, 64]])
            select(mask_ar8[0:64, 1, :], ALU.is_ge, 0, -1, [[1, 64]])
            for e in range(2):
                select(mask_ar8[0:64, e, :], ALU.is_ge, 0, 1, [[-ST, SB], [0, ST]])
            link(pool.memset(mask_lv[0:64, :, :], 1.0))
            for k in range(LV):
                m = 1 << k
                v = mask_lv[0:64, k, :]
                select(v, ALU.is_ge, -m, 1, [[-2 * m, 32 // m], [0, 2 * m]])
                select(v, ALU.is_ge, 2 * m - 1, -1, [[2 * m, 32 // m], [0, 2 * m]])
                select(v, ALU.is_ge, m - 1, 0, [[0, 32 // m], [-1, 2 * m]])
                select(v, ALU.not_equal, 0, 1, [[-1, 64]], 1.0)
            link(pool.memset(mask_lv0t[0:64, :], 1.0))
            select(mask_lv0t[0:64, :], ALU.is_ge, 0, 1, [[-2, 32], [0, 2]])
            select(mask_lv0t[0:64, :], ALU.is_ge, 0, -1, [[2, 32], [0, 2]])
            select(mask_lv0t[0:64, :], ALU.is_ge, -1, 0, [[0, 32], [1, 2]])
            select(mask_lv0t[0:64, :], ALU.not_equal, 0, 1, [[-1, 64]], 1.0)
            link(pool.memset(rowmask[0:64, :], 1.0))
            select(rowmask[0:64, :], ALU.is_ge, 0, 1, [[-ST, SB]])
            select(rowmask[0:64, :], ALU.is_ge, ST - 1, -1, [[ST, SB]])
            link(pool.memset(seqmask[:, :, :], 1.0))
            select(seqmask[:, :, :], ALU.is_ge, 0, 0, [[-ST, SB], [1, 64]])
            select(seqmask[:, :, :], ALU.is_ge, ST - 1, 0, [[ST, SB], [-1, 64]])
            for m, v in ((headsum, 1.0), (headmean, 1.0 / HD)):
                link(pool.memset(m[:, :], 0.0))
                link(pool.memset(m[0:64, 0:64], v))
                link(pool.memset(m[64:128, 64:128], v))
            link(pool.memset(head_sel[:, :, :], 0.0))
            for hp in range(CT):
                link(pool.memset(head_sel[0:64, hp, 2 * hp:2 * hp + 1], 1.0))
                link(pool.memset(head_sel[64:128, hp, 2 * hp + 1:2 * hp + 2], 1.0))
            link(pool.memset(w_da[64:128, :], 0.0))
            link(pool.memset(w_aa[0:64, :], 0.0))
            link(pool.memset(knorm, 0.0))
            link(pool.memset(head_back[:, :, :], 0.0))
            for hp in range(CT):
                select(head_back[:, hp, :], ALU.not_equal, 2 * hp, -1, [[1, 2], [0, 64]], 1.0)
            link(pool.memset(chmean[:, :], 1.0 / C))
            link(pool.memset(ones[:, :], 1.0))
            link(pool.memset(before[:, :], 1.0))
            pool.affine_select(out=before[:, :], in_=before[:, :], compare_op=ALU.is_ge, fill=0.0, base=-1,
                               pattern=[[1, P]], channel_multiplier=-1).then_inc(const_ready, 1)

            for j in range(ZT):
                q = NCONV + j
                zt = ORDER[q] - 8
                pool.wait_ge(z_ready, j + 1)
                pool.tensor_copy(lastz[:, zt, 0:1], zbuf[j % 2][:, SEQ:SEQ + 1])
                pool.tensor_copy(lastz[:, zt, 1:1 + SB], zbuf[j % 2][:, 1 + SEQ:].rearrange(
                    "p (b t) -> p b t", b=SB)[:, :, ST]).then_inc(last_done, 1)
            pool.wait_ge(kk_done, CT)
            pool.wait_ge(cstd_done, 1)
            pool.wait_ge(decay_done, NT)
            for t in (*GK0, *btok, *ktok, UB):
                pool.memset(t, 0.0)
            pool.memset(PT, 0.0)
            pool.memset(XT, 0.0)
            pool.memset(ST0, 0.0).then_inc(s_done, 1)

            def stage_in(i, r, first=False):
                if not first:
                    pool.wait_ge(c_psum, i)
                    pool.wait_ge(ln_done, i)
                pool.tensor_copy(lwst[0:r, :].rearrange("p (a n) -> p a n", a=1), sgw[0:r, bass.ds(i, 1), :])
                if not first:
                    pool.wait_ge(tok_psum, 3 * i - 2)
                pool.tensor_copy(vst[:, :, 0:r], zs[:, V0:V0 + CT, bass.ds(i * P, r)]).then_inc(c_in, 1)

            def scaled_r_k(i, q, r, first=False):
                pool.wait_ge(e_done, i + 1)
                if not first:
                    pool.wait_ge(gk_psum, 2 * i)
                pool.tensor_tensor(AR[q][:, :, 1, 0:r], zs[:, R0:R0 + CT, bass.ds(i * P, r)], e_in[q][:, :, 0:r],
                                   ALU.mult)
                pool.tensor_tensor(kt[:, :, 0:r], zs[:, K0:K0 + CT, bass.ds(i * P, r)], e_neg[:, :, 0:r], ALU.mult)\
                    .then_inc(prod2_done, 1)

            def x1t(n, c):
                pool.wait_ge(pt_done, n + 1)
                pool.tensor_tensor(XT[:, c, :, :].rearrange("p h (q n) -> p (h q) n", q=2),
                                   PT[:, c, :, :].rearrange("p h (q n) -> p (h q) n", q=2),
                                   mask_lv0t[:, :].unsqueeze(1).broadcast_to([P, 2 * CT, 64]), ALU.mult)\
                    .then_inc(x1t_done, 1)

            def pool_turn(i, q, next_r):
                stage_in(i + 1, next_r)
                for c in range(2):
                    x1t(2 * i + c, c)
                scaled_r_k(i + 1, 1 - q, next_r)

            stage_in(0, P, first=True)
            scaled_r_k(0, 0, P, first=True)
            rwkv_turns(pool, pool_turn)
            x1t(2 * (NT - 1), 0)

            pool.wait_ge(fin_psum, CT + 1)
            for v, pattern, base, cm in ((r_desc, [[-1, EG]], EG, 0), (r_thr, [[P, EG]], P, 0), (r_iote, [[1, NE]], 0, 0),
                                         (r_iots, [[1, P]], 0, 0), (r_iotc, [[1, NCOL]], 0, 0),
                                         (r_val[:, 0, :, :], [[TOPK * P, NT], [1, TOPK]], 1, TOPK),
                                         (r_val[:, 1, :, :], [[P, NT], [0, TOPK]], 1, 1)):
                ins = pool.iota(v, pattern=pattern, base=base, channel_multiplier=cm,
                                allow_small_or_imprecise_dtypes=True)
            ins.then_inc(iota_done, 1)

            pool.wait_ge(xn2_stored[0], 16 * ((NT + 1) // 2))
            pool.wait_ge(xn2_stored[1], 16 * (NT // 2))
            pool.wait_ge(lg_done, NT)

            def clear(s):
                for v in s:
                    ins = pool.memset(xg[v], 0.0)
                ins.then_inc(xg_zero, 1)

            clear((0, 1))
            pool.wait_ge(idx_done, 1)
            pool.wait_ge(xg_zero, 1)

            def gather(u, s):
                pool.tensor_copy(g_idx[s][:, :], idx[:, 1, bass.ds(u, 1)]).then_inc(gi_ready, 1)
                pool.wait_ge(gi_ready, u + 1)
                pool.sem_inc(pool_past_waits, 1)
                pool.indirect_dma_start(out=xg[s], out_offset=None, in_=xn2_rows,
                                        in_offset=bass.IndirectOffsetOnAxis(ap=g_idx[s][:, :], axis=0),
                                        bounds_check=N - 1, oob_is_err=False).then_inc(xg_in[s], 16)

            def scatter(u, s):
                pool.wait_ge(ye_act, u + 1)
                pool.wait_ge(ye_dve, u + 1)
                pool.tensor_copy(s_idx[s][:, :], idx[:, 0, bass.ds(u, 1)]).then_inc(si_ready, 1)
                pool.wait_ge(si_ready, u + 1)
                pool.sem_inc(pool_past_waits, 1)
                pool.indirect_dma_start(out=y_rows, out_offset=bass.IndirectOffsetOnAxis(ap=s_idx[s][:, :], axis=0),
                                        in_=ye[s], in_offset=None, bounds_check=N * TOPK - 1, oob_is_err=False)\
                    .then_inc(ye_out[s], 16)

            def pool_step(turn, s, ahead):
                u = UN * turn + s
                if ahead >= 3:
                    pool.wait_ge(xT_psum, 2 * NT + u)
                    gather(u + 3, (s + 3) % UN)
                scatter(u, s % 2)

            for u in range(2):
                gather(u, u)
            pool.wait_ge(turns_ready, 1)
            clear((2, 3))
            pool.wait_ge(xg_zero, 2)
            gather(2, 2)
            expert_turns(pool, pool_step)


        @block.scalar
        def _(act):
            def square(i):
                r = rows_of(i)
                act.wait_ge(x_loaded[i % 3], 16 * (i // 3 + 1))
                act.activation(squares[0:r, :], x_in[i % 3][0:r, :], ACT.Square,
                               accum_out=stat[0:r, 0, i:i + 1]).then_inc(sq_done, 1)

            def root(i):
                r = rows_of(i)
                act.wait_ge(ms_done, i + 1)
                act.activation(stat[0:r, 2, i:i + 1], stat[0:r, 1, i:i + 1], ACT.Sqrt).then_inc(std_done, 1)

            def copy_T(i):
                act.wait_ge(xT_psum, i + 1)
                r = rows_of(i)
                act.activation(xnT[:, 0:4, i * P:i * P + r],
                               banks(2 * (i % 2)).rearrange("p (c n) -> p c n", c=4)[:, :, 0:r], ACT.Copy)\
                    .then_inc(xT_act, 1)

            square(0)
            root(0)
            square(1)
            root(1)
            for i in range(NT):
                if i + 2 < NT:
                    square(i + 2)
                    root(i + 2)
                copy_T(i)

            for q, t in enumerate(ORDER):
                pr = banks(3 * (q % 2), 3)
                act.wait_ge(proj_done, q + 1)
                if q < NCONV:
                    if q % 2 == 0:
                        if q >= 2:
                            act.wait_ge(hx_ready, q // 2)
                        else:
                            act.wait_ge(xn_done, NT)
                            act.wait_ge(xT_psum, NT)
                        act.activation(sig[:, :], pr[:, 0:N], ACT.Sigmoid).then_inc(sig_done, 1)
                    continue
                j = q - NCONV
                zb = zbuf[j % 2]
                if j >= 2:
                    act.wait_ge(zs_done, j - 1)
                    act.wait_ge(last_done, j - 1)
                act.activation(zb[:, 1:1 + SEQ], pr[:, 0:SEQ], ACT.Copy)
                act.activation(zb[:, 1 + SEQ:].rearrange("p (b t) -> p b t", b=SB)[:, :, 1:],
                               pr[:, SEQ:N].rearrange("p (b t) -> p b t", b=SB), ACT.Copy)
                act.activation(zb[:, 1 + SEQ:].rearrange("p (b t) -> p b t", b=SB)[:, :, 0],
                               shift0[:, t - 8, :], ACT.Copy)
                act.activation(zb[:, 0:1], stat[:, 7, 0:1], ACT.Copy).then_inc(z_ready, 1)

            act.wait_ge(zs_done, ZT)
            act.activation(zs[0:64, WA0, :], zs[0:64, WA0, :], ACT.Tanh)
            act.activation(zs[:, GL0, :], zs[:, GL0, :], ACT.Sigmoid).then_inc(tanh_done, 1)
            for h in range(2):
                act.wait_ge(tail_psum, h + 1)
                act.activation(shift_tail[0:1 + SB, h * 7 * P:(h + 1) * 7 * P], banks(6, 2)[0:1 + SB, 0:7 * P],
                               ACT.Copy).then_inc(tail_copied, 1)
            for j, rows in enumerate([HB] + [(b1 - b0) * SK for b0, b1 in TG]):
                act.wait_ge(tail_psum, 3 + j)
                act.activation(conv_tail[0:rows, j, :], banks((6, 7, 6, 7)[j])[0:rows, :], ACT.Copy)\
                    .then_inc(tail_copied, 1)
            for i in range(NT):
                act.wait_ge(decay_sum, i + 1)
                r = rows_of(i)
                act.activation(sgw[0:r, i, :], sgw[0:r, i, :], ACT.Sigmoid).then_inc(decay_done, 1)
            for hp in range(CT):
                act.wait_ge(iclr_psum, hp + 1)
                if hp >= 2:
                    act.wait_ge(kprep_done, hp - 1)
                a0_col = PR["a0"][0] + hp
                act.activation(iclr[hp % 2], banks(3, 3)[:, 0:N], ACT.Sigmoid, bias=prm[:, a0_col:a0_col + 1])\
                    .then_inc(iclr_done, 1)
                act.wait_ge(kkr_done, hp + 1)
                if hp >= 1:
                    act.wait_ge(knorm_part, hp)
                act.activation(ksq, nkk[:, hp, :], ACT.Square).then_inc(ksq_done, 1)
            act.wait_ge(knorm_part, CT)
            act.activation(knorm[0:8, :], banks(0, 3)[0:8, 0:N], ACT.Sqrt).then_inc(knorm_root, 1)

            for c in range(CT):
                act.wait_ge(cdev_done, c + 1)
                act.wait_ge(knorm_part, CT)
                if c:
                    act.wait_ge(cvar_part, c)
                act.activation(conv_sq, co[:, c, :], ACT.Square).then_inc(csq_done, 1)
            act.wait_ge(cvar_done, 1)
            for v in conv_rstd:
                ins = act.activation(v, v, ACT.Sqrt)
            ins.then_inc(cstd_done, 1)

            def exps(i, q, r, part):
                if r == P:
                    cum = ps[:, 0:2, :].rearrange("p b (h e n) -> p (b h) e n", h=2, e=2)
                else:
                    cum = banks(0).rearrange("p (h e n) -> p h e n", h=CT, e=2)
                if part == 0:
                    act.wait_ge(c_psum, i + 1)
                    act.activation(e_in[q][:, :, 0:r], cum[:, :, 0, :], ACT.Exp)
                elif part == 1:
                    act.activation(e_neg[:, :, 0:r], cum[:, :, 0, :], ACT.Exp, scale=-1.0)
                else:
                    act.activation(e_ex[:, :, 0:r], cum[:, :, 1, :], ACT.Exp).then_inc(e_done, 1)

            def tok_copies(i, r):
                for j, (dst, b) in enumerate(((vtok, 0), (btok, 1), (ktok, 0))):
                    act.wait_ge(tok_psum, 3 * i + j + 1)
                    src = banks(b).rearrange("p (h n) -> p h n", h=CT)
                    act.activation(token_rows(dst, 0, 0), src[0:64, :, 0:64], ACT.Copy)
                    act.activation(token_rows(dst, 0, 64), src[0:64, :, 64:128], ACT.Copy).then_inc(tok_act, 1)

            def x_copy(n, c):
                act.wait_ge(x_psum, n + 1)
                act.activation(X[:, c, :, :], banks(6 + c)[:, 256:512].rearrange("p (h n) -> p h n", h=CT), ACT.Copy)\
                    .then_inc(x_done, 1)

            def xt_copy(m):
                act.wait_ge(m_psum, m + 1)
                src = banks(4)[0:64, :].rearrange("p (h n) -> p h n", h=CT)
                act.activation(XT[0:64, 0, :, 0:64], src[:, :, 0:64], ACT.Copy)
                act.activation(XT[64:128, 0, :, 64:128], src[:, :, 64:128], ACT.Copy).then_inc(xt_act, 1)

            def rhs_copy(n):
                act.wait_ge(rhs_psum, n + 1)
                act.activation(RHS, banks(2)[:, 0:CT * 64].rearrange("p (h n) -> p h n", h=CT), ACT.Copy)\
                    .then_inc(rhs_done, 1)

            def y_copy(i, n, c):
                act.wait_ge(y_psum, n + 1)
                act.activation(yT[:, bass.ds(i, 1), :, c * 64:c * 64 + 64].rearrange("p a h n -> p (a h) n"),
                               banks(4)[:, 0:CT * 64].rearrange("p (h n) -> p h n", h=CT), ACT.Copy)\
                    .then_inc(y_done, 1)

            act.sem_inc(y_done, 1)

            def conv_sigmoid(i, r):
                act.wait_ge(ln_step, 4 * i + 4)
                act.activation(conv_sig[:, :, 0:r], conv_tile(i, r), ACT.Sigmoid).then_inc(ln_sig, 1)

            def act_turn(i, q, next_r):
                tok_copies(i, P)
                for k in range(1, LV + 1):
                    if k >= 2:
                        xt_copy(MC * i + 2 * k)
                    if k == LV:
                        break
                    for c in range(2):
                        x_copy(XC * i + 2 * (k - 1) + c, c)
                    if k <= 3:
                        exps(i + 1, 1 - q, next_r, k - 1)
                conv_sigmoid(i, P)
                for c in range(2):
                    rhs_copy(2 * i + c)
                    y_copy(i, 2 * i + c, c)

            for part in range(3):
                exps(0, 0, P, part)
            rwkv_turns(act, act_turn)

            act.wait_ge(fin_psum, 1)
            act.activation(s_stage[0:64, :], banks(0)[0:64, :], ACT.Copy).then_inc(fin_copied, 1)
            i8, n8 = NT - 1, 2 * (NT - 1)
            for hp in range(CT):
                act.wait_ge(s8_psum, hp + 1)
                act.activation(S8[hp], banks(S_IN[hp]).rearrange("p (b n) -> p b n", b=SB), ACT.Copy)\
                    .then_inc(s8_in, 1)
            tok_copies(i8, NS)
            for k in range(1, LV8 + 1):
                if k >= 2:
                    xt_copy(MC * i8 + k)
                if k < LV8:
                    x_copy(XC * i8 + k - 1, 0)
            rhs_copy(n8)
            y_copy(i8, n8, 0)
            conv_sigmoid(i8, NS)
            for hp in range(CT):
                act.wait_ge(fin_psum, hp + 2)
                act.activation(s_raw[hp], banks(S_OUT[hp], 2)[0:64, :].rearrange("v (b n) -> v b n", b=SB), ACT.Copy)\
                    .then_inc(fin_copied, 1)

            for hp in range(CT):
                act.wait_ge(gdev_done, hp + 1)
                if hp:
                    act.wait_ge(gvar_part, hp)
                for m, (y3, flat) in enumerate(pieces(yT, gn_sq, hp)):
                    ins = act.activation(flat, y3, ACT.Square)
                ins.then_inc(gsq_done, 1)
            act.wait_ge(gvar_done, 1)
            act.activation(gn_rstd[0:8, :], gn_rstd[0:8, :], ACT.Sqrt).then_inc(gstd_done, 1)

            def square2(i):
                r = rows_of(i)
                act.wait_ge(h_done, i + 1)
                act.activation(squares2[0:r, :], hres[0:r, i, :], ACT.Square, accum_out=stat[0:r, 4, i:i + 1])\
                    .then_inc(sq_done, 1)
                act.wait_ge(ms_done, NT + i + 1)
                act.activation(stat[0:r, 6, i:i + 1], stat[0:r, 5, i:i + 1], ACT.Sqrt).then_inc(std_done, 1)

            def copy_T2(i):
                r = rows_of(i)
                act.wait_ge(xT_psum, NT + i + 1)
                if i >= 2:
                    act.wait_ge(lg_psum, i - 1)
                act.activation(x2T[i % 2][:, 0:4, 0:r], banks(4).rearrange("p (c n) -> p c n", c=4)[:, :, 0:r],
                               ACT.Copy).then_inc(xT_act, 1)

            for i in range(NT):
                square2(i)
                if i:
                    copy_T2(i - 1)
            copy_T2(NT - 1)

            act.wait_ge(softmax_in, 1)
            act.activation(r_gd, r_gd, ACT.Exp).then_inc(softmax_done, 1)
            act.wait_ge(softmax_in, 2)
            act.activation(r_ex, r_ex, ACT.Exp).then_inc(softmax_done, 1)

            def sigmoid(u, s):
                act.wait_ge(gu_psum, u + 1)
                act.wait_ge(hx_done, u)
                act.activation(gs, banks(s % 2)[:, 0:F], ACT.Sigmoid).then_inc(gs_done, 1)

            def copy_xg(u, s):
                act.wait_ge(xT_psum, 2 * NT + u + 1)
                act.activation(xgT[s % 2][:, 0:4, :], banks(2).rearrange("p (c n) -> p c n", c=4), ACT.Copy)\
                    .then_inc(xT_act, 1)

            def act_step(turn, s, ahead):
                u = UN * turn + s
                if ahead >= 1:
                    sigmoid(u + 1, s + 1)
                if ahead >= 2:
                    copy_xg(u + 2, s)
                act.wait_ge(yd_psum, u + 1)
                act.wait_ge(ye_out[s % 2], 16 * ((UN // 2) * turn + s // 2))
                act.activation(ye[s % 2][:, 0:512], banks(5), ACT.Copy).then_inc(ye_act, 1)

            copy_xg(0, 0)
            sigmoid(0, 0)
            copy_xg(1, 1)
            last_act = expert_turns(act, act_step)

            act.wait_ge(yd_psum, last_act * UN + UN)
            for i in range(NT + 1):
                if i < NT:
                    r = rows_of(i)
                    act.wait_ge(ff_done, i + 1)
                    act.activation(fin_sq[i % 2][0:r, :], hres[0:r, i, :], ACT.Square, accum_out=stat[0:r, 0, i:i + 1])\
                        .then_inc(sq_done, 1)
                if i >= 1:
                    r = rows_of(i - 1)
                    act.wait_ge(ms_done, 2 * NT + i)
                    act.activation(stat[0:r, 2, i - 1:i], stat[0:r, 1, i - 1:i], ACT.Sqrt).then_inc(std_done, 1)

        @block.tensor
        def _(pe):
            pe.wait_ge(const_ready, 1)
            def tables():
                pe.wait_ge(tables_in, 16 * N_TABLES)
                tb = banks(6)
                pe.transpose(tb[:, 0:NPR], ld_prm[0:NPR, :], ident[0:NPR, 0:NPR])
                pe.transpose(tb[:, 64:64 + W * CT], ld_cw[0:W * CT, :], ident[0:W * CT, 0:W * CT])
                for t in range(ZT):
                    pe.transpose(tb[:, 192 + SB * t:192 + SB * (t + 1)], ld_shift[0:SB, t * P:(t + 1) * P],
                                 ident[0:SB, 0:SB])
                for h in range(2):
                    for c in range(CT):
                        ins = pe.transpose(banks(4 + h)[:, c * 4 * HB:(c + 1) * 4 * HB],
                                           ld_conv[0:4 * HB, h, c * P:(c + 1) * P], ident[0:4 * HB, 0:4 * HB])
                ins.then_inc(tables_psum, 1)

            for i in range(NT):
                r = rows_of(i)
                pe.wait_ge(xn_done, i + 1)
                if i >= 2:
                    pe.wait_ge(xT_act, i - 1)
                    pe.wait_ge(xT_dve, i - 1)
                for c in range(DC):
                    ins = pe.transpose(banks(2 * (i % 2) + c // 4)[:, (c % 4) * P:(c % 4) * P + r],
                                       xn[i % 2][0:r, c * P:(c + 1) * P], ident[0:r, 0:r])
                ins.then_inc(xT_psum, 1)
                if i == 3:
                    tables()

            pe.wait_ge(xT_act, NT)
            pe.wait_ge(xT_dve, NT)
            pe.wait_ge(tables_done, 1)
            for q in range(MT):
                pe.wait_ge(w_loaded[q % 6], 16 * (q // 6 + 1))
                if q >= 2:
                    if q - 2 < NCONV:
                        if (q - 2) % 2 == 0:
                            pe.wait_ge(sig_done, (q - 2) // 2 + 1)
                        else:
                            pe.wait_ge(hx_ready, (q - 2) // 2 + 1)
                    else:
                        pe.wait_ge(z_ready, q - 2 - NCONV + 1)
                pr = banks(3 * (q % 2), 3)
                for n0 in range(0, N, 512):
                    n1 = min(n0 + 512, N)
                    for c in range(DC):
                        ins = pe.matmul(pr[:, n0:n1], win[q % 6][:, c, :], xnT[:, c, n0:n1],
                                        start=(c == 0), stop=(c == DC - 1))
                ins.then_inc(proj_done, 1)

            pe.wait_ge(const_ready, 2)
            def tail(step, dst, srcs):
                if step:
                    pe.wait_ge(tail_copied, step)
                else:
                    pe.wait_ge(last_done, ZT)
                    pe.wait_ge(hx_ready, CT)
                for j, src in enumerate(srcs):
                    ins = pe.transpose(dst[0:src.shape[1], j * P:(j + 1) * P], src, ident[:, :])
                ins.then_inc(tail_psum, 1)

            for h in range(2):
                tail(h, banks(6, 2), [lastz[:, 7 * h + t, :] for t in range(7)])
            tail(2, banks(6), [hx[:, c, SEQ:SEQ + HB] for c in range(CT)])
            for g, (b0, b1) in enumerate(TG):
                tail(3 + g, banks(7 - g % 2), [hx[:, c, HB + SEQ + b0 * SK:HB + SEQ + b1 * SK] for c in range(CT)])

            pe.wait_ge(tail_copied, 6)
            pe.wait_ge(tanh_done, 1)
            for i in range(NT):
                r = rows_of(i)
                if i >= 2:
                    pe.wait_ge(decay_sum, i - 1)
                pe.matmul(banks(6 + i % 2)[0:r, :], zs[:, WA0, i * P:i * P + r], w_da[:, :],
                          start=True, stop=True).then_inc(decay_psum, 1)
            kn = banks(0, 3)
            for hp in range(CT):
                if hp >= 1:
                    pe.wait_ge(iclr_done, hp)
                for n0 in range(0, N, 512):
                    n1 = min(n0 + 512, N)
                    ins = pe.matmul(banks(3, 3)[:, n0:n1], w_aa[:, hp * P:(hp + 1) * P], zs[:, WA0, n0:n1],
                                    start=True, stop=True)
                ins.then_inc(iclr_psum, 1)
                pe.wait_ge(ksq_done, hp + 1)
                for n0 in range(0, N, 512):
                    n1 = min(n0 + 512, N)
                    ins = pe.matmul(kn[0:8, n0:n1], head_sel[:, hp, :], ksq[:, n0:n1], start=(hp == 0),
                                    stop=(hp == CT - 1))
                ins.then_inc(knorm_part, 1)
            pe.wait_ge(knorm_done, 1)
            pe.wait_ge(iclr_done, CT)
            for hp in range(CT):
                if hp >= 2:
                    pe.wait_ge(kk_done, hp - 1)
                for n0 in range(0, N, 512):
                    n1 = min(n0 + 512, N)
                    ins = pe.matmul(banks(3 * (hp % 2), 3)[:, n0:n1], head_back[:, hp, :], knorm[:, n0:n1],
                                    start=True, stop=True)
                ins.then_inc(kback_psum, 1)

            pe.wait_ge(kk_done, CT)
            pe.wait_ge(conv_tap, 2 * CT * W)
            for n0 in range(0, N, 512):
                n1 = min(n0 + 512, N)
                for c in range(CT):
                    ins = pe.matmul(banks(0, 3)[:, n0:n1], chmean[:, :], co[:, c, n0:n1], start=(c == 0),
                                    stop=(c == CT - 1))
            ins.then_inc(cmean_psum, 1)
            for c in range(CT):
                pe.wait_ge(csq_done, c + 1)
                for n0 in range(0, N, 512):
                    n1 = min(n0 + 512, N)
                    ins = pe.matmul(banks(3, 3)[:, n0:n1], chmean[:, :], conv_sq[:, n0:n1], start=(c == 0),
                                    stop=(c == CT - 1))
                ins.then_inc(cvar_part, 1)
            pe.wait_ge(cdev_done, CT)
            pe.wait_ge(cvar_done, 1)

            def carry_waits():
                pe.sem_inc(pe_past_waits, 1)

            def cumulate(i, r, first=False):
                pe.wait_ge(c_in, i + 1)
                if not first:
                    pe.wait_ge(tok_act, 3 * i)
                    pe.wait_ge(tok_dve, 3 * i)
                for hp in range(CT):
                    if r == P:
                        ins = pe.matmul(banks(hp // 2)[:, hp % 2 * 256:hp % 2 * 256 + 256],
                                        lwst[:, hp * P:(hp + 1) * P], tri_cum[:, :, :, :].rearrange(
                                            "p e c t -> p (e c t)"), start=True, stop=True)
                    else:
                        ins = pe.matmul(banks(0)[:, hp * P:hp * P + P], lwst[0:r, hp * P:(hp + 1) * P],
                                        tri_cum8[:, :, :].rearrange("p e t -> p (e t)"), start=True, stop=True)
                ins.then_inc(c_psum, 1)

            def to_tokens(b, src, r):
                for hp in range(CT):
                    ins = pe.transpose(banks(b)[0:r, hp * P:(hp + 1) * P], src[:, hp, 0:r], ident[:, :])
                ins.then_inc(tok_psum, 1)

            def gram(b, lhs, q, done, chunks):
                carry_waits()
                for c in range(chunks):
                    t0 = c * 64
                    for hp in range(CT):
                        for p in (0, 64):
                            ins = pe.matmul(banks(b + c)[p:p + 64, hp * P:(hp + 1) * P],
                                            lhs[p:p + 64, hp, t0:t0 + 64], AR[q][p:p + 64, hp, :, t0:t0 + 64],
                                            start=True, stop=True)
                    ins.then_inc(done, 1)

            def pairs(dst, lhs, rhs):
                for hp in range(CT):
                    ins = pe.matmul(dst[:, hp * 64:hp * 64 + 64], lhs[:, hp, :], rhs[:, hp, :], start=True, stop=True)
                return ins

            def transpose_x(c):
                carry_waits()
                for hp in range(CT):
                    ins = pe.transpose(banks(4 + c)[0:64, hp * P:(hp + 1) * P], X[:, c, hp, :], ident[:, :])
                ins.then_inc(m_psum, 1)

            def prepare(i, q, r, chunks):
                pe.wait_ge(e_done, i + 1)
                to_tokens(0, vst, r)
                pe.wait_ge(prod_done, i + 1)
                to_tokens(1, bt, r)
                pe.wait_ge(prod2_done, i + 1)
                gram(2, bt, q, gb_psum, chunks)
                pe.wait_ge(tok_act, 3 * i + 1)
                if chunks == 2:
                    pe.wait_ge(tok_dve, 3 * i + 1)
                to_tokens(0, kt, r)
                for c in range(chunks):
                    pe.wait_ge(pt_done, 2 * i + c + 1)
                    for hp in range(CT):
                        ins = pe.transpose(banks(6 + c)[:, hp * P:(hp + 1) * P], PT[:, c, hp, :], ident[:, :])
                    ins.then_inc(m_psum, 1)
                pe.wait_ge(y_done, 2 * i + 1)
                pe.wait_ge(s_done, 2 * i + 1)
                gram(4, kt, q, gk_psum, chunks)

            def invert(i, chunks, levels, meanwhile=None):
                for k in range(1, levels):
                    for c in range(chunks):
                        if k == 1:
                            pe.wait_ge(m_done, MD * i + c + 1)
                            pairs(banks(6 + c), PT[:, c, :, :], MM[:, c, :, :]).then_inc(m_psum, 1)
                        else:
                            pe.wait_ge(x_done, XC * i + chunks * (k - 2) + c + 1)
                            pairs(banks(6 + c), PT[:, c, :, :], X[:, c, :, :])
                            if k == 2:
                                pe.wait_ge(gk_done, 2 * i + c + 1)
                            transpose_x(c)
                    if k == 1 and meanwhile:
                        meanwhile()
                    for c in range(chunks):
                        pe.wait_ge(m_done, MD * i + chunks * k + c + 1)
                        if k == 1:
                            pe.wait_ge(x1t_done, 2 * i + c + 1)
                        elif c == 0:
                            pe.wait_ge(xt_act, TC * i + k - 1)
                        pairs(banks(6 + c)[:, 256:512], XT[:, c, :, :], MM[:, c, :, :]).then_inc(x_psum, 1)
                for c in range(chunks):
                    pe.wait_ge(x_done, XC * i + chunks * (levels - 2) + c + 1)
                    transpose_x(c)

            def group(dst, terms, fresh=True, last=True):
                carry_waits()
                for m, (lhs, rhs) in enumerate(terms):
                    for hp in range(CT):
                        if not callable(lhs):
                            ins = pe.matmul(dst[:, hp * 64:hp * 64 + 64], lhs[:, hp, :], rhs[:, hp, :],
                                            start=(fresh and m == 0 and hp == 0),
                                            stop=(last and m == len(terms) - 1), skip_group_check=True)
                            continue
                        for p in (0, 64):
                            ins = pe.matmul(dst[p:p + 64, hp * 64:hp * 64 + 64], lhs(p, hp), rhs(p, hp),
                                            start=(fresh and m == 0 and hp == 0),
                                            stop=(last and m == len(terms) - 1), skip_group_check=True)
                return ins

            def chain(i, q, c):
                n = 2 * i + c
                t0 = c * 64
                if c == 0:
                    pe.wait_ge(tok_act, 3 * i + 3)
                    pe.wait_ge(gb_done, 2 * i + 2)
                    pe.wait_ge(gk_done, 2 * i + 2)
                else:
                    pe.wait_ge(tok_dve, 3 * i + 3)
                pe.wait_ge(s_done, n + 1)
                S = ST0
                group(banks(2), [
                    (GK0[c], vtok[:, c, :, :]),
                    (lambda p, hp: AR[q][p:p + 64, hp, 0, t0:t0 + 64], lambda p, hp: S[p:p + 64, hp, :]),
                ]).then_inc(rhs_psum, 1)
                if c:
                    pe.wait_ge(y_done, n + 1)
                else:
                    pe.wait_ge(xt_act, TC * i + TC)
                    pe.wait_ge(m_done, MD * i + MD)
                group(banks(4), [
                    (lambda p, hp: S[p:p + 64, hp, :], lambda p, hp: AR[q][p:p + 64, hp, 1, t0:t0 + 64]),
                    (lambda p, hp: vtok[p:p + 64, c, hp, :], lambda p, hp: GK1[p:p + 64, c, hp, :]),
                ], last=False)
                pe.wait_ge(rhs_done, n + 1)
                pairs(banks(3), XT[:, c, :, :], RHS).then_inc(u_psum, 1)
                group(banks(5), [(ktok[c], vtok[:, c, :, :])],
                      last=False)
                pe.wait_ge(u_done, n + 1)
                group(banks(5), [(btok[c], UU)],
                      fresh=False).then_inc(s_psum, 1)
                pe.wait_ge(ub_done, n + 1)
                group(banks(4), [(UB, GB[:, c, :, 1, :])], fresh=False).then_inc(y_psum, 1)

            def pe_turn(i, q, next_r):
                prepare(i, q, P, 2)
                invert(i, 2, LV, lambda: cumulate(i + 1, next_r))
                for c in range(2):
                    chain(i, q, c)

            cumulate(0, P, first=True)
            rwkv_turns(pe, pe_turn)

            pe.wait_ge(e_done, NT)
            pe.wait_ge(s_done, 2 * (NT - 1) + 1)
            pe.wait_ge(tok_act, 3 * (NT - 1))
            pe.wait_ge(tok_dve, 3 * (NT - 1))
            for hp in range(CT):
                ins = pe.transpose(banks(0)[0:64, hp * P:(hp + 1) * P], ST0[:, hp, :], ident[:, :])
            ins.then_inc(fin_psum, 1)
            pe.wait_ge(s_loaded, 32 * CT)
            for hp in range(CT):
                if hp == 3:
                    pe.wait_ge(s8_in, 1)
                for b in range(SB):
                    ins = pe.transpose(banks(S_IN[hp])[:, b * 64:b * 64 + 64], s_raw[hp][:, b, :], ident[0:64, 0:64])
                ins.then_inc(s8_psum, 1)
            pe.wait_ge(fin_copied, 1)
            i8, n8 = NT - 1, 2 * (NT - 1)
            prepare(i8, 0, NS, 1)
            invert(i8, 1, LV8)
            pe.wait_ge(tok_act, 3 * i8 + 3)
            pe.wait_ge(gb_done, n8 + 1)
            pe.wait_ge(gk_done, n8 + 1)
            pe.wait_ge(s8_in, CT)
            pe.wait_ge(a8_done, CT)
            for hp in range(CT):
                rhs = banks(2)[:, hp * 64:hp * 64 + 64]
                pe.matmul(rhs, GK0[0][:, hp, :], vtok[:, 0, hp, :], start=(hp == 0), stop=False, skip_group_check=True)
                for b in range(SB):
                    for p in (0, 64):
                        ins = pe.matmul(rhs[p:p + 64, :], A8[hp][p:p + 64, b, :], S8[hp][p:p + 64, b, :], start=False,
                                        stop=(b == SB - 1), skip_group_check=True)
            ins.then_inc(rhs_psum, 1)
            pe.wait_ge(xt_act, TC * i8 + LV8 - 1)
            for hp in range(CT):
                for p in (0, 64):
                    y = banks(4)[p:p + 64, hp * 64:hp * 64 + 64]
                    pe.matmul(y, vtok[p:p + 64, 0, hp, :], GK1[p:p + 64, 0, hp, :], start=(hp == 0), stop=False,
                              skip_group_check=True)
                    for b in range(SB):
                        pe.matmul(y[:, b * ST:(b + 1) * ST], S8[hp][p:p + 64, b, :],
                                  AR[0][p:p + 64, hp, 1, b * ST:(b + 1) * ST], start=False, stop=False,
                                  skip_group_check=True)
            pe.wait_ge(rhs_done, n8 + 1)
            pairs(banks(3), XT[:, 0, :, :], RHS).then_inc(u_psum, 1)
            pe.wait_ge(u_done, n8 + 1)
            pe.wait_ge(ub_done, n8 + 1)
            for hp in range(CT):
                ins = pe.matmul(banks(4)[:, hp * 64:hp * 64 + 64], UB[:, hp, :], GB[:, 0, hp, 1, :], start=False,
                                stop=(hp == CT - 1), skip_group_check=True)
            ins.then_inc(y_psum, 1)

            def new_states(hp):
                pe.wait_ge(uv8_done, hp + 1)
                if hp == 3:
                    pe.wait_ge(s8_done, 1)
                pe.matmul(banks(S_NEW[hp]), btok[0][:, hp, :], U8[hp % 2].rearrange("p b n -> p (b n)"), start=True,
                          stop=False)
                pe.matmul(banks(S_NEW[hp]), ktok[0][:, hp, :], V8[hp % 2].rearrange("p b n -> p (b n)"), start=False,
                          stop=True).then_inc(s_psum, 1)

            def states_back(hp):
                pe.wait_ge(s8_done, hp + 1)
                if hp >= 2:
                    pe.wait_ge(fin_copied, hp)
                for b in range(SB):
                    ins = pe.transpose(banks(S_OUT[hp] + b // 4)[0:64, b % 4 * P:(b % 4 + 1) * P], S8[hp][:, b, :],
                                       ident[:, :])
                ins.then_inc(fin_psum, 1)

            for hp in range(CT):
                new_states(hp)
                if hp:
                    states_back(hp - 1)
            states_back(CT - 1)

            pe.wait_ge(fin_copied, CT + 1)
            pe.wait_ge(y_done, 2 * (NT - 1) + 2)
            pe.wait_ge(s8_done, CT)

            def over_tokens(dst, lhs, hp, src=None, **flags):
                for n0 in range(0, N, 512):
                    n1 = min(n0 + 512, N)
                    if src is not None:
                        rhs = src[:, n0:n1]
                    elif n1 < N:
                        rhs = yT[:, n0 // P:n1 // P, hp, :]
                    else:
                        rhs = yT[:, NT - 1, hp, 0:NS]
                    ins = pe.matmul(dst[:, n0:n1], lhs, rhs, **flags)
                return ins

            for hp in range(CT):
                if hp:
                    pe.wait_ge(gdev_done, hp)
                over_tokens(banks(0, 3), headmean[:, :], hp, start=True, stop=True).then_inc(gmean_psum, 1)
                pe.wait_ge(gsq_done, hp + 1)
                over_tokens(banks(3, 3)[0:8, :], head_sel[:, hp, :], hp, gn_sq, start=(hp == 0),
                            stop=(hp == CT - 1)).then_inc(gvar_part, 1)
            pe.wait_ge(grstd_done, 1)
            for hp in range(CT):
                if hp:
                    pe.wait_ge(gback_used, hp)
                over_tokens(banks(0, 3), head_back[:, hp, :], hp, gn_rstd, start=True, stop=True)\
                    .then_inc(gback_psum, 1)
                pe.wait_ge(rk_done, hp + 1)
                if hp:
                    pe.wait_ge(mix_done, hp)
                over_tokens(banks(3, 3), headsum[:, :], hp, gn_bonus, start=True, stop=True).then_inc(rk_psum, 1)
                pe.wait_ge(rk_used, hp + 1)
                over_tokens(banks(3, 3), w_g[:, hp * P:(hp + 1) * P], hp, zs[:, GL0, :], start=True, stop=True)\
                    .then_inc(gate_psum, 1)
            pe.wait_ge(mix_done, CT)
            pe.wait_ge(tables2_in, 16 * 6)

            def project(i):
                r = rows_of(i)
                if i >= 2:
                    pe.wait_ge(h_done, i - 1)
                for half in range(2):
                    for c in range(2 * CT):
                        lhs = co[:, c, i * P:i * P + r] if c < CT else yT[:, i, c - CT, 0:r]
                        ins = pe.matmul(banks(2 * (i % 2) + half)[0:r, :], lhs, wout[:, c, half * 512:half * 512 + 512],
                                        start=(c == 0), stop=(c == 2 * CT - 1))
                ins.then_inc(o_psum, 1)

            def route(i):
                r = rows_of(i)
                pe.wait_ge(xn2_done, i + 1)
                if i:
                    pe.wait_ge(xT_act, NT + i)
                    pe.wait_ge(xT_dve, NT + i)
                for c in range(DC):
                    ins = pe.transpose(banks(4 + c // 4)[:, (c % 4) * P:(c % 4) * P + r],
                                       xn2[i % 2][0:r, c * P:(c + 1) * P], ident[0:r, 0:r])
                ins.then_inc(xT_psum, 1)

            def logits(i):
                r = rows_of(i)
                pe.wait_ge(xT_act, NT + i + 1)
                pe.wait_ge(xT_dve, NT + i + 1)
                if i:
                    pe.wait_ge(lg_done, i)
                for c in range(DC):
                    ins = pe.matmul(banks(6)[0:r, 0:NG + NE], x2T[i % 2][:, c, 0:r], w_rt[:, c, :], start=(c == 0),
                                    stop=(c == DC - 1))
                ins.then_inc(lg_psum, 1)

            for i in range(NT):
                project(i)
                if i:
                    route(i - 1)
                if i >= 2:
                    logits(i - 2)
            route(NT - 1)
            logits(NT - 2)
            logits(NT - 1)

            pe.wait_ge(cum_done, 1)
            rk = banks(7)
            pe.matmul(rk[:, 0:(NT + 1) * NE], ones[:, :], r_cum.rearrange("p i e -> p (i e)"), start=True, stop=False,
                      skip_group_check=True)
            pe.matmul(rk[:, 0:NT * NE], before[:, :], r_m.rearrange("p i e -> p (i e)"), start=False, stop=True,
                      skip_group_check=True).then_inc(rank_psum, 1)
            for k in range(TOPK):
                pe.wait_ge(onehot_done, k + 1)
                for i in range(NT):
                    r = rows_of(i)
                    ins = pe.matmul(banks(6)[:, 0:2 * NCOL], r_os[k][0:r, i, :], r_ot[k][0:r, i, :, :].rearrange(
                        "p a n -> p (a n)"), start=(k + i == 0), stop=(k + i == TOPK + NT - 2))
            ins.then_inc(onehot_used, 1)

            def transpose_rows(u, turn, v):
                pe.wait_ge(xg_in[v % UN], 16 * (turn + v // UN) + 16)
                for c in range(DC):
                    ins = pe.transpose(banks(2 + c // 4)[:, (c % 4) * P:(c % 4 + 1) * P],
                                       xg[v % UN][:, c * P:(c + 1) * P], ident[:, :])
                ins.then_inc(xT_psum, 1)

            def gate_up(u, turn, v):
                pe.wait_ge(xT_act, 2 * NT + u + 1)
                pe.wait_ge(xT_dve, 2 * NT + u + 1)
                pe.wait_ge(wx_in[v % UN], 48 * (turn + v // UN) + 48 + wx_0[v % UN])
                wgu = wx[v % UN][:, 0:2 * DC * F].rearrange("p (w c f) -> p w c f", w=2, c=DC)
                for c in range(DC):
                    ins = pe.matmul(banks(v % 2), xgT[v % 2][:, c, :], wgu[:, :, c, :], start=(c == 0),
                                    stop=(c == DC - 1))
                ins.then_inc(gu_psum, 1)

            def pe_step(turn, s, ahead):
                u = UN * turn + s
                if ahead >= 1:
                    gate_up(u + 1, turn, s + 1)
                pe.wait_ge(hx_done, u + 1)
                for c in range(2):
                    ins = pe.transpose(banks(4)[:, c * P:(c + 1) * P], gu[:, c * P:(c + 1) * P], ident[:, :])
                ins.then_inc(ht_psum, 1)
                if ahead >= 2:
                    transpose_rows(u + 2, turn, s + 2)
                pe.wait_ge(ht_done, u + 1)
                pe.wait_ge(ye_act, u)
                pe.wait_ge(ye_dve, u)
                wd = wx[s][:, 2 * DC * F:].rearrange("p (c n) -> p c n", c=2)
                for half in range(2):
                    for c in range(2):
                        ins = pe.matmul(banks(5 + half), hT[:, c, :], wd[:, c, half * 512:half * 512 + 512],
                                        start=(c == 0), stop=(c == 1))
                ins.then_inc(yd_psum, 1)

            transpose_rows(0, 0, 0)
            gate_up(0, 0, 0)
            transpose_rows(1, 0, 1)
            expert_turns(pe, pe_step)

        @block.vector
        def _(dve):
            step = [0]

            def link(ins):
                step[0] += 1
                ins.then_inc(dve_chain, 1)
                dve.wait_ge(dve_chain, step[0])

            dve.memset(stat[:, 7, :], 0.0)
            dve.memset(hx[:, :, 0:HB], 0.0)
            def mean_square(i):
                r = rows_of(i)
                dve.wait_ge(sq_done, i + 1)
                dve.tensor_scalar(stat[0:r, 1, i:i + 1], stat[0:r, 0, i:i + 1], 1.0 / D, RMS_EPS, ALU.mult, ALU.add)\
                    .then_inc(ms_done, 1)

            def scale(i):
                r = rows_of(i)
                dve.wait_ge(std_done, i + 1)
                link(dve.reciprocal(stat[0:r, 3, i:i + 1], stat[0:r, 2, i:i + 1]))
                if i == 0:
                    dve.wait_ge(gain1_in, 16)
                if i >= 2:
                    dve.wait_ge(xT_psum, i - 1)
                dve.scalar_tensor_tensor(out=xn[i % 2][0:r, :], in0=x_in[i % 3][0:r, :],
                                         scalar=stat[0:r, 3, i:i + 1], in1=gain[0:r, :], op0=ALU.mult,
                                         op1=ALU.mult).then_inc(xn_done, 1)

            def copy_T(i):
                dve.wait_ge(xT_psum, i + 1)
                r = rows_of(i)
                dve.tensor_copy(xnT[:, 4:8, i * P:i * P + r],
                                banks(2 * (i % 2) + 1).rearrange("p (c n) -> p c n", c=4)[:, :, 0:r])\
                    .then_inc(xT_dve, 1)

            mean_square(0)
            for i in range(NT):
                if i + 1 < NT:
                    mean_square(i + 1)
                scale(i)
                if i >= 1:
                    copy_T(i - 1)
                if i == 5:
                    dve.wait_ge(tables_psum, 1)
                    tb = banks(6)
                    dve.tensor_copy(prm[:, :], tb[:, 0:NPR])
                    dve.tensor_copy(cw[:, :, :].rearrange("p k c -> p (k c)"), tb[:, 64:64 + W * CT])
                    dve.tensor_copy(shift0[:, :, :].rearrange("p t b -> p (t b)"), tb[:, 192:192 + ZT * SB])
                    for h in range(2):
                        for c in range(CT):
                            ins = dve.tensor_copy(
                                hx[:, c, HB + SEQ:].rearrange("p (b k) -> p b k", b=SB)[:, 4 * h:4 * h + 4, 0:HB],
                                banks(4 + h)[:, c * 4 * HB:(c + 1) * 4 * HB].rearrange("p (b k) -> p b k", b=4))
                    link(ins)
                    dve.tensor_scalar(om_ka[:, :], prm[:, PR["k_a"][0]:PR["k_a"][0] + CT], -1.0, 1.0,
                                      ALU.mult, ALU.add).then_inc(tables_done, 1)
            copy_T(NT - 1)
            dve.wait_ge(const_ready, 2)
            for m in (mask_ar, mask_ar8, mask_lv, mask_lv0t, rowmask):
                flat = m[:, :] if len(m.shape) == 2 else m[:, :, :].rearrange("p a b -> p (a b)")
                dve.tensor_copy(flat[64:128, :], flat[0:64, :])

            taps = [(c, k) for c in range(CT) for k in range(W)]
            done = [0]

            def conv(n):
                for _ in range(n):
                    if done[0] == len(taps):
                        return
                    j = done[0]
                    c, k = taps[j]
                    w = cw[:, k, c:c + 1]
                    src_p = hx[:, c, k:k + SEQ]
                    src_s = hx[:, c, HB + SEQ:].rearrange("p (b k) -> p b k", b=SB)[:, :, k:k + ST]
                    dst_p, dst_s = co[:, c, 0:SEQ], co[:, c, SEQ:N].rearrange("p (b t) -> p b t", b=SB)
                    for m, (dst, src) in enumerate(((dst_p, src_p), (dst_s, src_s))):
                        if k == 0:
                            bias = prm[:, PR["conv_b"][0] + c:PR["conv_b"][0] + c + 1]
                            dve.tensor_scalar(dst, src, w, bias, ALU.mult, ALU.add).then_inc(conv_tap, 1)
                        else:
                            dve.wait_ge(conv_tap, 2 * j + m - 1)
                            dve.scalar_tensor_tensor(out=dst, in0=src, scalar=w, in1=dst, op0=ALU.mult,
                                                     op1=ALU.add).then_inc(conv_tap, 1)
                    done[0] += 1

            for q, t in enumerate(ORDER):
                pr = banks(3 * (q % 2), 3)
                if q < NCONV:
                    if q % 2 == 1:
                        c = q // 2
                        dve.wait_ge(proj_done, q + 1)
                        dve.wait_ge(sig_done, c + 1)
                        dve.tensor_tensor(hx[:, c, HB:HB + SEQ], pr[:, 0:SEQ], sig[:, 0:SEQ], ALU.mult)
                        dve.tensor_tensor(hx[:, c, HB + SEQ:].rearrange("p (b k) -> p b k", b=SB)[:, :, HB:],
                                          pr[:, SEQ:N].rearrange("p (b t) -> p b t", b=SB),
                                          sig[:, SEQ:N].rearrange("p (b t) -> p b t", b=SB), ALU.mult)\
                            .then_inc(hx_ready, 1)
                        dve.wait_ge(hx_ready, c + 1)
                        conv(6)
                    continue
                j = q - NCONV
                zb = zbuf[j % 2]
                dve.wait_ge(z_ready, j + 1)
                if j >= 1:
                    dve.wait_ge(zs_done, j)
                dve.tensor_tensor(zd[:, 0:SEQ], zb[:, 0:SEQ], zb[:, 1:1 + SEQ], ALU.subtract)
                zsm = zb[:, 1 + SEQ:].rearrange("p (b t) -> p b t", b=SB)
                link(dve.tensor_tensor(zd[:, SEQ:N].rearrange("p (b t) -> p b t", b=SB), zsm[:, :, 0:ST],
                                       zsm[:, :, 1:], ALU.subtract))
                mu = prm[:, PR["mu"][0] + t - 8:PR["mu"][0] + t - 7]
                dve.scalar_tensor_tensor(out=zs[:, t - 8, 0:SEQ], in0=zd[:, 0:SEQ], scalar=mu, in1=zb[:, 1:1 + SEQ],
                                         op0=ALU.mult, op1=ALU.add)
                dve.scalar_tensor_tensor(out=zs[:, t - 8, SEQ:N].rearrange("p (b t) -> p b t", b=SB),
                                         in0=zd[:, SEQ:N].rearrange("p (b t) -> p b t", b=SB), scalar=mu,
                                         in1=zsm[:, :, 1:], op0=ALU.mult, op1=ALU.add).then_inc(zs_done, 1)
                dve.wait_ge(zs_done, j + 1)
                conv(8)
            conv(len(taps))
            for i in range(NT):
                r = rows_of(i)
                dve.wait_ge(decay_psum, i + 1)
                dve.tensor_tensor(sgw[0:r, i, :], banks(6 + i % 2)[0:r, :], w0_all[0:r, :], ALU.add)\
                    .then_inc(decay_sum, 1)
            dve.wait_ge(tails_out, 16 * (3 + SB))
            for hp in range(CT):
                def col(name):
                    c0 = PR[name][0] + hp
                    return prm[:, c0:c0 + 1]

                dve.tensor_scalar(nkk[:, hp, :], zs[:, K0 + hp, :], col("k_k"), None, ALU.mult).then_inc(kkr_done, 1)
                dve.wait_ge(iclr_done, hp + 1)
                dve.tensor_scalar(kmul, iclr[hp % 2], col("k_a"), om_ka[:, hp:hp + 1], ALU.mult, ALU.add)\
                    .then_inc(dve_chain, 1)
                step[0] += 1
                dve.wait_ge(kkr_done, hp + 1)
                dve.tensor_tensor(kka[:, hp, :], nkk[:, hp, :], iclr[hp % 2], ALU.mult)
                dve.wait_ge(dve_chain, step[0])
                dve.tensor_tensor(zs[:, K0 + hp, :], zs[:, K0 + hp, :], kmul, ALU.mult).then_inc(kprep_done, 1)
                dve.wait_ge(kprep_done, hp + 1)
            dve.wait_ge(knorm_root, 1)
            link(dve.tensor_scalar(knorm[0:8, :], knorm[0:8, :], 1e-12, None, ALU.max))
            dve.reciprocal(knorm[0:8, :], knorm[0:8, :]).then_inc(knorm_done, 1)
            for hp in range(CT):
                dve.wait_ge(kback_psum, hp + 1)
                kb = banks(3 * (hp % 2), 3)[:, 0:N]
                dve.tensor_tensor(kka[:, hp, :], kka[:, hp, :], kb, ALU.mult)
                dve.scalar_tensor_tensor(out=nkk[:, hp, :], in0=nkk[:, hp, :], scalar=-1.0, in1=kb, op0=ALU.mult,
                                         op1=ALU.mult).then_inc(kk_done, 1)
            dve.wait_ge(cmean_psum, 1)
            dve.wait_ge(kprep_done, CT)
            for c in range(CT):
                dve.tensor_tensor(co[:, c, :], co[:, c, :], banks(0, 3)[:, 0:N], ALU.subtract).then_inc(cdev_done, 1)
            dve.wait_ge(cvar_part, CT)
            var = banks(3, 3)[:, 0:N]
            for v, src in zip(conv_rstd, (var[:, 0:SEQ], var[:, SEQ:N])):
                ins = dve.tensor_scalar(v, src, LN_EPS, None, ALU.add)
            ins.then_inc(cvar_done, 1)
            def scaled_a(i, q, r):
                dve.wait_ge(e_done, i + 1)
                dve.tensor_tensor(AR[q][:, :, 0, 0:r], nkk[:, :, bass.ds(i * P, r)], e_ex[:, :, 0:r], ALU.mult)

            def scaled_b(i, r):
                dve.tensor_tensor(bt[:, :, 0:r], kka[:, :, bass.ds(i * P, r)], e_neg[:, :, 0:r], ALU.mult)\
                    .then_inc(prod_done, 1)

            def tok_copy(i, j, dst, b):
                dve.wait_ge(tok_psum, 3 * i + j + 1)
                src = banks(b).rearrange("p (h n) -> p h n", h=CT)
                dve.tensor_copy(token_rows(dst, 1, 0), src[64:128, :, 0:64])
                dve.tensor_copy(token_rows(dst, 1, 64), src[64:128, :, 64:128]).then_inc(tok_dve, 1)

            def masked(n, c, b, dst, psum_sem, done, mask):
                dve.wait_ge(psum_sem, n + 1)
                dve.tensor_tensor(dst[:, c, :, :, :].rearrange("p h e n -> p h (e n)"),
                                  banks(b + c).rearrange("p (h n) -> p h n", h=CT),
                                  mask[:, :, :].rearrange("p e n -> p (e n)").unsqueeze(1).broadcast_to([P, CT, P]),
                                  ALU.mult).then_inc(done, 1)

            def masked_k(n, c, mask):
                dve.wait_ge(gk_psum, n + 1)
                src = banks(4 + c).rearrange("p (h e n) -> p h e n", h=CT, e=2)
                for p in (0, 64):
                    dve.tensor_tensor(GK0[c][p:p + 64, :, p:p + 64], src[p:p + 64, :, 0, :],
                                      mask[p:p + 64, 0, :].unsqueeze(1).broadcast_to([64, CT, 64]), ALU.mult)
                dve.tensor_tensor(GK1[:, c, :, :], src[:, :, 1, :],
                                  mask[:, 1, :].unsqueeze(1).broadcast_to([P, CT, 64]), ALU.mult).then_inc(gk_done, 1)

            def plus_identity(n, c):
                dve.wait_ge(gb_done, n + 1)
                for p in (0, 64):
                    ins = dve.tensor_tensor(PT[p:p + 64, c, :, p:p + 64], GB[p:p + 64, c, :, 0, :],
                                            ident[p:p + 64, p:p + 64].unsqueeze(1).broadcast_to([64, CT, 64]),
                                            ALU.add)
                ins.then_inc(pt_done, 1)

            def xt_copy():
                src = banks(5)[0:64, :].rearrange("p (h n) -> p h n", h=CT)
                dve.tensor_copy(XT[0:64, 1, :, 0:64], src[:, :, 0:64])
                return dve.tensor_copy(XT[64:128, 1, :, 64:128], src[:, :, 64:128])

            def level_mask(m, k, c):
                dve.wait_ge(m_psum, m + 1)
                if k == 0:
                    for p in (0, 64):
                        ins = dve.tensor_tensor(MM[p:p + 64, c, :, :], banks(6 + c)[p:p + 64, :].rearrange(
                            "p (h n) -> p h n", h=CT)[:, :, p:p + 64],
                            mask_lv[p:p + 64, k, :].unsqueeze(1).broadcast_to([64, CT, 64]), ALU.mult)
                else:
                    ins = dve.tensor_tensor(MM[:, c, :, :], banks(6 + c)[:, 0:CT * 64].rearrange(
                        "p (h n) -> p h n", h=CT), mask_lv[:, k, :].unsqueeze(1).broadcast_to([P, CT, 64]), ALU.mult)
                if k >= 2 and c == 1:
                    ins = xt_copy()
                ins.then_inc(m_done, 1)

            def last_xt(m):
                dve.wait_ge(m_psum, m + 1)
                xt_copy().then_inc(m_done, 1)

            def u_copy(n):
                dve.wait_ge(u_psum, n + 1)
                u = banks(3)[:, 0:CT * 64].rearrange("p (h n) -> p h n", h=CT)
                dve.tensor_copy(UU, u).then_inc(u_done, 1)
                for p in (0, 64):
                    ins = dve.tensor_copy(UB[p:p + 64, :, p:p + 64], u[p:p + 64, :, :])
                ins.then_inc(ub_done, 1)

            def new_state(n, q, c):
                dve.wait_ge(s_psum, n + 1)
                dve.tensor_tensor(ST0, banks(5)[:, 0:CT * 64].rearrange("p (h n) -> p h n", h=CT), ST0, ALU.add)\
                    .then_inc(s_sum, 1)
                dve.wait_ge(s_sum, n + 1)
                dve.tensor_tensor(ST0, ST0, e_in[q][:, :, c * 64 + 63:c * 64 + 64].broadcast_to([P, CT, 64]), ALU.mult)\
                    .then_inc(s_done, 1)

            dve.wait_ge(cstd_done, 1)
            dve.sem_inc(ln_done, 1)

            def conv_norm(i, r, s):
                if s:
                    dve.wait_ge(ln_step, 4 * i + s)
                v = conv_tile(i, r)
                rstd = conv_rstd[0][:, bass.ds(i * P, P)] if r == P else conv_rstd[1]
                g0, b0 = PR["ln_g"][0], PR["ln_b"][0]
                if s == 0:
                    ins = dve.reciprocal(rstd, rstd)
                elif s == 1:
                    ins = dve.tensor_tensor(v, v, rstd.unsqueeze(1).broadcast_to([P, CT, r]), ALU.mult)
                elif s == 2:
                    ins = dve.tensor_tensor(v, v, prm[:, g0:g0 + CT].unsqueeze(2).broadcast_to([P, CT, r]), ALU.mult)
                else:
                    ins = dve.tensor_tensor(v, v, prm[:, b0:b0 + CT].unsqueeze(2).broadcast_to([P, CT, r]), ALU.add)
                ins.then_inc(ln_step, 1)

            def conv_swish(i, r):
                dve.wait_ge(ln_sig, i + 1)
                v = conv_tile(i, r)
                dve.tensor_tensor(v, v, conv_sig[:, :, 0:r], ALU.mult).then_inc(ln_done, 1)

            def dve_turn(i, q, next_r):
                tok_copy(i, 0, vtok, 0)
                tok_copy(i, 1, btok, 1)
                for c in range(2):
                    masked(2 * i + c, c, 2, GB, gb_psum, gb_done, mask_ar)
                    plus_identity(2 * i + c, c)
                for c in range(2):
                    level_mask(MC * i + c, 0, c)
                tok_copy(i, 2, ktok, 0)
                for c in range(2):
                    masked_k(2 * i + c, c, mask_ar)
                for k in range(1, LV):
                    for c in range(2):
                        level_mask(MC * i + 2 * k + c, k, c)
                    if k <= 4:
                        conv_norm(i, P, k - 1)
                last_xt(MC * i + 2 * LV + 1)
                scaled_a(i + 1, 1 - q, next_r)
                scaled_b(i + 1, next_r)
                for c in range(2):
                    u_copy(2 * i + c)
                    new_state(2 * i + c, q, c)
                    if c == 0:
                        conv_swish(i, P)

            scaled_a(0, 0, P)
            scaled_b(0, P)
            rwkv_turns(dve, dve_turn)

            i8, n8 = NT - 1, 2 * (NT - 1)
            for hp in range(CT):
                dve.tensor_tensor(A8[hp], AR[0][:, hp, 0, 0:64].unsqueeze(1).broadcast_to([P, SB, 64]),
                                  seqmask[:, :, :], ALU.mult).then_inc(a8_done, 1)
            masked(n8, 0, 2, GB, gb_psum, gb_done, mask_ar8)
            plus_identity(n8, 0)
            level_mask(MC * i8, 0, 0)
            masked_k(n8, 0, mask_ar8)
            for k in range(LV8):
                if k:
                    level_mask(MC * i8 + k, k, 0)
                conv_norm(i8, NS, k)
            conv_norm(i8, NS, LV8)
            u_copy(n8)
            dve.wait_ge(u_done, n8 + 1)
            dve.wait_ge(tok_act, 3 * NT)

            def u_v_rows(hp):
                if hp >= 2:
                    dve.wait_ge(s_psum, n8 + hp - 1)
                rows = rowmask[:, :].unsqueeze(2).broadcast_to([P, SB, 64])
                dve.tensor_tensor(U8[hp % 2], UU[:, hp, :].unsqueeze(1).broadcast_to([P, SB, 64]), rows, ALU.mult)
                dve.tensor_tensor(V8[hp % 2], vtok[:, 0, hp, :].unsqueeze(1).broadcast_to([P, SB, 64]), rows, ALU.mult)\
                    .then_inc(uv8_done, 1)

            def sample_state(hp):
                dve.wait_ge(s_psum, n8 + hp + 1)
                link(dve.tensor_tensor(S8[hp], banks(S_NEW[hp]).rearrange("p (b n) -> p b n", b=SB), S8[hp], ALU.add))
                dve.tensor_tensor(S8[hp], S8[hp], e_in[0][:, hp, 0:64].rearrange("p (b t) -> p b t", b=SB)[:, :, ST - 1]
                                  .unsqueeze(2).broadcast_to([P, SB, 64]), ALU.mult).then_inc(s8_done, 1)

            u_v_rows(0)
            for hp in range(CT):
                if hp + 1 < CT:
                    u_v_rows(hp + 1)
                sample_state(hp)
            conv_swish(i8, NS)
            for hp in range(CT):
                dve.wait_ge(gmean_psum, hp + 1)
                for y3, mean in pieces(yT, banks(0, 3)[:, 0:N], hp):
                    ins = dve.tensor_tensor(y3, y3, mean, ALU.subtract)
                ins.then_inc(gdev_done, 1)
            link(dve.memset(gn_rstd, 0.0))
            dve.wait_ge(gvar_part, CT)
            dve.tensor_scalar(gn_rstd[0:8, :], banks(3, 3)[0:8, 0:N], 1.0 / HD, GN_EPS, ALU.mult, ALU.add)\
                .then_inc(gvar_done, 1)
            dve.wait_ge(gstd_done, 1)
            dve.reciprocal(gn_rstd[0:8, :], gn_rstd[0:8, :]).then_inc(grstd_done, 1)
            for hp in range(CT):
                def col(name):
                    c0 = PR[name][0] + hp
                    return prm[:, c0:c0 + 1]

                if hp:
                    dve.wait_ge(mix_done, hp)
                dve.scalar_tensor_tensor(out=gn_bonus, in0=zs[:, R0 + hp, :], scalar=col("r_k"),
                                         in1=zs[:, K0 + hp, :], op0=ALU.mult, op1=ALU.mult).then_inc(rk_done, 1)
                dve.wait_ge(gback_psum, hp + 1)
                for y3, rstd in pieces(yT, banks(0, 3)[:, 0:N], hp):
                    ins = dve.tensor_tensor(y3, y3, rstd, ALU.mult)
                ins.then_inc(gback_used, 1)
                dve.wait_ge(gback_used, hp + 1)
                for y3, _ in pieces(yT, gn_bonus, hp):
                    ins = dve.tensor_scalar(y3, y3, col("gn_g"), col("gn_b"), ALU.mult, ALU.add)
                dve.wait_ge(rk_psum, hp + 1)
                link(ins)
                dve.tensor_tensor(gn_bonus, banks(3, 3)[:, 0:N], zs[:, V0 + hp, :], ALU.mult).then_inc(rk_used, 1)
                dve.wait_ge(rk_used, hp + 1)
                for y3, bonus in pieces(yT, gn_bonus, hp):
                    ins = dve.tensor_tensor(y3, y3, bonus, ALU.add)
                link(ins)
                dve.wait_ge(gate_psum, hp + 1)
                for y3, gate in pieces(yT, banks(3, 3)[:, 0:N], hp):
                    ins = dve.tensor_tensor(y3, y3, gate, ALU.mult)
                ins.then_inc(mix_done, 1)
            link(dve.memset(lg, 0.0))

            def residual(i):
                r = rows_of(i)
                dve.wait_ge(o_psum, i + 1)
                dve.wait_ge(x_loaded[i % 3], 16 * (NT // 3 + i // 3 + 1))
                dve.tensor_tensor(hres[0:r, i, :], banks(2 * (i % 2), 2)[0:r, :], xres[i % 3][0:r, :], ALU.add)\
                    .then_inc(h_done, 1)

            def norm2(i):
                r = rows_of(i)
                dve.wait_ge(sq_done, NT + i + 1)
                dve.tensor_scalar(stat[0:r, 5, i:i + 1], stat[0:r, 4, i:i + 1], 1.0 / D, RMS_EPS, ALU.mult, ALU.add)\
                    .then_inc(ms_done, 1)
                dve.wait_ge(std_done, NT + i + 1)
                link(dve.reciprocal(stat[0:r, 6, i:i + 1], stat[0:r, 6, i:i + 1]))
                if i == 0:
                    dve.wait_ge(tables2_in, 16 * 6)
                if i >= 2:
                    dve.wait_ge(xT_psum, NT + i - 1)
                    dve.wait_ge(xn2_stored[i % 2], 16 * (i // 2))
                dve.scalar_tensor_tensor(out=xn2[i % 2][0:r, :].rearrange("q (c p) -> q p c", c=DC),
                                         in0=hres[0:r, i, :].rearrange("q (p c) -> q p c", c=DC),
                                         scalar=stat[0:r, 6, i:i + 1],
                                         in1=gain[0:r, :].rearrange("q (p c) -> q p c", c=DC), op0=ALU.mult,
                                         op1=ALU.mult).then_inc(xn2_done, 1)

            def copy_T2(i):
                r = rows_of(i)
                dve.wait_ge(xT_psum, NT + i + 1)
                if i >= 2:
                    dve.wait_ge(lg_psum, i - 1)
                dve.tensor_copy(x2T[i % 2][:, 4:8, 0:r], banks(5).rearrange("p (c n) -> p c n", c=4)[:, :, 0:r])\
                    .then_inc(xT_dve, 1)

            def add_bias(i):
                r = rows_of(i)
                dve.wait_ge(lg_psum, i + 1)
                dve.tensor_tensor(lg[0:r, i, :], banks(6)[0:r, 0:NG + NE], b_rt[0:r, :], ALU.add).then_inc(lg_done, 1)

            for i in range(NT):
                residual(i)
                norm2(i)
                if i:
                    copy_T2(i - 1)
                if i >= 2:
                    add_bias(i - 2)
            copy_T2(NT - 1)
            add_bias(NT - 2)
            add_bias(NT - 1)

            def TT(out, a, b, op):
                link(dve.tensor_tensor(out, a, b, op))

            def TS(out, a, s1, s2, op0, op1=ALU.bypass):
                link(dve.tensor_scalar(out, a, s1, s2, op0, op1))

            def RED(out, a, op):
                link(dve.tensor_reduce(out, a, AX.X, op))

            def last_dim(v, n):
                return v.unsqueeze(len(v.shape)).broadcast_to([*v.shape, n])

            def first(out, values, top, n, key):
                TT(key, values, last_dim(top, n), ALU.is_equal)
                TT(key, key, r_desc[:, EG - n:].unsqueeze(1).broadcast_to([P, NT, n]), ALU.mult)
                RED(r_km, key, ALU.max)
                TT(out, key, last_dim(r_km, n), ALU.is_equal)

            dve.wait_ge(lg_done, NT)
            dve.wait_ge(iota_done, 1)
            gl, el = lg[:, :, 0:NG], lg[:, :, NG:]
            RED(r_gmax, gl, ALU.max)
            first(r_g1, gl, r_gmax, NG, r_key4)
            dve.tensor_tensor(r_gd, gl, last_dim(r_gmax, NG), ALU.subtract).then_inc(softmax_in, 1)
            TT(r_e4, el.rearrange("p i (g e) -> p i g e", g=NG), last_dim(r_g1, EG), ALU.mult)
            RED(r_es, r_e4.rearrange("p i g e -> p i e g"), ALU.add)
            RED(r_m1, r_es, ALU.max)
            first(r_o[:, 0], r_es, r_m1, EG, r_key8)
            link(dve.scalar_tensor_tensor(out=r_es, in0=r_o[:, 0], scalar=-BIG, in1=r_es, op0=ALU.mult, op1=ALU.add))
            RED(r_m2, r_es, ALU.max)
            first(r_o[:, 1], r_es, r_m2, EG, r_key8)
            dve.tensor_tensor(r_ex, r_m2, r_m1, ALU.subtract).then_inc(softmax_in, 1)
            dve.wait_ge(softmax_done, 1)
            RED(r_pg, r_gd, ALU.add)
            dve.wait_ge(softmax_done, 2)
            TS(r_den, r_ex, 1.0, None, ALU.add)
            TT(r_den, r_den, r_pg, ALU.mult)
            link(dve.reciprocal(w_k[:, 0, :], r_den))
            TT(w_k[:, 1, :], w_k[:, 0, :], r_ex, ALU.mult)
            for k in range(TOPK):
                TT(r_oh[:, k].rearrange("p i (g e) -> p i g e", g=NG), r_o[:, k].unsqueeze(2).broadcast_to([P, NT, NG, EG]),
                   last_dim(r_g1, EG), ALU.mult)
            link(dve.memset(r_oh[NS:P, :, NT - 1, :], 0.0))
            TT(r_m, r_oh[:, 0], r_oh[:, 1], ALU.add)
            link(dve.memset(r_cum[:, 0, :], 0.0))
            for i in range(NT - 1):
                TT(r_cum[:, i + 1, :], r_cum[:, i, :], r_m[:, i, :], ALU.add)
            dve.tensor_tensor(r_cum[:, NT, :], r_cum[:, NT - 1, :], r_m[:, NT - 1, :], ALU.add).then_inc(cum_done, 1)
            dve.wait_ge(rank_psum, 1)
            link(dve.tensor_copy(r_c, banks(7)[:, 0:(NT + 1) * NE].rearrange("p (i e) -> p i e", e=NE)))
            flat = "p k i e -> p (k i) e"

            def pick(out, table):
                TT(r_tmp, r_oh, table, ALU.mult)
                RED(out, r_tmp.rearrange(flat), ALU.add)

            def per_expert(v):
                return v.unsqueeze(1).unsqueeze(1).broadcast_to([P, TOPK, NT, NE])

            pick(r_rank, r_c[:, 0:NT, :].unsqueeze(1).broadcast_to([P, TOPK, NT, NE]))
            pick(r_exp, per_expert(r_iote))
            TT(r_xc, last_dim(r_c[:, NT, :], EG), r_thr.unsqueeze(1).broadcast_to([P, NE, EG]), ALU.is_gt)
            for s in r_s:
                link(dve.memset(s, 0.0))
            RED(r_x, r_xc, ALU.add)
            TS(r_s[0][:, 1, :], r_x, 0.0, None, ALU.add)
            a, b = r_s
            for d in (1, 2, 4, 8, 16):
                fa = a.rearrange("p a n -> p (a n)")
                TT(b[:, 1, :], fa[:, NE:], fa[:, NE - d:2 * NE - d], ALU.add)
                a, b = b, a
            upto = a[:, 1, :]
            TT(r_x, upto, r_x, ALU.subtract)
            pick(r_base, per_expert(r_x))
            TT(r_qc, last_dim(r_rank, EG), r_thr.unsqueeze(1).broadcast_to([P, TOPK * NT, EG]), ALU.is_ge)
            RED(r_q, r_qc, ALU.add)
            link(dve.scalar_tensor_tensor(out=r_slot, in0=r_q, scalar=-float(P), in1=r_rank, op0=ALU.mult, op1=ALU.add))
            TS(r_q1, r_q, 1.0, None, ALU.min)
            TT(r_tile, r_base, r_q, ALU.add)
            TT(r_tile, r_tile, r_exp, ALU.subtract)
            TS(r_tile, r_tile, float(NE - 1), None, ALU.add)
            TT(r_tile, r_tile, r_q1, ALU.mult)
            TT(r_tile, r_tile, r_exp, ALU.add)
            for k in range(TOPK):
                slot, tile = (v.rearrange("p (k i) -> p k i", k=TOPK)[:, k, :] for v in (r_slot, r_tile))
                dve.tensor_tensor(r_os[k], r_iots.unsqueeze(1).broadcast_to([P, NT, P]), last_dim(slot, P),
                                  ALU.is_equal)
                TT(r_eq, r_iotc.unsqueeze(1).broadcast_to([P, NT, NCOL]), last_dim(tile, NCOL), ALU.is_equal)
                for a in range(2):
                    ins = dve.tensor_tensor(r_ot[k][:, :, a, :], r_eq, last_dim(r_val[:, a, :, k], NCOL), ALU.mult)
                ins.then_inc(onehot_done, 1)
                if k == 0:
                    dve.wait_ge(onehot_done, 1)
            dve.wait_ge(onehot_used, 1)
            link(dve.tensor_copy(r_f, banks(6)[:, 0:2 * NCOL].rearrange("p (a n) -> p a n", a=2)))
            TS(r_z, r_f, 0.0, 65536.0, ALU.is_equal, ALU.mult)
            TS(r_f, r_f, -1.0, None, ALU.add)
            TT(r_f, r_f, r_z, ALU.add)
            link(dve.tensor_copy(idx[:, :, :], r_f))
            dve.sem_inc(idx_done, 1)
            TT(r_tc, upto.unsqueeze(1).broadcast_to([P, EXTRA, NE]), last_dim(r_iotc[:, 0:EXTRA], NE), ALU.is_le)
            RED(r_te, r_tc, ALU.add)
            TS(r_te, r_te, float(NE - 1), None, ALU.min)
            link(dve.tensor_copy(te_u[:, 0:NE], r_iotc[0:1, 0:NE]))
            link(dve.tensor_copy(te_u[:, NE:], r_te[0:1, :]))
            TS(r_tc[:, 0, 0:EXTRA // UN], r_iotc[:, 0:EXTRA // UN], float(UN), None, ALU.mult)
            TS(r_tc[:, 0, 0:EXTRA // UN], r_tc[:, 0, 0:EXTRA // UN], upto[:, NE - 1:NE], None, ALU.is_lt)
            RED(r_n[:, 0:1], r_tc[:, 0, 0:EXTRA // UN], ALU.add)
            TS(r_n[:, 0:1], r_n[:, 0:1], float(NE // UN - 1), None, ALU.add)
            dve.tensor_copy(last_turn[:, :], r_n[0:1, 0:1]).then_inc(turns_ready, 1)

            def copy_xg(u, s):
                dve.wait_ge(xT_psum, 2 * NT + u + 1)
                dve.tensor_copy(xgT[s % 2][:, 4:8, :], banks(3).rearrange("p (c n) -> p c n", c=4)).then_inc(xT_dve, 1)

            def hidden(u, s):
                bank = banks(s % 2)
                dve.wait_ge(gs_done, u + 1)
                dve.tensor_tensor(gs, bank[:, 0:F], gs, ALU.mult).then_inc(gmul_done, 1)
                dve.wait_ge(gmul_done, u + 1)
                dve.tensor_tensor(gu.rearrange("q (c p) -> q p c", c=2), bank[:, F:2 * F].rearrange(
                    "q (p c) -> q p c", c=2), gs.rearrange("q (p c) -> q p c", c=2), ALU.mult).then_inc(hx_done, 1)

            def dve_step(turn, s, ahead):
                u = UN * turn + s
                dve.wait_ge(ht_psum, u + 1)
                dve.tensor_copy(hT, banks(4)[:, 0:F].rearrange("p (c n) -> p c n", c=2)).then_inc(ht_done, 1)
                if ahead >= 2:
                    copy_xg(u + 2, s)
                if ahead >= 1:
                    hidden(u + 1, s + 1)
                dve.wait_ge(yd_psum, u + 1)
                dve.wait_ge(ye_out[s % 2], 16 * ((UN // 2) * turn + s // 2))
                dve.tensor_copy(ye[s % 2][:, 512:], banks(6)).then_inc(ye_dve, 1)

            copy_xg(0, 0)
            hidden(0, 0)
            copy_xg(1, 1)
            expert_turns(dve, dve_step)
            def combine(i):
                r = rows_of(i)
                dve.wait_ge(yk_in[i % YS], 16 * (i // YS + 1))
                for k in range(TOPK):
                    ins = dve.scalar_tensor_tensor(out=hres[0:r, i, :], in0=yk[i % YS][0:r, k, :],
                                                   scalar=w_k[0:r, k, i:i + 1], in1=hres[0:r, i, :], op0=ALU.mult,
                                                   op1=ALU.add)
                    if k == 0:
                        link(ins)
                ins.then_inc(ff_done, 1)

            def last_mean_square(i):
                r = rows_of(i)
                dve.wait_ge(sq_done, 2 * NT + i + 1)
                dve.tensor_scalar(stat[0:r, 1, i:i + 1], stat[0:r, 0, i:i + 1], 1.0 / D, RMS_EPS, ALU.mult, ALU.add)\
                    .then_inc(ms_done, 1)

            def last_scale(i):
                r = rows_of(i)
                dve.wait_ge(std_done, 2 * NT + i + 1)
                link(dve.reciprocal(stat[0:r, 3, i:i + 1], stat[0:r, 2, i:i + 1]))
                if i == 0:
                    dve.wait_ge(tables2_in, 16 * 7)
                if i >= 2:
                    dve.wait_ge(fin_out[i % 2], 16 * (i // 2))
                dve.wait_ge(ff_done, i + 1)
                dve.scalar_tensor_tensor(out=fin[i % 2][0:r, :], in0=hres[0:r, i, :], scalar=stat[0:r, 3, i:i + 1],
                                         in1=gain[0:r, :], op0=ALU.mult, op1=ALU.mult).then_inc(fin_done, 1)

            for i in range(NT + 2):
                if i < NT:
                    combine(i)
                if 1 <= i <= NT:
                    last_mean_square(i - 1)
                if i >= 2:
                    last_scale(i - 2)



_INS = ['x_prompt', 'x_sample', 'state_conv', 'state_shift', 'state_wkv', 'norm1_g', 'w_in', 'conv_w', 'conv_b',
        'conv_ln_g', 'conv_ln_b', 'mu_shift', 'w0', 'w_decay_up', 'a0', 'w_aaa_up', 'w_gate_up', 'k_k', 'k_a', 'r_k',
        'gn_g', 'gn_b', 'w_out', 'norm2_g', 'w_router_group', 'b_router_group', 'w_router_expert',
        'b_router_expert', 'w_exp_gate', 'w_exp_up', 'w_exp_down', 'norm_f_g']
_OUTS = [((1, SEQ, D), 'float32'), ((SB, ST, D), 'float32'), ((1, 1, HB, C), 'float32'), ((1, 1, DS), 'float32'),
         ((1, 1, 2 * CT, HD, HD), 'float32'), ((1, SB, HB, C), 'float32'), ((1, SB, DS), 'float32'),
         ((1, SB, 2 * CT, HD, HD), 'float32')]


def kernel(**inputs):
    import numpy as _np
    import concourse.bacc as _bacc
    from concourse import mybir as _mybir
    from concourse.bass_utils import run_bass_kernel_spmd as _run

    nc = _bacc.Bacc("TRN2", target_bir_lowering=False, num_devices=1)
    arrays, args = {}, []
    for name in _INS:
        a = _np.ascontiguousarray(inputs[name])
        arrays[f"in_{name}_dram"] = a
        args.append(nc.dram_tensor(f"in_{name}_dram", a.shape, _mybir.dt.from_np(a.dtype), kind="ExternalInput").ap())
    for i, (shape, dtype) in enumerate(_OUTS):
        dt = _mybir.dt.from_np(_np.dtype(dtype))
        args.append(nc.dram_tensor(f"out_{i}_dram", shape, dt, kind="ExternalOutput").ap())
    hybrid_decoder_step(nc, *args)
    r = _run(nc, [arrays], core_ids=[0])
    return tuple(r.results[0][f"out_{i}_dram"] for i in range(len(_OUTS)))
```
